# Optimizing a Trainium2 kernel written in Bass

```python
import jax, jax.numpy as jnp
from jax import lax
import numpy as np
import math

D_MODEL = 1024
BATCH = 1
SEQ = 512
DEPTH = 1

CTX_LEN = 256
GRID_W = 64
N_MIXERS = 3
ALPHA = (2 * DEPTH) ** 0.25
BETA = (8 * DEPTH) ** -0.25
LN_EPS = 1e-6
RMS_EPS = 1e-6
N_MOD = 6
FFN_HIDDEN = -(-8 * D_MODEL // (3 * 256)) * 256
POOL_WINDOWS = (2, 4, 8, 16)
N_POOL_GROUPS = len(POOL_WINDOWS)
POOL_GROUP_DIM = D_MODEL // N_POOL_GROUPS
HGRN_HEAD_DIM = 128
HGRN_HEADS = D_MODEL // HGRN_HEAD_DIM
HGRN_CHUNK = 64
NA_HEAD_DIM = 64
NA_HEADS = D_MODEL // NA_HEAD_DIM
NA_ROWS = 8
NA_COLS = 16
NA_QBLOCK = 16
NA_KBAND = 32
N_POOL_LAYERS = len(range(0, DEPTH, N_MIXERS))
N_HGRN_LAYERS = len(range(1, DEPTH, N_MIXERS))
N_NA_LAYERS = len(range(2, DEPTH, N_MIXERS))


def layer_norm(x, g, b):
    xf = x.astype(jnp.float32)
    mu = jnp.mean(xf, axis=-1, keepdims=True)
    var = jnp.mean(jnp.square(xf - mu), axis=-1, keepdims=True)
    return ((xf - mu) * lax.rsqrt(var + LN_EPS) * g + b).astype(x.dtype)

def swiglu(h, w_in, w_out):
    gt, up = jnp.split(h @ w_in, 2, axis=-1)
    return (jax.nn.silu(gt) * up) @ w_out

def centred_window_mean(h, w):
    L = h.shape[1]
    lo = w // 2
    hi = w - 1 - lo
    t = np.arange(L)
    start = np.clip(t - lo, 0, L)
    end = np.clip(t + hi + 1, 0, L)
    hf = h.astype(jnp.float32)
    cs = jnp.concatenate([jnp.zeros_like(hf[:, :1]), jnp.cumsum(hf, axis=1)], axis=1)
    cnt = jnp.asarray((end - start).astype(np.float32))
    return ((cs[:, end] - cs[:, start]) / cnt[None, :, None]).astype(h.dtype)

def multiscale_pool(h, w_group, scale):
    B, L, D = h.shape
    outs = []
    for g, w in enumerate(POOL_WINDOWS):
        hg = h[..., g * POOL_GROUP_DIM:(g + 1) * POOL_GROUP_DIM]
        outs.append(centred_window_mean(hg, w) - hg)
    p = jnp.stack(outs, axis=2)
    y = jnp.einsum('blgc,gcd->blgd', p, w_group).reshape(B, L, D)
    return y * scale

def pool_mixer(hx, hc, w_group, scale, need_ctx):
    ox = multiscale_pool(hx, w_group, scale)
    oc = multiscale_pool(hc, w_group, scale) if need_ctx else None
    return ox, oc

def chunk_gated_scan(q, k, v, log_f, s0):
    B, H, L, DK = q.shape
    DV = v.shape[-1]
    C = HGRN_CHUNK
    n = L // C

    def chunks(a):
        return jnp.moveaxis(a.reshape(B, H, n, C, a.shape[-1]), 2, 0)

    lower = jnp.asarray(np.tril(np.ones((C, C), dtype=bool)))

    def step(s, inp):
        q_c, k_c, v_c, g_c = inp
        b = jnp.cumsum(g_c, axis=2)
        rel = jnp.where(lower[:, :, None], b[:, :, :, None, :] - b[:, :, None, :, :], -jnp.inf)
        a = jnp.einsum('bhtd,bhsd,bhtsd->bhts', q_c, k_c, jnp.exp(rel))
        o = jnp.einsum('bhts,bhse->bhte', a, v_c) + jnp.einsum('bhtd,bhde->bhte', q_c * jnp.exp(b), s)
        b_end = b[:, :, -1:, :]
        s_new = jnp.exp(b_end)[:, :, 0, :, None] * s + jnp.einsum('bhsd,bhse->bhde', k_c * jnp.exp(b_end - b), v_c)
        return s_new, o

    s_fin, o = lax.scan(step, s0, (chunks(q), chunks(k), chunks(v), chunks(log_f)))
    o = jnp.moveaxis(o, 0, 2).reshape(B, H, L, DV)
    return o, s_fin

def hgrn2_mixer(hx, hc, w_in, lb_fwd, lb_bwd, norm_w, w_out, need_ctx):
    def heads(a):
        B_, L_, _ = a.shape
        return a.reshape(B_, L_, HGRN_HEADS, HGRN_HEAD_DIM).transpose(0, 2, 1, 3).astype(jnp.float32)

    def project(h):
        q, v, zf, zb, g = jnp.split(h @ w_in, 5, axis=-1)
        return heads(jax.nn.silu(q)), heads(v), heads(zf), heads(zb), g

    def gate(z, lb):
        lb = lb.reshape(HGRN_HEADS, 1, HGRN_HEAD_DIM)
        f = lb + (1.0 - lb) * jax.nn.sigmoid(z)
        return 1.0 - f, jnp.log(f)

    def flip(a):
        return jnp.flip(a, axis=2)

    qx, vx, zfx, zbx, gx = project(hx)
    qc, vc, zfc, zbc, gc = project(hc)
    s0 = jnp.zeros((hc.shape[0], HGRN_HEADS, HGRN_HEAD_DIM, HGRN_HEAD_DIM), jnp.float32)
    kcf, lcf = gate(zfc, lb_fwd)
    kxf, lxf = gate(zfx, lb_fwd)
    oc_f, sc_f = chunk_gated_scan(qc, kcf, vc, lcf, s0)
    ox_f, _ = chunk_gated_scan(qx, kxf, vx, lxf, sc_f)
    kcb, lcb = gate(zbc, lb_bwd)
    kxb, lxb = gate(zbx, lb_bwd)
    oc_b, sc_b = chunk_gated_scan(flip(qc), flip(kcb), flip(vc), flip(lcb), s0)
    ox_b, _ = chunk_gated_scan(flip(qx), flip(kxb), flip(vx), flip(lxb), sc_b)

    def readout(o, g, dtype):
        B_, H_, L_, E_ = o.shape
        o = o * lax.rsqrt(jnp.mean(o * o, axis=-1, keepdims=True) + RMS_EPS)
        o = o.transpose(0, 2, 1, 3).reshape(B_, L_, H_ * E_).astype(dtype)
        return (o * norm_w * jax.nn.silu(g)) @ w_out

    ox = readout(ox_f + flip(ox_b), gx, hx.dtype)
    oc = readout(oc_f + flip(oc_b), gc, hc.dtype) if need_ctx else None
    return ox, oc

def na_mixer(hx, hc, w_qkv, rpb, w_out, need_ctx):
    B, L, D = hx.shape
    rows = L // GRID_W
    kr = min(NA_ROWS, rows)
    scale = NA_HEAD_DIM ** -0.5

    def qkv(h):
        B_, L_, _ = h.shape
        z = (h @ w_qkv).reshape(B_, L_, 3, NA_HEADS, NA_HEAD_DIM)
        return [jnp.moveaxis(z[:, :, m], 1, 2) for m in range(3)]

    qx, kx, vx = qkv(hx)
    qc, kc, vc = qkv(hc)

    def grid(a):
        return a.reshape(B, NA_HEADS, rows, GRID_W, NA_HEAD_DIM)

    qg, kg, vg = grid(qx), grid(kx), grid(vx)
    n_cb = GRID_W // NA_QBLOCK
    qcol = np.arange(GRID_W).reshape(n_cb, NA_QBLOCK)
    band_start = np.clip(np.arange(n_cb) * NA_QBLOCK - NA_COLS // 2, 0, GRID_W - NA_KBAND)
    kcol = band_start[:, None] + np.arange(NA_KBAND)
    win_start = np.clip(qcol - NA_COLS // 2, 0, GRID_W - NA_COLS)
    col_ok = (kcol[:, None, :] >= win_start[:, :, None]) & (kcol[:, None, :] < win_start[:, :, None] + NA_COLS)
    dcol_idx = np.clip(kcol[:, None, :] - qcol[:, :, None] + NA_COLS - 1, 0, 2 * NA_COLS - 2)
    col_ok = jnp.asarray(col_ok)
    n_loc = kr * NA_KBAND

    def row_block(r):
        rs = jnp.clip(r - kr // 2, 0, rows - kr)
        q_r = lax.dynamic_index_in_dim(qg, r, axis=2, keepdims=False)
        k_r = lax.dynamic_slice_in_dim(kg, rs, kr, axis=2)[:, :, :, kcol]
        v_r = lax.dynamic_slice_in_dim(vg, rs, kr, axis=2)[:, :, :, kcol]
        q_b = q_r.reshape(B, NA_HEADS, n_cb, NA_QBLOCK, NA_HEAD_DIM)
        s_loc = jnp.einsum('bhjqd,bhajkd->bhjqak', q_b, k_r).astype(jnp.float32) * scale
        drow = rs + jnp.arange(kr) - r + NA_ROWS - 1
        bias = rpb[:, drow][:, :, dcol_idx].transpose(0, 2, 3, 1, 4)
        s_loc = jnp.where(col_ok[:, :, None, :], s_loc + bias.astype(jnp.float32), -jnp.inf)
        s_loc = s_loc.reshape(B, NA_HEADS, n_cb, NA_QBLOCK, n_loc)
        s_ctx = jnp.einsum('bhjqd,bhmd->bhjqm', q_b, kc).astype(jnp.float32) * scale
        p = jax.nn.softmax(jnp.concatenate([s_loc, s_ctx], axis=-1), axis=-1).astype(vx.dtype)
        p_loc = p[..., :n_loc].reshape(B, NA_HEADS, n_cb, NA_QBLOCK, kr, NA_KBAND)
        o = jnp.einsum('bhjqak,bhajke->bhjqe', p_loc, v_r) + jnp.einsum('bhjqm,bhme->bhjqe', p[..., n_loc:], vc)
        return o.reshape(B, NA_HEADS, GRID_W, NA_HEAD_DIM)

    o = lax.map(row_block, jnp.arange(rows))
    ox = o.transpose(1, 0, 3, 2, 4).reshape(B, L, D) @ w_out
    oc = None
    if need_ctx:
        s = jnp.einsum('bhqd,bhkd->bhqk', qc, kc).astype(jnp.float32) * scale
        pc = jax.nn.softmax(s, axis=-1).astype(vc.dtype)
        occ = jnp.einsum('bhqk,bhkd->bhqd', pc, vc)
        oc = occ.transpose(0, 2, 1, 3).reshape(hc.shape[0], hc.shape[1], D) @ w_out
    return ox, oc

def first_inputs(seed: int = 0) -> dict:
    key = jax.random.key(seed)
    ks = jax.random.split(key, 20)
    D = D_MODEL
    F = FFN_HIDDEN
    GD = POOL_GROUP_DIM

    def nrm(k, shape, s):
        return jax.random.normal(k, shape, jnp.float32) * s

    return {
        'x': nrm(ks[0], (BATCH, SEQ, D), 1.0),
        'c': nrm(ks[1], (BATCH, D), 1.0),
        'ctx': nrm(ks[2], (BATCH, CTX_LEN, D), 1.0),
        'c_ctx': nrm(ks[3], (D,), 1.0),
        'mod_w': nrm(ks[4], (DEPTH, D, N_MOD * D), 0.5 * D ** -0.5),
        'mod_b': nrm(ks[5], (DEPTH, N_MOD * D), 0.02),
        'ln_g': 1.0 + nrm(ks[6], (DEPTH, 2, D), 0.02),
        'ln_b': nrm(ks[7], (DEPTH, 2, D), 0.02),
        'ffn_w_in': nrm(ks[8], (DEPTH, D, 2 * F), D ** -0.5),
        'ffn_w_out': nrm(ks[9], (DEPTH, F, D), BETA * F ** -0.5),
        'pool_w': nrm(ks[10], (N_POOL_LAYERS, N_POOL_GROUPS, GD, GD), BETA * GD ** -0.5),
        'pool_scale': 1.0 + nrm(ks[11], (N_POOL_LAYERS, D), 0.02),
        'hgrn_w_in': nrm(ks[12], (N_HGRN_LAYERS, D, 5 * D), D ** -0.5),
        'hgrn_lb_logits': 1.0 + nrm(ks[13], (2, DEPTH, D), 0.02),
        'hgrn_norm_w': 1.0 + nrm(ks[14], (N_HGRN_LAYERS, D), 0.02),
        'hgrn_w_out': nrm(ks[15], (N_HGRN_LAYERS, D, D), BETA * D ** -0.5),
        'na_w_qkv': nrm(ks[16], (N_NA_LAYERS, D, 3 * D), D ** -0.5),
        'na_rpb': nrm(ks[17], (N_NA_LAYERS, NA_HEADS, 2 * NA_ROWS - 1, 2 * NA_COLS - 1), 0.02),
        'na_w_out': nrm(ks[18], (N_NA_LAYERS, D, D), BETA * D ** -0.5),
    }

def first_block(x, c, ctx, c_ctx, mod_w, mod_b, ln_g, ln_b, ffn_w_in, ffn_w_out,
              pool_w, pool_scale, hgrn_w_in, hgrn_lb_logits, hgrn_norm_w, hgrn_w_out,
              na_w_qkv, na_rpb, na_w_out):
    p_lb = jax.nn.softmax(hgrn_lb_logits.astype(jnp.float32), axis=1)
    lower_bounds = jnp.cumsum(p_lb, axis=1) - p_lb[:, :1]
    s_c = jax.nn.silu(c)
    s_cc = jax.nn.silu(c_ctx)
    for i in range(DEPTH):
        last = i == DEPTH - 1
        kind = i % N_MIXERS
        j = i // N_MIXERS
        mod_x = s_c @ mod_w[i] + mod_b[i]
        mod_c = s_cc @ mod_w[i] + mod_b[i]
        sh1, sc1, g1, sh2, sc2, g2 = jnp.split(mod_x[:, None, :], N_MOD, axis=-1)
        csh1, csc1, cg1, csh2, csc2, cg2 = jnp.split(mod_c, N_MOD, axis=-1)
        hx = x * (1.0 + sc1) + sh1
        hc = ctx * (1.0 + csc1) + csh1 if (kind != 0 or not last) else None
        if kind == 0:
            ox, oc = pool_mixer(hx, hc, pool_w[j], pool_scale[j], not last)
        elif kind == 1:
            ox, oc = hgrn2_mixer(hx, hc, hgrn_w_in[j], lower_bounds[0, i], lower_bounds[1, i],
                                 hgrn_norm_w[j], hgrn_w_out[j], not last)
        else:
            ox, oc = na_mixer(hx, hc, na_w_qkv[j], na_rpb[j], na_w_out[j], not last)
        x = layer_norm(ALPHA * x + g1 * ox, ln_g[i, 0], ln_b[i, 0])
        x = layer_norm(ALPHA * x + g2 * swiglu(x * (1.0 + sc2) + sh2, ffn_w_in[i], ffn_w_out[i]),
                       ln_g[i, 1], ln_b[i, 1])
        if not last:
            ctx = layer_norm(ALPHA * ctx + cg1 * oc, ln_g[i, 0], ln_b[i, 0])
            ctx = layer_norm(ALPHA * ctx + cg2 * swiglu(ctx * (1.0 + csc2) + csh2, ffn_w_in[i], ffn_w_out[i]),
                             ln_g[i, 1], ln_b[i, 1])
    return x


DEPTH_2 = 2

N_MIXERS_2 = 2
N_MLA_LAYERS = (DEPTH_2 + 1) // N_MIXERS_2
N_HYENA_LAYERS = DEPTH_2 // N_MIXERS_2

MLA_HEADS = 8
QK_NOPE_DIM = 128
QK_ROPE_DIM = 64
V_HEAD_DIM = 128
Q_LORA_RANK = 384
KV_LORA_RANK = 256
MLA_IN_DIM = Q_LORA_RANK + KV_LORA_RANK + QK_ROPE_DIM
ROPE_THETA = 10000.0
Q_BLOCK = 128

HYENA_ORDER = 2
HYENA_EMB_DIM = 33
HYENA_FILTER_WIDTH = 64
HYENA_FAST_DECAY = 0.3
HYENA_SLOW_DECAY = 1.5
HYENA_TARGET = 1e-2
SHORT_CONV_WIDTH = 3

D_FF = 2816
FFN_CONV_WIDTH = 3

NORM_EPS = 1e-5
DEEPNORM_ALPHA = (2.0 * DEPTH_2) ** 0.25
DEEPNORM_BETA = (8.0 * DEPTH_2) ** -0.25


def layer_norm_2(x, g, b):
    xf = x.astype(jnp.float32)
    mu = jnp.mean(xf, -1, keepdims=True)
    var = jnp.mean(jnp.square(xf - mu), -1, keepdims=True)
    return ((xf - mu) * lax.rsqrt(var + NORM_EPS) * g.astype(jnp.float32) + b.astype(jnp.float32)).astype(x.dtype)

def rms_norm(x, g):
    xf = x.astype(jnp.float32)
    ms = jnp.mean(jnp.square(xf), -1, keepdims=True)
    return (xf * lax.rsqrt(ms + RMS_EPS) * g.astype(jnp.float32)).astype(x.dtype)

def dwconv_centred(x, w):
    k_width = w.shape[0]
    pad = k_width // 2
    s = x.shape[1]
    xp = jnp.pad(x, ((0, 0), (pad, pad), (0, 0)))
    return sum(xp[:, k:k + s] * w[k] for k in range(k_width))

def rope_tables(positions):
    inv = 1.0 / (ROPE_THETA ** (jnp.arange(0, QK_ROPE_DIM, 2, dtype=jnp.float32) / QK_ROPE_DIM))
    ang = positions.astype(jnp.float32)[..., None] * inv
    return jnp.cos(ang), jnp.sin(ang)

def apply_rope(x, cos, sin):
    x1, x2 = jnp.split(x.astype(jnp.float32), 2, axis=-1)
    return jnp.concatenate([x1 * cos - x2 * sin, x1 * sin + x2 * cos], -1).astype(x.dtype)

def mla_mixer(x, cos, sin, w_in, g_q, w_uq, g_kv, w_ukv, w_o):
    b, s, _ = x.shape
    h = x @ w_in
    c_q, c_kv, k_rope = jnp.split(h, [Q_LORA_RANK, Q_LORA_RANK + KV_LORA_RANK], axis=-1)
    q = (rms_norm(c_q, g_q) @ w_uq).reshape(b, s, MLA_HEADS, QK_NOPE_DIM + QK_ROPE_DIM)
    q_nope = q[..., :QK_NOPE_DIM]
    q_rope = apply_rope(q[..., QK_NOPE_DIM:], cos[:, :, None], sin[:, :, None])
    k_rope = apply_rope(k_rope, cos, sin)
    kv = (rms_norm(c_kv, g_kv) @ w_ukv).reshape(b, s, MLA_HEADS, QK_NOPE_DIM + V_HEAD_DIM)
    k_nope, v = kv[..., :QK_NOPE_DIM], kv[..., QK_NOPE_DIM:]
    scale = (QK_NOPE_DIM + QK_ROPE_DIM) ** -0.5
    nb = s // Q_BLOCK
    qn_blocks = q_nope.reshape(b, nb, Q_BLOCK, MLA_HEADS, QK_NOPE_DIM).transpose(1, 0, 2, 3, 4)
    qr_blocks = q_rope.reshape(b, nb, Q_BLOCK, MLA_HEADS, QK_ROPE_DIM).transpose(1, 0, 2, 3, 4)

    def attend(blk):
        qn, qr = blk
        sc = (jnp.einsum('bqhd,bkhd->bhqk', qn, k_nope)
              + jnp.einsum('bqhr,bkr->bhqk', qr, k_rope))
        p = jax.nn.softmax(sc.astype(jnp.float32) * scale, axis=-1).astype(v.dtype)
        return jnp.einsum('bhqk,bkhd->bqhd', p, v)

    o = lax.map(attend, (qn_blocks, qr_blocks))
    o = o.transpose(1, 0, 2, 3, 4).reshape(b, s, MLA_HEADS * V_HEAD_DIM)
    return o @ w_o

def hyena_positional_features(length):
    t = jnp.linspace(0.0, 1.0, length, dtype=jnp.float32)[:, None]
    bands = (HYENA_EMB_DIM - 1) // 2
    w = 2.0 * math.pi * jnp.arange(length, dtype=jnp.float32)[:, None] / length
    f = jnp.linspace(1e-4, bands - 1, bands, dtype=jnp.float32)[None, :]
    z = jnp.concatenate([t, jnp.cos(f * w), -jnp.sin(f * w)], axis=-1)
    return t, z

def hyena_filters(length, fw1, fb1, fw2, fb2, fw3, fb3, freq, fw_out):
    t, z = hyena_positional_features(length)
    freq = freq.astype(jnp.float32)
    h = jnp.sin(freq * (z @ fw1.astype(jnp.float32) + fb1.astype(jnp.float32)))
    h = jnp.sin(freq * (h @ fw2.astype(jnp.float32) + fb2.astype(jnp.float32)))
    h = jnp.sin(freq * (h @ fw3.astype(jnp.float32) + fb3.astype(jnp.float32)))
    h = h @ fw_out.astype(jnp.float32)
    deltas = jnp.abs(jnp.linspace(math.log(HYENA_FAST_DECAY) / HYENA_TARGET,
                                  math.log(HYENA_SLOW_DECAY) / HYENA_TARGET,
                                  D_MODEL, dtype=jnp.float32))
    decay = jnp.exp(-t * deltas)
    return h.reshape(length, HYENA_ORDER, 2, D_MODEL) * decay[:, None, None, :]

def two_sided_kernel(h_fwd, h_bwd):
    zero = jnp.zeros_like(h_fwd[:1])
    return jnp.concatenate([h_fwd.at[0].add(h_bwd[0]), zero, h_bwd[:0:-1]], axis=0)

def hyena_mixer(x, w_in, w_short, fw1, fb1, fw2, fb2, fw3, fb3, freq, fw_out, d_bias, w_o):
    b, length, _ = x.shape
    u = dwconv_centred(x @ w_in, w_short)
    v, g1, g2 = jnp.split(u, 3, axis=-1)
    filt = hyena_filters(length, fw1, fb1, fw2, fb2, fw3, fb3, freq, fw_out)
    n = 2 * length
    z = v.astype(jnp.float32)
    for o, gate in enumerate((g1, g2)):
        k_f = jnp.fft.rfft(two_sided_kernel(filt[:, o, 0], filt[:, o, 1]), n=n, axis=0)
        z_f = jnp.fft.rfft(z, n=n, axis=1)
        y = jnp.fft.irfft(z_f * k_f, n=n, axis=1)[:, :length]
        z = gate.astype(jnp.float32) * (y + d_bias[o].astype(jnp.float32) * z)
    return z.astype(x.dtype) @ w_o

def conv_ffn(x, w_up, w_conv, w_down):
    h = dwconv_centred(x @ w_up, w_conv)
    a, g = jnp.split(h, 2, axis=-1)
    return (jax.nn.silu(g) * a) @ w_down

def second_inputs(seed: int = 0) -> dict:
    key = jax.random.key(seed)
    ks = iter(jax.random.split(key, 40))

    def nrm(shape, scale):
        return jax.random.normal(next(ks), shape, jnp.float32) * scale

    def gain(shape):
        return 1.0 + nrm(shape, 0.01)

    nm, nh = N_MLA_LAYERS, N_HYENA_LAYERS
    hf = HYENA_FILTER_WIDTH
    return {
        "x": nrm((BATCH, SEQ, D_MODEL), 1.0),
        "positions": jnp.broadcast_to(jnp.arange(SEQ, dtype=jnp.int32), (BATCH, SEQ)),
        "mla_w_in": nrm((nm, D_MODEL, MLA_IN_DIM), D_MODEL ** -0.5),
        "mla_g_q": gain((nm, Q_LORA_RANK)),
        "mla_w_uq": nrm((nm, Q_LORA_RANK, MLA_HEADS * (QK_NOPE_DIM + QK_ROPE_DIM)), Q_LORA_RANK ** -0.5),
        "mla_g_kv": gain((nm, KV_LORA_RANK)),
        "mla_w_ukv": nrm((nm, KV_LORA_RANK, MLA_HEADS * (QK_NOPE_DIM + V_HEAD_DIM)), KV_LORA_RANK ** -0.5),
        "mla_w_o": nrm((nm, MLA_HEADS * V_HEAD_DIM, D_MODEL), (MLA_HEADS * V_HEAD_DIM) ** -0.5 * DEEPNORM_BETA),
        "hy_w_in": nrm((nh, D_MODEL, 3 * D_MODEL), D_MODEL ** -0.5),
        "hy_w_short": nrm((nh, SHORT_CONV_WIDTH, 3 * D_MODEL), SHORT_CONV_WIDTH ** -0.5),
        "hy_fw1": nrm((nh, HYENA_EMB_DIM, hf), HYENA_EMB_DIM ** -0.5),
        "hy_fb1": nrm((nh, hf), 0.02),
        "hy_fw2": nrm((nh, hf, hf), hf ** -0.5),
        "hy_fb2": nrm((nh, hf), 0.02),
        "hy_fw3": nrm((nh, hf, hf), hf ** -0.5),
        "hy_fb3": nrm((nh, hf), 0.02),
        "hy_freq": gain((nh, hf)),
        "hy_fw_out": nrm((nh, hf, HYENA_ORDER * 2 * D_MODEL), hf ** -0.5),
        "hy_d_bias": nrm((nh, HYENA_ORDER, D_MODEL), 0.1),
        "hy_w_o": nrm((nh, D_MODEL, D_MODEL), D_MODEL ** -0.5 * DEEPNORM_BETA),
        "ffn_w_up": nrm((DEPTH_2, D_MODEL, 2 * D_FF), D_MODEL ** -0.5),
        "ffn_w_conv": nrm((DEPTH_2, FFN_CONV_WIDTH, 2 * D_FF), FFN_CONV_WIDTH ** -0.5),
        "ffn_w_down": nrm((DEPTH_2, D_FF, D_MODEL), D_FF ** -0.5 * DEEPNORM_BETA),
        "ln1_g": gain((DEPTH_2, D_MODEL)),
        "ln1_b": nrm((DEPTH_2, D_MODEL), 0.01),
        "ln2_g": gain((DEPTH_2, D_MODEL)),
        "ln2_b": nrm((DEPTH_2, D_MODEL), 0.01),
    }

def second_block(x, positions, mla_w_in, mla_g_q, mla_w_uq, mla_g_kv, mla_w_ukv, mla_w_o,
              hy_w_in, hy_w_short, hy_fw1, hy_fb1, hy_fw2, hy_fb2, hy_fw3, hy_fb3, hy_freq,
              hy_fw_out, hy_d_bias, hy_w_o, ffn_w_up, ffn_w_conv, ffn_w_down,
              ln1_g, ln1_b, ln2_g, ln2_b):
    cos, sin = rope_tables(positions)
    for i in range(DEPTH_2):
        j = i // N_MIXERS_2
        if i % N_MIXERS_2 == 0:
            m = mla_mixer(x, cos, sin, mla_w_in[j], mla_g_q[j], mla_w_uq[j],
                          mla_g_kv[j], mla_w_ukv[j], mla_w_o[j])
        else:
            m = hyena_mixer(x, hy_w_in[j], hy_w_short[j], hy_fw1[j], hy_fb1[j], hy_fw2[j],
                            hy_fb2[j], hy_fw3[j], hy_fb3[j], hy_freq[j], hy_fw_out[j],
                            hy_d_bias[j], hy_w_o[j])
        x = layer_norm_2(DEEPNORM_ALPHA * x + m, ln1_g[i], ln1_b[i])
        x = layer_norm_2(DEEPNORM_ALPHA * x + conv_ffn(x, ffn_w_up[i], ffn_w_conv[i], ffn_w_down[i]),
                       ln2_g[i], ln2_b[i])
    return x


def setup_inputs(seed=0):
    out = dict(first_inputs(seed))
    for name, value in second_inputs(seed + 1).items():
        if name != "x":
            out[name + "_2"] = value
    return out


def reference(
    x, c, ctx, c_ctx, mod_w, mod_b, ln_g, ln_b, ffn_w_in, ffn_w_out, pool_w, pool_scale,
    hgrn_w_in, hgrn_lb_logits, hgrn_norm_w, hgrn_w_out, na_w_qkv, na_rpb, na_w_out, positions_2,
    mla_w_in_2, mla_g_q_2, mla_w_uq_2, mla_g_kv_2, mla_w_ukv_2, mla_w_o_2, hy_w_in_2,
    hy_w_short_2, hy_fw1_2, hy_fb1_2, hy_fw2_2, hy_fb2_2, hy_fw3_2, hy_fb3_2, hy_freq_2,
    hy_fw_out_2, hy_d_bias_2, hy_w_o_2, ffn_w_up_2, ffn_w_conv_2, ffn_w_down_2, ln1_g_2,
    ln1_b_2, ln2_g_2, ln2_b_2,
):
    x = first_block(
        x, c, ctx, c_ctx, mod_w, mod_b, ln_g, ln_b, ffn_w_in, ffn_w_out, pool_w, pool_scale,
        hgrn_w_in, hgrn_lb_logits, hgrn_norm_w, hgrn_w_out, na_w_qkv, na_rpb, na_w_out,
    )
    return second_block(
        x, positions_2, mla_w_in_2, mla_g_q_2, mla_w_uq_2, mla_g_kv_2, mla_w_ukv_2, mla_w_o_2,
        hy_w_in_2, hy_w_short_2, hy_fw1_2, hy_fb1_2, hy_fw2_2, hy_fb2_2, hy_fw3_2, hy_fb3_2,
        hy_freq_2, hy_fw_out_2, hy_d_bias_2, hy_w_o_2, ffn_w_up_2, ffn_w_conv_2, ffn_w_down_2,
        ln1_g_2, ln1_b_2, ln2_g_2, ln2_b_2,
    )


_drawn_inputs = setup_inputs


def setup_inputs(seed=0):
    import zlib

    import numpy as np

    out = dict(_drawn_inputs(seed))
    spreads = {}
    factors = {'pool_scale': 8.0,
     'mla_g_q_2': 8.0,
     'mla_g_kv_2': 8.0,
     'hy_freq_2': 3.381,
     'ln2_g_2': 2.762,
     'hy_d_bias_2': 2.853,
     'ln2_b_2': 5.025}
    for name, (base, spread) in spreads.items():
        noise = np.random.default_rng([zlib.crc32(name.encode()), seed]).standard_normal(out[name].shape)
        drawn = base * np.exp(spread * noise) if base else spread * noise
        out[name] = __import__('jax').numpy.asarray(drawn.astype(out[name].dtype))
    for name, factor in factors.items():
        out[name] = (out[name] * factor).astype(out[name].dtype)
    return out
```

```python
import math
from contextlib import ExitStack, contextmanager

import numpy as np

import concourse.bass as bass
from concourse import mybir

F32 = mybir.dt.float32
F32R = mybir.dt.float32r
I32 = mybir.dt.int32
ACT = mybir.ActivationFunctionType
ALU = mybir.AluOpType
AX_X = mybir.AxisListType.X

P = 128
T = 512
D = 1024
KD = D // P
FF = 2816
KF = FF // P
CHUNK = 1024
HEADS, NOPE, ROPE, VD = 8, 128, 64, 128
RQ, RKV = 384, 256
KQ, KKV = RQ // P, RKV // P
POOL_WINDOWS = (2, 4, 8, 16)
PAD = 8
HALF = T // 2
ALPHA_1 = 2.0 ** 0.25
ALPHA_2 = 4.0 ** 0.25
EPS_1, EPS_2, EPS_RMS = 1e-6, 1e-5, 1e-6
HY_EMB, HY_W = 33, 64
SM_SCALE = (NOPE + ROPE) ** -0.5

INV_2PI = float(np.float32(1.0 / (2 * math.pi)))
PI2_A = 6.28125
PI2_B = float(np.float32(2 * math.pi - PI2_A))
PI2_C = float(np.float32(2 * math.pi - PI2_A - PI2_B))
ROUND = float(1.5 * 2 ** 23)
PI_LOW = 3.1415925

PARAMS = {}
_at = 0
for _name, _n in (("c", KD), ("mod_b", 48), ("ln_g0", KD), ("ln_b0", KD), ("ln_g1", KD), ("ln_b1", KD),
                  ("pool_scale", KD), ("g_q", KQ), ("g_kv", KKV), ("hy_short", 3 * 24), ("hy_d", 2 * KD),
                  ("conv0", 3 * 2 * KF), ("conv1", 3 * 2 * KF),
                  ("a_g0", KD), ("a_b0", KD), ("f_g0", KD), ("f_b0", KD),
                  ("a_g1", KD), ("a_b1", KD), ("f_g1", KD), ("f_b1", KD)):
    PARAMS[_name] = (_at, _n)
    _at += _n
N_PARAMS = _at

N_GROUPS = 2
STREAM = (("pool", 2), ("up_1", 2 * KF), ("down_1", KF), ("mla_in", 6), ("mla_heads", 6 * N_GROUPS),
          ("mla_out", KD), ("up_2", 2 * KF), ("down_2", KF), ("hy_in", 24), ("hy_out", KD),
          ("up_3", 2 * KF), ("down_3", KF))
FIRST_CHUNK = {}
_at = 0
for _name, _n in STREAM:
    FIRST_CHUNK[_name] = _at
    _at += _n
N_CHUNKS = _at


class Val:

    def __init__(self, const, step=0):
        self.const, self.step = const, step

    def __add__(self, n):
        return Val(self.const + n, self.step)

    def __mul__(self, n):
        return Val(self.const * n, self.step * n)

    def half(self):
        assert self.step % 2 == 0
        return Val(self.const // 2, self.step // 2)

    def of(self, loop_index):
        return self.const if not self.step else loop_index * self.step + self.const


class Token:

    def __init__(self, count, val):
        self.count, self.val = count, val

    def before(self):
        assert self.val.step
        return Token(self.count, self.val + -self.val.step)


class Count:

    def __init__(self, handle):
        self.handle, self.val = handle, Val(0)

    def did(self, instruction, by=1):
        instruction.then_inc(self.handle, by)
        self.val = self.val + by
        return Token(self, self.val)


class Program:
    def __init__(self, nc, ctx):
        self.nc, self.ctx, self.index = nc, ctx, None
        self.pe, self.act, self.dve, self.pool = (self.count(n) for n in ("pe", "act", "dve", "pool"))
        self.raw = [self.count("raw_even"), self.count("raw_odd")]
        self.hi_done, self.lo_done = self.count("hi_done"), self.count("lo_done")
        self.used = self.count("chunk_used")
        self.everything = [self.pe, self.act, self.dve, self.pool, *self.raw, self.hi_done, self.lo_done, self.used]

    def count(self, name):
        return Count(self.ctx.enter_context(self.nc.semaphore("s_" + name)))

    def sb(self, ctx, name, shape, dt=F32):
        return ctx.enter_context(self.nc.sbuf_tensor(name, shape, dt))

    def wait(self, engine, *tokens):
        for t in tokens:
            if t is not None:
                engine.wait_ge(t.count.handle, t.val.of(self.index))

    @contextmanager
    def loop(self, n, per, extra=()):
        start = {c: c.val.const for c in self.everything + list(extra)}
        with self.nc.Fori(0, n) as i:
            self.index = i
            for c in start:
                c.val = Val(start[c], per.get(c, 0))
            yield i
        for c, v in start.items():
            assert c.val.const - v == per.get(c, 0), (c.handle, c.val.const - v, per.get(c, 0))
            c.val = Val(v + n * per.get(c, 0))
        self.index = None


def build_program(nc, a, out):
    ctx = ExitStack()
    with ctx:
        p = Program(nc, ctx)
        PE, SC, VE, GP, SP = nc.tensor, nc.scalar, nc.vector, nc.gpsimd, nc.sync
        pe, act, dve, pool, used = p.pe, p.act, p.dve, p.pool, p.used
        wait = p.wait

        X = p.sb(ctx, "x_residual", [P, KD, T])
        AH = p.sb(ctx, "act_hi", [P, KD, T], F32R)
        AL = p.sb(ctx, "act_lo", [P, KD, T], F32R)
        WR = p.sb(ctx, "w_raw", [P, 2, CHUNK])
        WH = p.sb(ctx, "w_hi", [P, 2, CHUNK], F32R)
        WL = p.sb(ctx, "w_lo", [P, 2, CHUNK], F32R)
        PV = p.sb(ctx, "params", [P, N_PARAMS])
        MOD = p.sb(ctx, "mod_x", [P, 48])
        AFF = p.sb(ctx, "affine", [P, 7, 2, KD])
        ident = p.sb(ctx, "identity", [P, P])
        mean_w = p.sb(ctx, "mean_weights", [P, P])
        ones = p.sb(ctx, "ones", [P, P])
        stat = p.sb(ctx, "stat", [P, 4, 4])
        minus_half = p.sb(ctx, "minus_half", [P, 4])
        ps = ctx.enter_context(nc.psum_tensor("ps", [P, 8, 512], F32))

        def par(name, k=0):
            at, n = PARAMS[name]
            assert k < n
            return PV[:, at + k:at + k + 1]

        def par_all(name):
            at, n = PARAMS[name]
            return PV[:, at:at + n]

        def f32(ap):
            return ap.bitcast(F32)

        def tile(buf, k):
            if not isinstance(k, Val) or not k.step:
                return buf[:, k.const if isinstance(k, Val) else k, :]
            return buf[:, bass.ds(k.of(p.index), 1), :].rearrange("p a b -> p (a b)")

        def mm3(o, lh, ll, rh, rl, start, stop, **kw):
            PE.matmul(o, lh, rh, start=start, stop=False, **kw)
            PE.matmul(o, lh, rl, start=False, stop=False, **kw)
            return PE.matmul(o, ll, rh, start=False, stop=stop, **kw)

        stream = a["w_stream"]

        def fetch(c):
            if c.step == 0 and c.const >= N_CHUNKS:
                return
            slot = c.const % 2
            if c.const >= 2:
                wait(SP, Token(p.lo_done, c + -1))
            src = stream[c.const] if not c.step else stream[bass.ds(c.of(p.index), 1)].rearrange("a p n -> (a p) n")
            p.raw[slot].did(SP.dma_start(WR[:, slot, :], src), 16)

        def split(c):
            if c.step == 0 and c.const >= N_CHUNKS:
                return
            slot = c.const % 2
            landed = Token(p.raw[slot], c.half() * 16 + 16)
            if c.const >= 2:
                wait(SC, Token(used, c + -1))
            wait(SC, landed)
            p.hi_done.did(SC.activation(WH[:, slot, :], WR[:, slot, :], ACT.Copy))
            wait(GP, Token(p.hi_done, c + 1))
            p.lo_done.did(GP.tensor_tensor(WL[:, slot, :], WR[:, slot, :], f32(WH[:, slot, :]), ALU.subtract))

        def take(c):
            split(c + 1)
            fetch(c + 2)
            wait(PE, Token(p.lo_done, c + 1))
            slot = c.const % 2
            return (WH[:, slot, :].rearrange("p (b m) -> p b m", m=P),
                    WL[:, slot, :].rearrange("p (b m) -> p b m", m=P))

        def per(chunks, **own):
            rises = {used: chunks, p.hi_done: chunks, p.lo_done: chunks, p.raw[0]: 8 * chunks, p.raw[1]: 8 * chunks}
            rises.update({{"pe": pe, "act": act, "dve": dve, "pool": pool}[k]: v for k, v in own.items()})
            return rises

        s_par, s_x, s_hy, s_con = p.count("params"), p.count("x"), p.count("hyena_small"), p.count("constants")
        got_par = s_par.did(SP.dma_start(PV[:, :], a["params"]), 16)
        VE.memset(ones[:, :], 1.0)
        VE.memset(minus_half[:, :], -0.5)
        made_ones = dve.did(VE.memset(mean_w[:, :], 1.0 / D))

        s1 = ExitStack()
        with s1:
            MR = 6
            MW = p.sb(s1, "mod_ring", [P, MR, CHUNK])
            sc = p.sb(s1, "silu_c", [P, KD])
            zt = p.sb(s1, "positions_features", [HY_EMB, T])
            fw1 = p.sb(s1, "fw1", [HY_EMB, HY_W])
            fws = p.sb(s1, "fw23_bias_freq", [HY_W, 2 * HY_W + 4])
            fwo = p.sb(s1, "fw_out", [HY_W, 2, 2, D])
            fsd = p.sb(s1, "fw_out_sum_diff", [HY_W, 2, 2, D])
            hid = p.sb(s1, "filter_hidden", [HY_W, T])
            red = p.sb(s1, "sin_turns", [HY_W, T])
            decay = p.sb(s1, "decay", [P, 4, D])
            tabr = p.sb(s1, "dft_raw", [P, 16, P])
            tabh = p.sb(s1, "dft_hi", [P, 16, P], F32R)
            tabl = p.sb(s1, "dft_lo", [P, 16, P], F32R)
            flt = p.sb(s1, "filter_taps", [P, 4, T])
            flh = p.sb(s1, "filter_taps_hi", [P, 4, T], F32R)
            fll = p.sb(s1, "filter_taps_lo", [P, 4, T], F32R)
            odd = p.sb(s1, "odd_spectrum", [P, 2, T])
            kspec = X[:, :, :].rearrange("p (f c) t -> p f c t", f=2)

            for dst, name in ((zt, "hy_z"), (fw1, "hy_fw1"), (fws, "hy_small")):
                got_small = s_hy.did(SP.dma_start(dst[:, :], a[name]), 16)
            got_fwo = s_con.did(SP.dma_start(fwo[:, :, :, :], a["hy_fw_out"]), 16)
            got_tab = s_con.did(SP.dma_start(tabr[:, :, :], a["dft_fwd"]), 16)
            got_decay = s_con.did(SP.dma_start(decay[:, :, :], a["decay"]), 16)
            s_spec = p.count("filter_io")
            got_ident = s_spec.did(SP.dma_start(ident[:, :], a["identity"]), 16)

            s_mod = [p.count(f"mod{i}") for i in range(MR)]
            mod_used = p.count("mod_used")
            for i in range(MR):
                s_mod[i].did(SP.dma_start(MW[:, i, :], a["mod_w"][i]), 16)

            wait(SC, got_par)
            got_sc = act.did(SC.activation(sc[:, :], par_all("c"), ACT.Silu))

            def reduce_sin(out_ap, arg, turns, np_):
                t = dve.did(VE.tensor_scalar(turns, arg, INV_2PI, ROUND, ALU.mult, ALU.add))
                wait(VE, t)
                t = dve.did(VE.tensor_scalar(turns, turns, ROUND, None, ALU.subtract))
                for part in (PI2_A, PI2_B, PI2_C):
                    wait(VE, t)
                    t = dve.did(VE.scalar_tensor_tensor(out=arg, in0=turns, scalar=-part, in1=arg,
                                                        op0=ALU.mult, op1=ALU.add))
                wait(VE, t)
                t = dve.did(VE.tensor_scalar(arg, arg, PI_LOW, -PI_LOW, ALU.min, ALU.max))
                if out_ap is None:
                    return t
                wait(SC, t)
                return act.did(SC.activation(out_ap, arg, ACT.Sin))

            wait(PE, got_small)
            mlp = pe.did(PE.matmul(ps[0:HY_W, 0, :], fw1[:, :], zt[:, :], start=True, stop=True))
            for layer in range(3):
                wait(VE, mlp, got_small)
                at = 2 * HY_W
                arg = flt[0:HY_W, 0, :]
                t = dve.did(VE.tensor_scalar(arg, ps[0:HY_W, 0, :], fws[:, at + layer:at + layer + 1],
                                             fws[:, at + 3:at + 4], ALU.add, ALU.mult))
                wait(VE, t)
                h_done = reduce_sin(hid[:, :], arg, red[:, :], HY_W)
                if layer < 2:
                    wait(PE, h_done)
                    mlp = pe.did(PE.matmul(ps[0:HY_W, 0, :], fws[:, layer * HY_W:(layer + 1) * HY_W], hid[:, :],
                                           start=True, stop=True))
            wait(VE, got_decay)
            dve.did(VE.tensor_tensor(fsd[:, 0, :, :], fwo[:, :, 0, :], fwo[:, :, 1, :], ALU.add))
            fsd_done = dve.did(VE.tensor_tensor(fsd[:, 1, :, :], fwo[:, :, 0, :], fwo[:, :, 1, :], ALU.subtract))
            th = dve.did(VE.tensor_copy(tabh[:, :, :], tabr[:, :, :]))
            wait(GP, th)
            tab_done = pool.did(GP.tensor_tensor(tabl[:, :, :], tabr[:, :, :], f32(tabh[:, :, :]), ALU.subtract))

            def mod_chunk(m, slot, landed, first):
                wait(PE, landed)
                if first:
                    wait(PE, got_sc)
                col = ps[:, 7, m:m + 1] if isinstance(m, int) else ps[:, 7, bass.ds(m.of(p.index), 1)]
                for k in range(KD):
                    ins = PE.matmul(col, MW[:, slot, k * P:(k + 1) * P], sc[:, k:k + 1],
                                    start=(k == 0), stop=(k == KD - 1))
                mod_used.did(ins)

            def mod_fetch(m, slot):
                wait(SP, Token(mod_used, m + (1 - MR)))
                s_mod[slot].did(SP.dma_start(MW[:, slot, :], a["mod_w"][bass.ds(m.of(p.index), 1)]
                                             .rearrange("a p n -> (a p) n")), 16)

            wait(PE, h_done, fsd_done)
            wait(VE, got_decay)
            rises = {pe: 4 * (1 + 4), dve: 4 * 12, act: 4 * (4 + 2), s_spec: 64}
            with p.loop(2, rises, extra=[s_spec]) as order:
                stored = Token(s_spec, s_spec.val)
                for n in range(2):
                    for kind in range(2):
                        for q in range(4):
                            fw = fsd[:, kind, bass.ds(order, 1), n * 512:(n + 1) * 512].rearrange("p a b -> p (a b)")
                            ins = PE.matmul(ps[:, q, :], hid[:, q * P:(q + 1) * P], fw, start=True, stop=True)
                        taps = pe.did(ins)
                        wait(VE, taps)
                        tok = []
                        for q in range(4):
                            tok.append(dve.did(VE.tensor_tensor(flt[:, q, :], ps[:, q, :],
                                                                decay[:, q, n * 512:(n + 1) * 512], ALU.mult)))
                        his = []
                        for q in range(4):
                            wait(SC, tok[q])
                            his.append(act.did(SC.activation(flh[:, q, :], flt[:, q, :], ACT.Copy)))
                        for q in range(4):
                            wait(VE, his[q])
                            lo = dve.did(VE.tensor_tensor(fll[:, q, :], flt[:, q, :], f32(flh[:, q, :]), ALU.subtract))
                        wait(PE, lo, tab_done)
                        for f in range(2):
                            if f == 1:
                                wait(PE, butterfly)
                            for parity in range(2):
                                for k in range(2):
                                    b = ((kind * 2 + parity) * 2 + k) * 2 + f
                                    ins = mm3(ps[:, 4 + parity, :], tabh[:, b, :], tabl[:, b, :],
                                              flh[:, 2 * parity + k, :], fll[:, 2 * parity + k, :], k == 0, k == 1)
                                got = pe.did(ins)
                            wait(SC, got)
                            copied = act.did(SC.activation(odd[:, f, :], ps[:, 5, :], ACT.Copy))
                            wait(VE, copied)
                            if kind == 0 and f == 0:
                                wait(VE, stored)
                            dve.did(VE.tensor_tensor(kspec[:, f, 2 * kind, :], ps[:, 4, :], odd[:, f, :], ALU.add))
                            butterfly = dve.did(VE.tensor_tensor(kspec[:, f, 2 * kind + 1, :], ps[:, 4, :],
                                                                 odd[:, f, :], ALU.subtract))
                    wait(SC, butterfly)
                    for f in range(2):
                        dst = a["spectra"][bass.ds(order, 1), n, f].rearrange("a p c t -> (a p) c t")
                        stored = s_spec.did(SC.dma_start(dst, kspec[:, f, :, :]), 16)
            spectra_stored = s_spec.val

            for m in range(MR):
                mod_chunk(m, m, Token(s_mod[m], Val(16)), m == 0)
            with p.loop(48 // MR - 1, {mod_used: MR, **{s: 16 for s in s_mod}}, extra=[mod_used, *s_mod]):
                for slot in range(MR):
                    m = Val(MR + slot, MR)
                    mod_fetch(m, slot)
                    mod_chunk(m, slot, Token(s_mod[slot], Val(32, 16)), False)
            wait(VE, Token(mod_used, mod_used.val))
            mod_done = dve.did(VE.tensor_tensor(MOD[:, :], ps[:, 7, 0:48], par_all("mod_b"), ALU.add))
            wait(SP, Token(s_spec, spectra_stored))
            for k in range(KD):
                got_x = s_x.did(SP.dma_start(X[:, k, :], a["xT"][k * P:(k + 1) * P, :]), 16)
            wait(VE, mod_done)
            SH1, SC1, G1, SH2, SC2, G2 = (MOD[:, 8 * i:8 * i + 8] for i in range(6))
            dve.did(VE.tensor_scalar(AFF[:, 0, 0, :], SC1, 1.0, None, ALU.add))
            t = dve.did(VE.tensor_scalar(AFF[:, 1, 1, :], SC2, 1.0, None, ALU.add))
            wait(VE, t)
            dve.did(VE.tensor_tensor(AFF[:, 1, 0, :], par_all("ln_g0"), AFF[:, 1, 1, :], ALU.mult))
            t = dve.did(VE.tensor_tensor(AFF[:, 1, 1, :], par_all("ln_b0"), AFF[:, 1, 1, :], ALU.mult))
            wait(VE, t)
            dve.did(VE.tensor_tensor(AFF[:, 1, 1, :], AFF[:, 1, 1, :], SH2, ALU.add))
            dve.did(VE.tensor_tensor(AFF[:, 0, 1, :], G1, par_all("pool_scale"), ALU.mult))
            for row, (g, b), alpha in ((2, ("ln_g0", "ln_b0"), ALPHA_1), (3, ("ln_g1", "ln_b1"), ALPHA_2),
                                       (4, ("a_g0", "a_b0"), ALPHA_2), (5, ("f_g0", "f_b0"), ALPHA_2),
                                       (6, ("a_g1", "a_b1"), ALPHA_2)):
                dve.did(VE.tensor_scalar(AFF[:, row, 0, :], par_all(g), alpha, None, ALU.mult))
                aff_done = dve.did(VE.tensor_scalar(AFF[:, row, 1, :], par_all(b), alpha, None, ALU.mult))
            stage1_dve = aff_done

        def layer_norm(tag, arrived, mean_by_sum, eps, to_a, keep, last=False):
            st = ExitStack()
            with st:
                sq = p.sb(st, f"{tag}_squares", [P, 2, T])
                val = p.sb(st, f"{tag}_values", [P, 2, T])
                settle(SC, VE)
                if mean_by_sum is not None:
                    wait(PE, arrived[-1], made_ones)
                    ins = PE.matmul(ps[:, 0, :], mean_w[:, :], mean_by_sum, start=True, stop=True)
                else:
                    for k in range(KD):
                        wait(PE, arrived[k])
                        ins = PE.matmul(ps[:, 0, :], mean_w[:, :], X[:, k, :], start=(k == 0), stop=(k == KD - 1))
                mean = pe.did(ins)
                wait(VE, mean)
                summed = [None] * KD
                for k in range(KD):
                    centred = dve.did(VE.tensor_tensor(X[:, k, :], X[:, k, :], ps[:, 0, :], ALU.subtract))
                    wait(SC, centred, summed[k - 2] if k >= 2 else None)
                    squared = act.did(SC.activation(sq[:, k % 2, :], X[:, k, :], ACT.Square))
                    wait(PE, squared)
                    for q in range(4):
                        ins = PE.matmul(ps[:, 1, q:q + 1], sq[:, k % 2, q * P:(q + 1) * P], ones[:, 0:1],
                                        start=(k == 0 and q == 0), stop=(k == KD - 1), skip_group_check=True)
                    summed[k] = pe.did(ins)
                wait(VE, summed[-1])
                t = dve.did(VE.tensor_scalar(stat[:, 0, :], ps[:, 1, 0:4], 1.0 / D, eps, ALU.mult, ALU.add))
                wait(GP, t)
                t = pool.did(GP.tensor_tensor(stat[:, 1, :], stat[:, 0, :], minus_half[:, :], ALU.pow))
                wait(PE, t)
                for q in range(4):
                    ins = PE.matmul(ps[:, 2, q * P:(q + 1) * P], stat[:, 1, q:q + 1].broadcast_to([P, P]),
                                    ident[:, :], start=True, stop=True, skip_group_check=True)
                rstd = pe.did(ins)
                wait(VE, rstd)
                ready, lows = [], []
                gain, bias = to_a if to_a is not None else (None, None)
                keep_g, keep_b = keep
                for k in range(KD):
                    normed = dve.did(VE.tensor_tensor(X[:, k, :], X[:, k, :], ps[:, 2, :], ALU.mult))
                    if last:
                        wait(SC, normed)
                        ready.append(act.did(SC.activation(X[:, k, :], X[:, k, :], ACT.Identity,
                                                           scale=keep_g[:, k:k + 1], bias=keep_b[:, k:k + 1])))
                        continue
                    wait(SC, normed)
                    hi = act.did(SC.activation(AH[:, k, :], X[:, k, :], ACT.Identity,
                                               scale=gain[:, k:k + 1], bias=bias[:, k:k + 1]))
                    wait(VE, normed, lows[k - 2] if k >= 2 else None)
                    value = dve.did(VE.tensor_scalar(val[:, k % 2, :], X[:, k, :], gain[:, k:k + 1],
                                                     bias[:, k:k + 1], ALU.mult, ALU.add))
                    if k % 2:
                        wait(VE, hi, value)
                        lows.append(dve.did(VE.tensor_tensor(AL[:, k, :], val[:, 1, :], f32(AH[:, k, :]),
                                                             ALU.subtract)))
                    else:
                        wait(GP, hi, value)
                        lows.append(pool.did(GP.tensor_tensor(AL[:, k, :], val[:, 0, :], f32(AH[:, k, :]),
                                                              ALU.subtract)))
                    ready.append(lows[-1])
                    wait(SC, value)
                    kept = act.did(SC.activation(X[:, k, :], X[:, k, :], ACT.Identity,
                                                 scale=keep_g[:, k:k + 1], bias=keep_b[:, k:k + 1]))
                if not last:
                    wait(VE, kept, lows[-2])
                    wait(SC, lows[-1], lows[-2])
                    wait(GP, lows[-1])
                return ready

        def settle(*engines):
            for engine in engines:
                wait(engine, *(Token(c, c.val) for c in (pe, act, dve, pool)))

        def conv3(dst, bank, taps, used_tok, free_tok):
            wait(SC, used_tok, free_tok)
            t = act.did(SC.activation(dst, ps[:, bank, :], ACT.Copy, scale=taps[1]))
            wait(VE, t)
            t = dve.did(VE.scalar_tensor_tensor(out=dst[:, 1:T], in0=ps[:, bank, 0:T - 1], scalar=taps[0],
                                                in1=dst[:, 1:T], op0=ALU.mult, op1=ALU.add))
            wait(VE, t)
            return dve.did(VE.scalar_tensor_tensor(out=dst[:, 0:T - 1], in0=ps[:, bank, 1:T], scalar=taps[2],
                                                   in1=dst[:, 0:T - 1], op0=ALU.mult, op1=ALU.add))

        def split_act(dst_hi, dst_lo, src, ready, hi_by=None):
            wait(VE, ready)
            hi = dve.did(VE.tensor_copy(dst_hi, src))
            wait(VE, hi)
            return dve.did(VE.tensor_tensor(dst_lo, src, f32(dst_hi), ALU.subtract))

        def column(name, k):
            at, n = PARAMS[name]
            if isinstance(k, Val) and k.step:
                return PV[:, bass.ds((k + at).of(p.index), 1)]
            k = k.const if isinstance(k, Val) else k
            return PV[:, at + k:at + k + 1]

        def ffn(tag, up, down, conv, a_ready, gate_col):
            st = ExitStack()
            with st:
                HH = p.sb(st, f"{tag}_hidden_hi", [P, KF, T], F32R)
                HL = p.sb(st, f"{tag}_hidden_lo", [P, KF, T], F32R)
                CA = p.sb(st, f"{tag}_value", [P, 2, T])
                CG = p.sb(st, f"{tag}_gate", [P, 2, T])
                HF = p.sb(st, f"{tag}_hidden", [P, 2, T])
                base_c = FIRST_CHUNK[up]
                settle(VE, SC)

                def pair(c, j, u, prev, tiles):
                    free_a, free_g, free_h = prev
                    order = (2 * u, 2 * u + 1)
                    for s in range(2):
                        cc = c + s
                        wh, wl = take(cc)
                        if s == 0:
                            wait(PE, free_a, free_g)
                        for k in range(KD):
                            if tiles is not None and s == 0:
                                wait(PE, tiles[k])
                            ins = mm3(ps[:, order[s], :], wh[:, k, :], wl[:, k, :], AH[:, k, :], AL[:, k, :],
                                      k == 0, k == KD - 1)
                        done = used.did(ins)
                        if s == 0:
                            first = done
                    if conv is None:
                        wait(SC, first, free_h)
                        g = act.did(SC.activation(CG[:, u, :], ps[:, order[0], :], ACT.Silu))
                        wait(VE, g, done)
                        h = dve.did(VE.tensor_tensor(HF[:, u, :], CG[:, u, :], ps[:, order[1], :], ALU.mult))
                        free_g = free_a = h
                    else:
                        av = conv3(CA[:, u, :], order[0], [column(conv, j * 3 + s) for s in range(3)], first, free_h)
                        gv = conv3(CG[:, u, :], order[1], [column(conv, j * 3 + (3 * KF + s)) for s in range(3)],
                                   done, None)
                        wait(SC, gv)
                        g = act.did(SC.activation(CG[:, u, :], CG[:, u, :], ACT.Silu))
                        wait(VE, g)
                        h = dve.did(VE.tensor_tensor(HF[:, u, :], CG[:, u, :], CA[:, u, :], ALU.mult))
                        free_a, free_g = av, gv
                    low = split_act(tile(HH, j), tile(HL, j), HF[:, u, :], h)
                    return free_a, free_g, h, low

                n_dve = 2 * (3 if conv is None else 7)
                n_act = 2 * (1 if conv is None else 3)
                f0 = pair(Val(base_c), 0, 0, (None, None, None), a_ready)
                f1 = pair(Val(base_c + 2), 1, 1, (None, None, None), None)
                with p.loop(KF // 2 - 1, per(4, dve=n_dve, act=n_act)):
                    for u, f in ((0, f0), (1, f1)):
                        prev = tuple(Token(t.count, Val(t.val.const, n_dve)) for t in f[:3])
                        g = pair(Val(base_c + 4 + 2 * u, 4), Val(2 + u, 2), u, prev, None)
                hidden_done = Token(dve, dve.val)

                base_d = FIRST_CHUNK[down]

                def down_chunk(c, k, first, last_):
                    wh, wl = take(c)
                    for m in range(KD):
                        ins = mm3(ps[:, m, :], wh[:, m, :], wl[:, m, :], tile(HH, k), tile(HL, k), first, last_)
                        if last_:
                            banks.append(pe.did(ins))
                    return ins

                banks = []
                wait(PE, hidden_done)
                used.did(down_chunk(Val(base_d), 0, True, False))
                used.did(down_chunk(Val(base_d + 1), 1, False, False))
                with p.loop(KF // 2 - 2, per(2)):
                    for s in range(2):
                        used.did(down_chunk(Val(base_d + 2 + s, 2), Val(2 + s, 2), False, False))
                used.did(down_chunk(Val(base_d + KF - 2), KF - 2, False, False))
                last_ins = down_chunk(Val(base_d + KF - 1), KF - 1, False, True)
                wait(PE, banks[-1])
                used.did(PE.nop())
                arrived = []
                for m in range(KD):
                    wait(VE, banks[m])
                    factor = gate_col[:, m:m + 1] if gate_col is not None else 1.0
                    arrived.append(dve.did(VE.scalar_tensor_tensor(out=X[:, m, :], in0=ps[:, m, :], scalar=factor,
                                                                   in1=X[:, m, :], op0=ALU.mult, op1=ALU.add)))
                return arrived

        def out_linear(tag, layer, rh, rl, tiles, st):
            acc = p.sb(st, f"{tag}_sum", [P, T])
            base = FIRST_CHUNK[layer]

            def one(c, m, s, first):
                wh, wl = take(c)
                out_bank = tile(ps, m)
                for k in range(KD):
                    if first:
                        wait(PE, tiles[k])
                    ins = mm3(out_bank, wh[:, k, :], wl[:, k, :], rh[:, k, :], rl[:, k, :], k == 0, k == KD - 1)
                done = used.did(ins)
                wait(VE, done)
                t = dve.did(VE.tensor_tensor(tile(X, m), tile(X, m), out_bank, ALU.add))
                wait(VE, t)
                if first:
                    return dve.did(VE.tensor_copy(acc[:, :], tile(X, m)))
                return dve.did(VE.tensor_tensor(acc[:, :], acc[:, :], tile(X, m), ALU.add))

            one(Val(base), Val(0), 0, True)
            one(Val(base + 1), Val(1), 1, False)
            with p.loop(KD // 2 - 1, per(2, dve=4)):
                for s in range(2):
                    t = one(Val(base + 2 + s, 2), Val(2 + s, 2), s, False)
            return [Token(dve, dve.val)], acc[:, :]

        fetch(Val(0))
        fetch(Val(1))
        split(Val(0))

        s2 = ExitStack()
        with s2:
            hx = p.sb(s2, "pool_in", [P, 2, T + 2 * PAD])
            wa = p.sb(s2, "pool_sum_a", [P, T + 2 * PAD])
            wb = p.sb(s2, "pool_sum_b", [P, T + 2 * PAD])
            icnt = p.sb(s2, "pool_1_over_count", [P, 4, T])
            df = p.sb(s2, "pool_diff", [P, 2, T])
            settle(SP, VE, SC)
            wait(SP, Token(mod_used, mod_used.val))
            wait(VE, Token(mod_used, mod_used.val))
            got_cnt = s_con.did(SP.dma_start(icnt[:, :, :], a["inv_count"]), 16)
            t = dve.did(VE.memset(hx[:, :, :], 0.0))
            wait(VE, got_x, got_cnt, stage1_dve, t)
            wait(SC, stage1_dve, got_x)
            lows = []
            scaled = []
            diff_read = [None, None]
            L = T + 2 * PAD
            for g, w in enumerate(POOL_WINDOWS):
                for half in range(2):
                    k = 2 * g + half
                    slot = k % 2
                    x_in = hx[:, slot, PAD:PAD + T]
                    t = dve.did(VE.tensor_scalar(x_in, X[:, k, :], AFF[:, 0, 0, k:k + 1], MOD[:, k:k + 1],
                                                 ALU.mult, ALU.add))
                    wait(SC, t)
                    scaled.append(act.did(SC.activation(X[:, k, :], X[:, k, :], ACT.Copy, scale=ALPHA_1)))
                    src, dsts = hx[:, slot, :], (wa, wb)
                    reach, width, at = 0, 2, 0
                    lo, hi = 1, 0
                    low_edge, high_edge = 1, L
                    while True:
                        dst = dsts[at % 2]
                        wait(VE, t)
                        t = dve.did(VE.tensor_tensor(dst[:, low_edge:high_edge],
                                                     src[:, low_edge - lo:high_edge - lo],
                                                     src[:, low_edge + hi:high_edge + hi], ALU.add))
                        if width == w:
                            break
                        src, lo = dst, width // 2
                        hi = width // 2
                        low_edge, high_edge = low_edge + lo, high_edge - hi
                        width *= 2
                        at += 1
                    wait(VE, t)
                    t = dve.did(VE.tensor_tensor(df[:, slot, :], dst[:, PAD:PAD + T], icnt[:, g, :], ALU.mult))
                    wait(VE, t)
                    t = dve.did(VE.tensor_tensor(df[:, slot, :], df[:, slot, :], x_in, ALU.subtract))
                    lows.append(split_act(AH[:, k, :], AL[:, k, :], df[:, slot, :], t))
            arrived = []
            for cc in range(2):
                wh, wl = take(Val(cc))
                banks = []
                for g2 in range(2):
                    g = 2 * cc + g2
                    wait(PE, lows[2 * g + 1])
                    for m in range(2):
                        for k in range(2):
                            b = (g2 * 2 + m) * 2 + k
                            ins = mm3(ps[:, 2 * g + m, :], wh[:, b, :], wl[:, b, :], AH[:, 2 * g + k, :],
                                      AL[:, 2 * g + k, :], k == 0, k == 1)
                done = used.did(ins)
                wait(VE, done)
                for m in range(4 * cc, 4 * cc + 4):
                    wait(VE, scaled[m])
                    arrived.append(dve.did(VE.scalar_tensor_tensor(out=X[:, m, :], in0=ps[:, m, :],
                                                                   scalar=AFF[:, 0, 1, m:m + 1], in1=X[:, m, :],
                                                                   op0=ALU.mult, op1=ALU.add)))
        ready = layer_norm("n0", arrived, None, EPS_1, (AFF[:, 1, 0, :], AFF[:, 1, 1, :]),
                           (AFF[:, 2, 0, :], AFF[:, 2, 1, :]))
        arrived = ffn("f0", "up_1", "down_1", None, ready, G2)
        ready = layer_norm("n1", arrived, None, EPS_1, (par_all("ln_g1"), par_all("ln_b1")),
                           (AFF[:, 3, 0, :], AFF[:, 3, 1, :]))

        s4 = ExitStack()
        with s4:
            OH = p.sb(s4, "heads_hi", [P, HEADS, T], F32R)
            OL = p.sb(s4, "heads_lo", [P, HEADS, T], F32R)
            cosv = p.sb(s4, "rope_cos", [P, T])
            sinv = p.sb(s4, "rope_sin", [P, T])
            swap = p.sb(s4, "rope_swap", [P, P])
            rc = p.sb(s4, "rope_consts", [P, 2])
            krh = p.sb(s4, "k_rope_hi", [P, T], F32R)
            krl = p.sb(s4, "k_rope_lo", [P, T], F32R)
            W0 = p.sb(s4, "rope_a", [P, T])
            W1 = p.sb(s4, "rope_b", [P, T])
            s_rope = p.count("rope")
            settle(SP, VE, SC)
            s_rope.did(SP.dma_start(swap[:, :], a["rope_swap"]), 16)
            s_rope.did(SP.dma_start(rc[:, :], a["rope_consts"]), 16)
            s4a = ExitStack()
            with s4a:
                LAT = p.sb(s4a, "latents", [P, 6, T])
                posi = p.sb(s4a, "positions", [P, T], I32)
                turns = p.sb(s4a, "rope_turns", [P, T])
                sq2 = p.sb(s4a, "rms_squares", [P, 2, T])
                got_rope = s_rope.did(SP.dma_start(posi[:, :], a["positions"].broadcast_to([P, T])), 16)
                wait(VE, got_rope)
                t = dve.did(VE.tensor_copy(W0[:, :], posi[:, :]))
                wait(VE, t)
                t = dve.did(VE.tensor_scalar(W0[:, :], W0[:, :], rc[:, 0:1], None, ALU.mult))
                wait(VE, t)
                t = reduce_sin(None, W0[:, :], turns[:, :], P)
                wait(SC, t)
                sine = act.did(SC.activation(sinv[:, :], W0[:, :], ACT.Sin))
                wait(VE, t)
                t = dve.did(VE.scalar_tensor_tensor(out=turns[:, :], in0=W0[:, :], scalar=-1.0, in1=W0[:, :],
                                                    op0=ALU.mult, op1=ALU.max))
                wait(VE, t)
                t = dve.did(VE.tensor_scalar(turns[:, :], turns[:, :], -1.0, math.pi / 2, ALU.mult, ALU.add))
                wait(SC, t)
                cosine = act.did(SC.activation(cosv[:, :], turns[:, :], ACT.Sin))
                wait(VE, sine)
                signed = dve.did(VE.tensor_scalar(sinv[:, :], sinv[:, :], rc[:, 1:2], None, ALU.mult))

                base = FIRST_CHUNK["mla_in"]
                lat = []
                for m in range(6):
                    wh, wl = take(Val(base + m))
                    for k in range(KD):
                        if m == 0:
                            wait(PE, ready[k])
                        ins = mm3(ps[:, m, :], wh[:, k, :], wl[:, k, :], AH[:, k, :], AL[:, k, :],
                                  k == 0, k == KD - 1)
                    done = used.did(ins)
                    wait(SC, done)
                    lat.append(act.did(SC.activation(LAT[:, m, :], ps[:, m, :], ACT.Copy)))
                sums, free = [], [None, None]
                for m in range(KQ + KKV):
                    group, first = (6, m == 0) if m < KQ else (7, m == KQ)
                    wait(SC, lat[m], free[m % 2])
                    t = act.did(SC.activation(sq2[:, m % 2, :], LAT[:, m, :], ACT.Square))
                    wait(PE, t)
                    for q in range(4):
                        ins = PE.matmul(ps[:, group, q:q + 1], sq2[:, m % 2, q * P:(q + 1) * P], ones[:, 0:1],
                                        start=(first and q == 0), stop=(m in (KQ - 1, KQ + KKV - 1)),
                                        skip_group_check=True)
                    free[m % 2] = pe.did(ins)
                a_lows = []
                for g, (bank, rank, first, n) in enumerate(((6, RQ, 0, KQ), (7, RKV, KQ, KKV))):
                    wait(VE, free[0], free[1])
                    t = dve.did(VE.tensor_scalar(stat[:, 2 * g, :], ps[:, bank, 0:4], 1.0 / rank, EPS_RMS,
                                                 ALU.mult, ALU.add))
                    wait(GP, t)
                    t = pool.did(GP.tensor_tensor(stat[:, 2 * g + 1, :], stat[:, 2 * g, :], minus_half[:, :],
                                                  ALU.pow))
                    wait(PE, t, lat[g])
                    for q in range(4):
                        ins = PE.matmul(ps[:, g, q * P:(q + 1) * P],
                                        stat[:, 2 * g + 1, q:q + 1].broadcast_to([P, P]),
                                        ident[:, :], start=True, stop=True, skip_group_check=True)
                    t = pe.did(ins)
                    wait(VE, t, lat[5])
                    for m in range(first, first + n):
                        gcol = par("g_q", m) if g == 0 else par("g_kv", m - KQ)
                        t = dve.did(VE.scalar_tensor_tensor(out=LAT[:, m, :], in0=LAT[:, m, :], scalar=gcol,
                                                            in1=ps[:, g, :], op0=ALU.mult, op1=ALU.mult))
                        a_lows.append(split_act(AH[:, m, :], AL[:, m, :], LAT[:, m, :], t))

                def rotate(bank_swap, src, tmp, dst_hi, dst_lo, ready_tok):
                    wait(PE, ready_tok, got_rope)
                    t1 = pe.did(PE.matmul(ps[:, bank_swap, :], swap[:, :], src, start=True, stop=True))
                    wait(VE, t1, signed)
                    t2 = dve.did(VE.tensor_tensor(tmp, sinv[:, :], ps[:, bank_swap, :], ALU.mult))
                    wait(VE, t1, cosine)
                    t3 = dve.did(VE.tensor_tensor(src, src, cosv[:, :], ALU.mult))
                    wait(VE, t2, t3)
                    t4 = dve.did(VE.tensor_tensor(src, src, tmp, ALU.add))
                    return split_act(dst_hi, dst_lo, src, t4)

                wait(PE, a_lows[-1])
                k_rope = rotate(2, LAT[:, 5, :], W1[:, :], krh[:, :], krl[:, :], lat[5])
                lat_done = k_rope

            QH = p.sb(s4, "q_hi", [P, 6, T], F32R)
            QL = p.sb(s4, "q_lo", [P, 6, T], F32R)
            KH = p.sb(s4, "k_hi", [P, 4, T], F32R)
            KL = p.sb(s4, "k_lo", [P, 4, T], F32R)
            VH = p.sb(s4, "v_hi", [P, 4, T], F32R)
            VL = p.sb(s4, "v_lo", [P, 4, T], F32R)
            PB = p.sb(s4, "probabilities", [P, 2, T])
            PTH = p.sb(s4, "probs_t_hi", [P, 4, T], F32R)
            PTL = p.sb(s4, "probs_t_lo", [P, 4, T], F32R)
            sm = p.sb(s4, "softmax_stats", [P, 4, 4])
            settle(VE, SC, PE)
            base = FIRST_CHUNK["mla_heads"]

            def head_group(g, base_c):
                banks_read = {}
                for ch in range(4):
                    wh, wl = take(base_c + ch)
                    tiles_of = (2 * ch, 2 * ch + 1) if ch < 2 else (2 + ch,)
                    for i, m in enumerate(tiles_of):
                        for k in range(KQ):
                            b = i * KQ + k
                            ins = mm3(ps[:, m, :], wh[:, b, :], wl[:, b, :], AH[:, k, :], AL[:, k, :],
                                      k == 0, k == KQ - 1)
                    done = used.did(ins)
                    for m in tiles_of:
                        if ch < 2:
                            wait(SC, done)
                            hi = act.did(SC.activation(QH[:, m, :], ps[:, m, :], ACT.Copy))
                            wait(VE, hi)
                            banks_read[m] = dve.did(VE.tensor_tensor(QL[:, m, :], ps[:, m, :], f32(QH[:, m, :]),
                                                                     ALU.subtract))
                        else:
                            wait(SC, done, banks_read.get("w0"))
                            raw = act.did(SC.activation(W0[:, :], ps[:, m, :], ACT.Copy))
                            banks_read["w0"] = rotate(6, W0[:, :], W1[:, :], QH[:, m, :], QL[:, m, :], raw)
                wh, wl = take(base_c + 4)
                wait(PE, *[banks_read[m] for m in range(4)])
                for h in range(4):
                    for k in range(KKV):
                        ins = mm3(ps[:, h, :], wh[:, h * KKV + k, :], wl[:, h * KKV + k, :], AH[:, KQ + k, :],
                                  AL[:, KQ + k, :], k == 0, k == KKV - 1)
                done = used.did(ins)
                kread = []
                for h in range(4):
                    wait(SC, done)
                    hi = act.did(SC.activation(KH[:, h, :], ps[:, h, :], ACT.Copy))
                    wait(VE, hi)
                    kread.append(dve.did(VE.tensor_tensor(KL[:, h, :], ps[:, h, :], f32(KH[:, h, :]), ALU.subtract)))
                slot = (base_c + 5).const % 2
                take(base_c + 5)
                vread = []
                wait(PE, banks_read["w0"])
                for q in range(4):
                    bank = 4 + q
                    for k in range(KKV):
                        cols = slice(q * P, (q + 1) * P)
                        ins = mm3(ps[:, bank, :], AH[:, KQ + k, cols], AL[:, KQ + k, cols],
                                  WH[:, slot, k * T:(k + 1) * T], WL[:, slot, k * T:(k + 1) * T],
                                  k == 0, k == KKV - 1)
                done = used.did(ins)
                for q in range(4):
                    wait(SC, done)
                    hi = act.did(SC.activation(VH[:, q, :], ps[:, 4 + q, :], ACT.Copy))
                    wait(VE, hi)
                    vread.append(dve.did(VE.tensor_tensor(VL[:, q, :], ps[:, 4 + q, :], f32(VH[:, q, :]),
                                                          ALU.subtract)))
                wait(PE, kread[-1], vread[-1])
                score_read = {}
                pt_read = {}
                pv_done = {}
                o_read = {}
                p_free = {}
                for h in range(4):
                    rows = slice((h % 2) * ROPE, (h % 2) * ROPE + ROPE)
                    scores = []
                    for q in range(4):
                        cols = slice(q * P, (q + 1) * P)
                        wait(PE, score_read.get(q))
                        mm3(ps[:, q, :], QH[:, h, cols], QL[:, h, cols], KH[:, h, :], KL[:, h, :], True, False)
                        ins = mm3(ps[:, q, :], QH[rows, 4 + h // 2, cols], QL[rows, 4 + h // 2, cols],
                                  krh[rows, :], krl[rows, :], False, True)
                        scores.append(pe.did(ins))
                    pts = []
                    for q in range(4):
                        n = 4 * h + q
                        slot = n % 2
                        wait(VE, scores[q])
                        t = dve.did(VE.tensor_reduce(sm[:, q, 0:1], ps[:, q, :], AX_X, ALU.max))
                        wait(VE, t)
                        t = dve.did(VE.tensor_scalar(sm[:, q, 1:2], sm[:, q, 0:1], -SM_SCALE, None, ALU.mult))
                        wait(SC, t, p_free.get(slot))
                        e = act.did(SC.activation(PB[:, slot, :], ps[:, q, :], ACT.Exp, bias=sm[:, q, 1:2],
                                                  scale=SM_SCALE, accum_out=sm[:, q, 2:3]))
                        score_read[q] = e
                        wait(VE, e)
                        t = dve.did(VE.reciprocal(sm[:, q, 3:4], sm[:, q, 2:3]))
                        wait(VE, t)
                        t = dve.did(VE.tensor_scalar(PB[:, slot, :], PB[:, slot, :], sm[:, q, 3:4], None, ALU.mult))
                        bank = 4 + slot
                        wait(PE, t, pt_read.get(bank))
                        for kt in range(4):
                            ins = PE.transpose(ps[:, bank, kt * P:(kt + 1) * P], PB[:, slot, kt * P:(kt + 1) * P],
                                               ident[:, :])
                        t = pe.did(ins)
                        p_free[slot] = t
                        cols = slice(q * P, (q + 1) * P)
                        src = ps[:, bank, :].rearrange("p (k q) -> p k q", k=4)
                        wait(SC, t, pv_done.get("last"))
                        hi = act.did(SC.activation(PTH[:, :, cols], src, ACT.Copy))
                        wait(VE, hi)
                        pt_read[bank] = dve.did(VE.tensor_tensor(PTL[:, :, cols], src, f32(PTH[:, :, cols]),
                                                                 ALU.subtract))
                    bank = 6 + h % 2
                    wait(PE, pt_read[4], pt_read[5], o_read.get(bank))
                    for kt in range(4):
                        ins = mm3(ps[:, bank, :], VH[:, kt, h * P:(h + 1) * P], VL[:, kt, h * P:(h + 1) * P],
                                  PTH[:, kt, :], PTL[:, kt, :], kt == 0, kt == 3)
                    pv_done["last"] = pe.did(ins)
                    wait(SC, pv_done["last"])
                    oh, ol = tile(OH, g + h), tile(OL, g + h)
                    hi = act.did(SC.activation(oh, ps[:, bank, :], ACT.Copy))
                    wait(VE, hi)
                    o_read[bank] = dve.did(VE.tensor_tensor(ol, ps[:, bank, :], f32(oh), ALU.subtract))
                wait(PE, o_read[6], o_read[7])
                wait(SC, pv_done["last"])
                wait(VE, pv_done["last"])

            with p.loop(N_GROUPS, per(6, pe=2 + 4 * (4 + 4 + 1), act=4 + 2 + 4 + 4 + 4 * (4 + 4 + 1),
                                      dve=4 + 2 * 5 + 4 + 4 + 4 * (4 * 5 + 1))):
                head_group(Val(0, 4), Val(base, 6))
            heads_done = Token(dve, dve.val)
            arrived, acc = out_linear("mla", "mla_out", OH, OL, [heads_done] * KD, s4)
            ready = layer_norm("n2", arrived, acc, EPS_2, (par_all("a_g0"), par_all("a_b0")),
                               (AFF[:, 4, 0, :], AFF[:, 4, 1, :]))

        arrived = ffn("f1", "up_2", "down_2", "conv0", ready, None)
        ready = layer_norm("n3", arrived, None, EPS_2, (par_all("f_g0"), par_all("f_b0")),
                           (AFF[:, 5, 0, :], AFF[:, 5, 1, :]))

        s5 = ExitStack()
        with s5:
            U = p.sb(s5, "hy_branches", [P, 24, T])
            YH = p.sb(s5, "hy_product_hi", [P, 2, 4, T], F32R)
            YL = p.sb(s5, "hy_product_lo", [P, 2, 4, T], F32R)
            FH = p.sb(s5, "dft_fwd_hi", [P, 16, P], F32R)
            FL = p.sb(s5, "dft_fwd_lo", [P, 16, P], F32R)
            IH = p.sb(s5, "dft_inv_hi", [P, 8, HALF], F32R)
            IL = p.sb(s5, "dft_inv_lo", [P, 8, HALF], F32R)
            KS = p.sb(s5, "hy_filter", [P, 4, T])
            s_tab, s_xs, s_ks = p.count("tables"), p.count("x_spill"), p.count("filter_load")
            spilled = []
            SP_wait = ready
            kept_all = Token(act, act.val)
            wait(SP, kept_all)
            for k in range(KD):
                spilled = s_xs.did(SP.dma_start(a["x_spill"][k], X[:, k, :]), 16)
            base = FIRST_CHUNK["hy_in"]
            settle(VE, SC, SP)

            def branch(c, m, u, prev, tiles):
                wh, wl = take(c)
                wait(PE, prev)
                for k in range(KD):
                    if tiles is not None:
                        wait(PE, tiles[k])
                    ins = mm3(ps[:, u, :], wh[:, k, :], wl[:, k, :], AH[:, k, :], AL[:, k, :], k == 0, k == KD - 1)
                done = used.did(ins)
                return conv3(tile(U, m), u, [column("hy_short", m * 3 + s) for s in range(3)], done, None)

            b0 = branch(Val(base), Val(0), 0, None, ready)
            b1 = branch(Val(base + 1), Val(1), 1, None, None)
            with p.loop(11, per(2, act=2, dve=4)):
                for u, b in ((0, b0), (1, b1)):
                    branch(Val(base + 2 + u, 2), Val(2 + u, 2), u, Token(dve, Val(b.val.const, 4)), None)
            branches = Token(dve, dve.val)

            raw_t = X[:, 0:4, :].rearrange("p a b -> p (a b)")
            raw_i = X[:, 4:8, :].rearrange("p a b -> p (a b)")
            wait(SP, spilled)
            s_tab.did(SP.dma_start(raw_t, a["dft_fwd"].rearrange("p a b -> p (a b)")), 16)
            got_tabs = s_tab.did(SP.dma_start(raw_i, a["dft_inv"].rearrange("p a b -> p (a b)")), 16)
            wait(VE, got_tabs)
            flat = lambda t: t[:, :, :].rearrange("p a b -> p (a b)")
            for raw_, h_, l_ in ((raw_t, FH, FL), (raw_i, IH, IL)):
                tabs_done = split_act(flat(h_), flat(l_), raw_, None)

            def conv_half(order, n, z_ready):
                wait(PE, z_ready)
                zsplit = []
                for q in range(4):
                    for m in range(4):
                        zt_ = U[:, 4 * n + m, :].rearrange("p (t two) -> p two t", two=2)
                        src = zt_[:, q // 2, (q % 2) * P:(q % 2 + 1) * P]
                        ins = PE.transpose(ps[:, q, m * P:(m + 1) * P], src, ident[:, :])
                    t = pe.did(ins)
                    wait(SC, t)
                    hi = act.did(SC.activation(AH[:, 4 + q, :], ps[:, q, :], ACT.Copy))
                    wait(VE, hi)
                    zsplit.append(dve.did(VE.tensor_tensor(AL[:, 4 + q, :], ps[:, q, :], f32(AH[:, 4 + q, :]),
                                                           ALU.subtract)))
                wait(PE, zsplit[-1])
                mult_done = zsplit[-1]
                for f in range(2):
                    wait(SP, mult_done, tabs_done, Token(s_spec, Val(s_spec.val.const)))
                    ks = s_ks.did(SP.dma_start(KS[:, :, :], a["spectra"][order, n, f]), 16)
                    for kind in range(2):
                        for parity in range(2):
                            for k in range(2):
                                b = ((kind * 2 + parity) * 2 + k) * 2 + f
                                ins = mm3(ps[:, 4 * (1 - f) + 2 * kind + parity, :], FH[:, b, :], FL[:, b, :],
                                          AH[:, 4 + 2 * parity + k, :], AL[:, 4 + 2 * parity + k, :], k == 0, k == 1)
                    fwd = pe.did(ins)
                    bk = 4 * (1 - f)
                    S = lambda i: X[:, i, :]
                    wait(SC, fwd, mult_done)
                    act.did(SC.activation(S(4), ps[:, bk + 1, :], ACT.Copy))
                    t = act.did(SC.activation(S(5), ps[:, bk + 3, :], ACT.Copy))
                    wait(VE, t, mult_done)
                    dve.did(VE.tensor_tensor(S(0), ps[:, bk, :], S(4), ALU.add))
                    dve.did(VE.tensor_tensor(S(1), ps[:, bk + 2, :], S(5), ALU.add))
                    dve.did(VE.tensor_tensor(S(2), ps[:, bk, :], S(4), ALU.subtract))
                    zpm = dve.did(VE.tensor_tensor(S(3), ps[:, bk + 2, :], S(5), ALU.subtract))
                    wait(GP, zpm, ks)
                    pool.did(GP.tensor_tensor(S(6), S(2), KS[:, 1, :], ALU.mult))
                    t = pool.did(GP.tensor_tensor(S(7), S(3), KS[:, 3, :], ALU.mult))
                    wait(GP, t)
                    t = pool.did(GP.tensor_tensor(S(6), S(6), S(7), ALU.subtract))
                    pool.did(GP.tensor_tensor(S(2), S(2), KS[:, 3, :], ALU.mult))
                    t = pool.did(GP.tensor_tensor(S(3), S(3), KS[:, 1, :], ALU.mult))
                    wait(GP, t)
                    vdone = pool.did(GP.tensor_tensor(S(2), S(2), S(3), ALU.add))
                    wait(VE, zpm, ks)
                    dve.did(VE.tensor_tensor(S(4), S(0), KS[:, 0, :], ALU.mult))
                    t = dve.did(VE.tensor_tensor(S(5), S(1), KS[:, 2, :], ALU.mult))
                    wait(VE, t)
                    dve.did(VE.tensor_tensor(S(4), S(4), S(5), ALU.subtract))
                    dve.did(VE.tensor_tensor(S(0), S(0), KS[:, 2, :], ALU.mult))
                    t = dve.did(VE.tensor_tensor(S(1), S(1), KS[:, 0, :], ALU.mult))
                    wait(VE, t)
                    t = dve.did(VE.tensor_tensor(S(0), S(0), S(1), ALU.add))
                    wait(VE, t, vdone)
                    sums = []
                    for i, (dst, x1, x2, op) in enumerate(((1, 4, 6, ALU.add), (3, 0, 2, ALU.add),
                                                           (5, 4, 6, ALU.subtract), (7, 0, 2, ALU.subtract))):
                        sums.append(dve.did(VE.tensor_tensor(S(dst), S(x1), S(x2), op)))
                    for i, dst in enumerate((1, 3, 5, 7)):
                        wait(SC, sums[i])
                        hi = act.did(SC.activation(YH[:, f, i, :], S(dst), ACT.Copy))
                        wait(VE, hi)
                        mult_done = dve.did(VE.tensor_tensor(YL[:, f, i, :], S(dst), f32(YH[:, f, i, :]),
                                                             ALU.subtract))
                wait(PE, mult_done)
                outs = []
                for m in range(4):
                    for parity in range(2):
                        n_k = 0
                        for f in range(2):
                            for kind in range(2):
                                b = (kind * 2 + parity) * 2 + f
                                cols = slice(m * P, (m + 1) * P)
                                ins = mm3(ps[:, m, parity * HALF:(parity + 1) * HALF],
                                          YH[:, f, 2 * parity + kind, cols], YL[:, f, 2 * parity + kind, cols],
                                          IH[:, b, :], IL[:, b, :], n_k == 0, n_k == 3)
                                n_k += 1
                    t = pe.did(ins)
                    wait(VE, t)
                    view = lambda ap: ap.rearrange("p (t two) -> p two t", two=2)
                    z = U[:, 4 * n + m, :]
                    gate = U[:, 8 * (order + 1) + 4 * n + m, :]
                    y = ps[:, m, :].rearrange("p (two t) -> p two t", two=2)
                    t = dve.did(VE.scalar_tensor_tensor(out=view(z), in0=view(z),
                                                        scalar=par("hy_d", 8 * order + 4 * n + m), in1=y,
                                                        op0=ALU.mult, op1=ALU.add))
                    wait(VE, t)
                    t = dve.did(VE.tensor_tensor(z, z, gate, ALU.mult))
                    if order == 1:
                        t = split_act(AH[:, 4 * n + m, :], AL[:, 4 * n + m, :], z, t)
                    outs.append(t)
                wait(PE, outs[-1])
                return outs

            z0 = conv_half(0, 0, branches)
            z1 = conv_half(0, 1, branches)
            r0 = conv_half(1, 0, z0[-1])
            r1 = conv_half(1, 1, z1[-1])
            wait(SP, r1[-1])
            for k in range(KD):
                back = s_xs.did(SP.dma_start(X[:, k, :], a["x_spill"][k]), 16)
            wait(VE, back)
            arrived, acc = out_linear("hy", "hy_out", AH, AL, r0 + r1, s5)
            ready = layer_norm("n4", arrived, acc, EPS_2, (par_all("a_g1"), par_all("a_b1")),
                               (AFF[:, 6, 0, :], AFF[:, 6, 1, :]))

        arrived = ffn("f2", "up_3", "down_3", "conv1", ready, None)
        done = layer_norm("n5", arrived, None, EPS_2, None, (par_all("f_g1"), par_all("f_b1")), last=True)
        s_out = p.count("stored")
        for k in range(KD):
            wait(SP, done[k])
            stored = s_out.did(SP.dma_start(out[k * P:(k + 1) * P, :], X[:, k, :]), 16)
        wait(SP, stored)
        wait(SP, Token(s_xs, s_xs.val))


def time_order():
    return np.concatenate([np.arange(0, T, 2), np.arange(1, T, 2)])


def shape_constants():
    f32 = np.float32
    order = time_order()
    freq = (2 * np.arange(HALF) + 1) * np.pi / (2 * T)
    fwd = np.zeros((P, 16, P), f32)
    inv = np.zeros((P, 8, HALF), f32)
    for kind, fn in enumerate((np.cos, np.sin)):
        for parity in range(2):
            times = np.arange(parity, T, 2)
            table = fn(np.outer(times, freq))
            for k in range(2):
                for f in range(2):
                    fwd[:, ((kind * 2 + parity) * 2 + k) * 2 + f] = table[k * P:(k + 1) * P, f * P:(f + 1) * P]
            for f in range(2):
                inv[:, (kind * 2 + parity) * 2 + f] = table.T[f * P:(f + 1) * P] / T
    t = np.linspace(0.0, 1.0, T, dtype=f32)[:, None]
    bands = (HY_EMB - 1) // 2
    w = (2.0 * math.pi * np.arange(T, dtype=f32)[:, None] / T).astype(f32)
    fr = np.linspace(1e-4, bands - 1, bands, dtype=f32)[None, :]
    z = np.concatenate([t, np.cos(fr * w), -np.sin(fr * w)], axis=-1).astype(f32)
    deltas = np.abs(np.linspace(math.log(0.3) / 1e-2, math.log(1.5) / 1e-2, D, dtype=f32))
    decay = np.exp(-t * deltas).astype(f32)
    steps = np.arange(T)
    counts = []
    for win in POOL_WINDOWS:
        lo = win // 2
        start, end = np.clip(steps - lo, 0, T), np.clip(steps + win - lo, 0, T)
        counts.append(1.0 / (end - start))
    inv_freq = (1.0 / (10000.0 ** (np.arange(0, ROPE, 2, dtype=f32) / f32(ROPE)))).astype(f32)
    rope = np.stack([np.tile(inv_freq, 4), np.tile(np.repeat([-1.0, 1.0], ROPE // 2), 2)], 1).astype(f32)
    swap = np.zeros((P, P), f32)
    rows = np.arange(P)
    swap[rows, rows ^ (ROPE // 2)] = 1.0
    return {
        "dft_fwd": fwd, "dft_inv": inv, "hy_z": np.ascontiguousarray(z[order].T),
        "decay": np.ascontiguousarray(decay[order].reshape(4, P, D).transpose(1, 0, 2)),
        "inv_count": np.ascontiguousarray(np.broadcast_to(np.array(counts, f32), (P, 4, T))),
        "rope_consts": rope, "rope_swap": swap, "identity": np.eye(P, dtype=f32),
    }


def columns(v):
    return np.asarray(v).reshape(-1, P).T


def by_output_tile(w):
    k, m = w.shape
    return w.reshape(k // P, P, m // P, P).transpose(2, 1, 0, 3).reshape(m // P, P, k)


def weight_stream(i):
    parts = []
    pw = i["pool_w"][0].reshape(2, 2, 2, P, 2, P)
    parts.append(pw.transpose(0, 3, 1, 4, 2, 5).reshape(2, P, CHUNK))
    w = by_output_tile(i["ffn_w_in"][0])
    parts.append(w.reshape(2, KF, P, CHUNK).transpose(1, 0, 2, 3).reshape(2 * KF, P, CHUNK))
    parts.append(i["ffn_w_out"][0].reshape(KF, P, D))
    w = i["mla_w_in_2"][0]
    parts.append(by_output_tile(np.concatenate([w, w[:, RQ + RKV:]], axis=1)))
    uq = i["mla_w_uq_2"][0].reshape(KQ, P, HEADS, NOPE + ROPE)
    ukv = i["mla_w_ukv_2"][0].reshape(KKV, P, HEADS, NOPE + VD)
    for g in range(N_GROUPS):
        hs = slice(4 * g, 4 * g + 4)
        nope = uq[:, :, hs, :NOPE].reshape(KQ, P, 2, 2, P).transpose(2, 1, 3, 0, 4).reshape(2, P, 2 * KQ * P)
        rope = uq[:, :, hs, NOPE:].reshape(KQ, P, 2, P).transpose(2, 1, 0, 3).reshape(2, P, KQ * P)
        for part in (nope, rope):
            padded = np.zeros((2, P, CHUNK), part.dtype)
            padded[:, :, :part.shape[2]] = part
            parts.append(padded)
        parts.append(ukv[:, :, hs, :NOPE].transpose(1, 2, 0, 3).reshape(1, P, CHUNK))
        parts.append(ukv[:, :, hs, NOPE:].transpose(1, 0, 2, 3).reshape(1, P, CHUNK))
    parts.append(by_output_tile(i["mla_w_o_2"][0]))

    def conv_ffn(layer):
        w = by_output_tile(i["ffn_w_up_2"][layer])
        parts.append(w.reshape(2, KF, P, CHUNK).transpose(1, 0, 2, 3).reshape(2 * KF, P, CHUNK))
        parts.append(i["ffn_w_down_2"][layer].reshape(KF, P, D))

    conv_ffn(0)
    parts.append(by_output_tile(i["hy_w_in_2"][0]))
    parts.append(by_output_tile(i["hy_w_o_2"][0]))
    conv_ffn(1)
    out = np.concatenate(parts, axis=0)
    assert out.shape == (N_CHUNKS, P, CHUNK), out.shape
    return out


def taps(w):
    return w.reshape(3, -1, P).transpose(2, 1, 0).reshape(P, -1)


def lay_out(i):
    cols = {
        "c": columns(i["c"][0]), "mod_b": columns(i["mod_b"][0]),
        "ln_g0": columns(i["ln_g"][0, 0]), "ln_b0": columns(i["ln_b"][0, 0]),
        "ln_g1": columns(i["ln_g"][0, 1]), "ln_b1": columns(i["ln_b"][0, 1]),
        "pool_scale": columns(i["pool_scale"][0]), "g_q": columns(i["mla_g_q_2"][0]),
        "g_kv": columns(i["mla_g_kv_2"][0]), "hy_short": taps(i["hy_w_short_2"][0]),
        "hy_d": columns(i["hy_d_bias_2"][0]), "conv0": taps(i["ffn_w_conv_2"][0]),
        "conv1": taps(i["ffn_w_conv_2"][1]),
    }
    for layer in range(2):
        for key, name in (("a", "ln1"), ("f", "ln2")):
            cols[f"{key}_g{layer}"] = columns(i[f"{name}_g_2"][layer])
            cols[f"{key}_b{layer}"] = columns(i[f"{name}_b_2"][layer])
    arrays = {
        "params": np.ascontiguousarray(np.concatenate([cols[n] for n in PARAMS], axis=1)),
        "xT": np.ascontiguousarray(i["x"][0].T),
        "mod_w": np.ascontiguousarray(by_output_tile(i["mod_w"][0])),
        "w_stream": weight_stream(i),
        "positions": np.ascontiguousarray(i["positions_2"]),
        "hy_fw1": np.ascontiguousarray(i["hy_fw1_2"][0]),
        "hy_small": np.ascontiguousarray(np.concatenate(
            [i["hy_fw2_2"][0], i["hy_fw3_2"][0]] +
            [i[n][0][:, None] for n in ("hy_fb1_2", "hy_fb2_2", "hy_fb3_2", "hy_freq_2")], axis=1)),
        "hy_fw_out": np.ascontiguousarray(i["hy_fw_out_2"][0].reshape(HY_W, 2, 2, D)),
    }
    arrays.update(shape_constants())
    return arrays


def kernel(**inputs):
    import concourse.bacc as bacc
    from concourse.bass_utils import run_bass_kernel_spmd

    arrays = lay_out({k: np.asarray(v) for k, v in inputs.items()})
    nc = bacc.Bacc("TRN2", target_bir_lowering=False, num_devices=1)
    aps = {n: nc.dram_tensor(f"in_{n}", v.shape, mybir.dt.from_np(v.dtype), kind="ExternalInput").ap()
           for n, v in arrays.items()}
    aps["spectra"] = nc.dram_tensor("spectra", (2, 2, 2, P, 4, T), F32, kind="Internal").ap()
    aps["x_spill"] = nc.dram_tensor("x_spill", (KD, P, T), F32, kind="Internal").ap()
    out = nc.dram_tensor("out_x", (D, T), F32, kind="ExternalOutput").ap()
    build_program(nc, aps, out)
    result = run_bass_kernel_spmd(nc, [{f"in_{n}": v for n, v in arrays.items()}], core_ids=[0])
    return np.ascontiguousarray(result.results[0]["out_x"].T)[None]
```

```python
import math
from contextlib import ExitStack, contextmanager

import numpy as np

import concourse.bass as bass
from concourse import mybir

F32 = mybir.dt.float32
F32R = mybir.dt.float32r
I32 = mybir.dt.int32
ACT = mybir.ActivationFunctionType
ALU = mybir.AluOpType
AX_X = mybir.AxisListType.X

P = 128
T = 512
D = 1024
KD = D // P
FF = 2816
KF = FF // P
CHUNK = 1024
HEADS, NOPE, ROPE, VD = 8, 128, 64, 128
RQ, RKV = 384, 256
KQ, KKV = RQ // P, RKV // P
POOL_WINDOWS = (2, 4, 8, 16)
PAD = 8
HALF = T // 2
ALPHA_1 = 2.0 ** 0.25
ALPHA_2 = 4.0 ** 0.25
EPS_1, EPS_2, EPS_RMS = 1e-6, 1e-5, 1e-6
HY_EMB, HY_W = 33, 64
SM_SCALE = (NOPE + ROPE) ** -0.5

INV_2PI = float(np.float32(1.0 / (2 * math.pi)))
PI2_A = 6.28125
PI2_B = float(np.float32(2 * math.pi - PI2_A))
PI2_C = float(np.float32(2 * math.pi - PI2_A - PI2_B))
ROUND = float(1.5 * 2 ** 23)
PI_LOW = 3.1415925

PARAMS = {}
_at = 0
for _name, _n in (("c", KD), ("mod_b", 48), ("ln_g0", KD), ("ln_b0", KD), ("ln_g1", KD), ("ln_b1", KD),
                  ("pool_scale", KD), ("g_q", KQ), ("g_kv", KKV), ("hy_short", 3 * 24), ("hy_d", 2 * KD),
                  ("conv0", 3 * 2 * KF), ("conv1", 3 * 2 * KF),
                  ("a_g0", KD), ("a_b0", KD), ("f_g0", KD), ("f_b0", KD),
                  ("a_g1", KD), ("a_b1", KD), ("f_g1", KD), ("f_b1", KD)):
    PARAMS[_name] = (_at, _n)
    _at += _n
N_PARAMS = _at

N_GROUPS = 2
STREAM = (("pool", 2), ("up_1", 2 * KF), ("down_1", KF), ("mla_in", 6), ("mla_heads", 6 * N_GROUPS),
          ("mla_out", KD), ("up_2", 2 * KF), ("down_2", KF), ("hy_in", 24), ("hy_out", KD),
          ("up_3", 2 * KF), ("down_3", KF))
FIRST_CHUNK = {}
_at = 0
for _name, _n in STREAM:
    FIRST_CHUNK[_name] = _at
    _at += _n
N_CHUNKS = _at


class Val:

    def __init__(self, const, step=0):
        self.const, self.step = const, step

    def __add__(self, n):
        return Val(self.const + n, self.step)

    def __mul__(self, n):
        return Val(self.const * n, self.step * n)

    def half(self):
        assert self.step % 2 == 0
        return Val(self.const // 2, self.step // 2)

    def of(self, loop_index):
        return self.const if not self.step else loop_index * self.step + self.const


class Token:

    def __init__(self, count, val):
        self.count, self.val = count, val

    def before(self):
        assert self.val.step
        return Token(self.count, self.val + -self.val.step)


class Count:

    def __init__(self, handle):
        self.handle, self.val = handle, Val(0)

    def did(self, instruction, by=1):
        instruction.then_inc(self.handle, by)
        self.val = self.val + by
        return Token(self, self.val)


class Program:
    def __init__(self, nc, ctx):
        self.nc, self.ctx, self.index = nc, ctx, None
        self.pe, self.act, self.dve, self.pool = (self.count(n) for n in ("pe", "act", "dve", "pool"))
        self.raw = [self.count("raw_even"), self.count("raw_odd")]
        self.hi_done, self.lo_done = self.count("hi_done"), self.count("lo_done")
        self.used = self.count("chunk_used")
        self.everything = [self.pe, self.act, self.dve, self.pool, *self.raw, self.hi_done, self.lo_done, self.used]

    def count(self, name):
        return Count(self.ctx.enter_context(self.nc.semaphore("s_" + name)))

    def sb(self, ctx, name, shape, dt=F32):
        return ctx.enter_context(self.nc.sbuf_tensor(name, shape, dt))

    def wait(self, engine, *tokens):
        for t in tokens:
            if t is not None:
                engine.wait_ge(t.count.handle, t.val.of(self.index))

    @contextmanager
    def loop(self, n, per, extra=()):
        start = {c: c.val.const for c in self.everything + list(extra)}
        with self.nc.Fori(0, n) as i:
            self.index = i
            for c in start:
                c.val = Val(start[c], per.get(c, 0))
            yield i
        for c, v in start.items():
            assert c.val.const - v == per.get(c, 0), (c.handle, c.val.const - v, per.get(c, 0))
            c.val = Val(v + n * per.get(c, 0))
        self.index = None


def build_program(nc, a, out):
    ctx = ExitStack()
    with ctx:
        p = Program(nc, ctx)
        PE, SC, VE, GP, SP = nc.tensor, nc.scalar, nc.vector, nc.gpsimd, nc.sync
        pe, act, dve, pool, used = p.pe, p.act, p.dve, p.pool, p.used
        wait = p.wait

        X = p.sb(ctx, "x_residual", [P, KD, T])
        AH = p.sb(ctx, "act_hi", [P, KD, T], F32R)
        AL = p.sb(ctx, "act_lo", [P, KD, T], F32R)
        WR = p.sb(ctx, "w_raw", [P, 2, CHUNK])
        WH = p.sb(ctx, "w_hi", [P, 2, CHUNK], F32R)
        WL = p.sb(ctx, "w_lo", [P, 2, CHUNK], F32R)
        PV = p.sb(ctx, "params", [P, N_PARAMS])
        MOD = p.sb(ctx, "mod_x", [P, 48])
        icnt = p.sb(ctx, "pool_1_over_count", [P, 4, 2 * PAD])
        AFF = p.sb(ctx, "affine", [P, 7, 2, KD])
        ident = p.sb(ctx, "identity", [P, P])
        mean_w = p.sb(ctx, "mean_weights", [P, P])
        ones = p.sb(ctx, "ones", [P, P])
        stat = p.sb(ctx, "stat", [P, 4, 4])
        minus_half = p.sb(ctx, "minus_half", [P, 4])
        ps = ctx.enter_context(nc.psum_tensor("ps", [P, 8, 512], F32))

        def par(name, k=0):
            at, n = PARAMS[name]
            assert k < n
            return PV[:, at + k:at + k + 1]

        def par_all(name):
            at, n = PARAMS[name]
            return PV[:, at:at + n]

        def f32(ap):
            return ap.bitcast(F32)

        def tile(buf, k):
            if not isinstance(k, Val) or not k.step:
                return buf[:, k.const if isinstance(k, Val) else k, :]
            return buf[:, bass.ds(k.of(p.index), 1), :].rearrange("p a b -> p (a b)")

        def mm3(o, lh, ll, rh, rl, start, stop, **kw):
            PE.matmul(o, lh, rh, start=start, stop=False, **kw)
            PE.matmul(o, lh, rl, start=False, stop=False, **kw)
            return PE.matmul(o, ll, rh, start=False, stop=stop, **kw)

        stream = a["w_stream"]

        def fetch(c):
            if c.step == 0 and c.const >= N_CHUNKS:
                return
            slot = c.const % 2
            if c.const >= 2:
                wait(SP, Token(p.lo_done, c + -1))
            src = stream[c.const] if not c.step else stream[bass.ds(c.of(p.index), 1)].rearrange("a p n -> (a p) n")
            p.raw[slot].did(SP.dma_start(WR[:, slot, :], src), 16)

        def split(c):
            if c.step == 0 and c.const >= N_CHUNKS:
                return
            slot = c.const % 2
            landed = Token(p.raw[slot], c.half() * 16 + 16)
            if c.const >= 2:
                wait(SC, Token(used, c + -1))
            wait(SC, landed)
            p.hi_done.did(SC.activation(WH[:, slot, :], WR[:, slot, :], ACT.Copy))
            wait(GP, Token(p.hi_done, c + 1))
            p.lo_done.did(GP.tensor_tensor(WL[:, slot, :], WR[:, slot, :], f32(WH[:, slot, :]), ALU.subtract))

        def take(c):
            split(c + 1)
            fetch(c + 2)
            wait(PE, Token(p.lo_done, c + 1))
            slot = c.const % 2
            return (WH[:, slot, :].rearrange("p (b m) -> p b m", m=P),
                    WL[:, slot, :].rearrange("p (b m) -> p b m", m=P))

        def per(chunks, **own):
            rises = {used: chunks, p.hi_done: chunks, p.lo_done: chunks, p.raw[0]: 8 * chunks, p.raw[1]: 8 * chunks}
            rises.update({{"pe": pe, "act": act, "dve": dve, "pool": pool}[k]: v for k, v in own.items()})
            return rises

        s_par, s_x, s_hy, s_con = p.count("params"), p.count("x"), p.count("hyena_small"), p.count("constants")
        got_par = s_par.did(SP.dma_start(PV[:, :], a["params"]), 16)
        VE.memset(ones[:, :], 1.0)
        VE.memset(minus_half[:, :], -0.5)
        made_ones = dve.did(VE.memset(mean_w[:, :], 1.0 / D))

        s1 = ExitStack()
        with s1:
            MC = 3
            MW = p.sb(s1, "mod_ring", [P, 4, KD, MC * P])
            macc = p.sb(s1, "mod_sums", [P, 2, MC * P])
            sc = p.sb(s1, "silu_c", [P, KD])
            zt = p.sb(s1, "positions_features", [HY_EMB, T])
            fw1 = p.sb(s1, "fw1", [HY_EMB, HY_W])
            fws = p.sb(s1, "fw23_bias_freq", [HY_W, 2 * HY_W + 4])
            fwo = X[0:HY_W, :, :].rearrange("p (o d h) t -> p o d (h t)", o=2, d=2)
            fsd = p.sb(s1, "fw_out_sum_diff", [P, 2, 2, D])
            hid = p.sb(s1, "filter_hidden", [P, T])
            red = p.sb(s1, "sin_turns", [HY_W, T])
            decay = p.sb(s1, "decay", [P, 4, D])
            tabr = WR[:, :, :].rearrange("p s (b m) -> p (s b) m", m=P)
            tabh, tabl = (t[:, 4:8, :].rearrange("p k (b m) -> p (k b) m", m=P) for t in (AH, AL))
            flt = p.sb(s1, "filter_taps", [P, 4, T])
            flh, fll = AH[:, 0:4, :], AL[:, 0:4, :]
            odd = p.sb(s1, "odd_spectrum", [P, 2, T])
            kspec = p.sb(s1, "filter_spectra", [P, 2, 4, T])

            for dst, name in ((zt, "hy_z"), (fw1, "hy_fw1"), (fws, "hy_small")):
                got_small = s_hy.did(SP.dma_start(dst[:, :], a[name]), 16)
            got_fwo = s_con.did(SP.dma_start(fwo, a["hy_fw_out"]), 16)
            got_tab = s_con.did(SP.dma_start(tabr, a["dft_fwd"]), 16)
            got_decay = s_con.did(SP.dma_start(decay[:, :, :], a["decay"]), 16)
            s_spec = p.count("filter_io")
            got_decay = s_con.did(SP.dma_start(icnt[:, :, :], a["inv_count"]), 16)
            got_ident = s_spec.did(SP.dma_start(ident[:, :], a["identity"]), 16)

            s_mod = [p.count(f"mod{i}") for i in range(4)]
            mod_used, mod_summed = p.count("mod_used"), p.count("mod_summed")
            for h in range(4):
                mod_used.did(VE.memset(hid[:, h * P:(h + 1) * P], 0.0))
                if h < 2:
                    mod_summed.did(PE.nop())
            cleared = dve.did(VE.memset(fsd[:, :, :, :], 0.0))
            wait(VE, cleared, Token(mod_used, Val(4)))
            wait(SC, Token(mod_used, Val(4)))

            wait(SC, got_par)
            got_sc = act.did(SC.activation(sc[:, :], par_all("c"), ACT.Silu))

            def reduce_sin(out_ap, arg, turns, np_):
                t = dve.did(VE.tensor_scalar(turns, arg, INV_2PI, ROUND, ALU.mult, ALU.add))
                wait(VE, t)
                t = dve.did(VE.tensor_scalar(turns, turns, ROUND, None, ALU.subtract))
                for part in (PI2_A, PI2_B, PI2_C):
                    wait(VE, t)
                    t = dve.did(VE.scalar_tensor_tensor(out=arg, in0=turns, scalar=-part, in1=arg,
                                                        op0=ALU.mult, op1=ALU.add))
                wait(VE, t)
                t = dve.did(VE.tensor_scalar(arg, arg, PI_LOW, -PI_LOW, ALU.min, ALU.max))
                if out_ap is None:
                    return t
                wait(SC, t)
                return act.did(SC.activation(out_ap, arg, ACT.Sin))

            wait(PE, got_small)
            mlp = pe.did(PE.matmul(ps[0:HY_W, 0, :], fw1[:, :], zt[:, :], start=True, stop=True))
            for layer in range(3):
                wait(VE, mlp, got_small)
                at = 2 * HY_W
                arg = flt[0:HY_W, 0, :]
                t = dve.did(VE.tensor_scalar(arg, ps[0:HY_W, 0, :], fws[:, at + layer:at + layer + 1],
                                             fws[:, at + 3:at + 4], ALU.add, ALU.mult))
                wait(VE, t)
                h_done = reduce_sin(hid[0:HY_W, :], arg, red[:, :], HY_W)
                if layer < 2:
                    wait(PE, h_done)
                    mlp = pe.did(PE.matmul(ps[0:HY_W, 0, :], fws[:, layer * HY_W:(layer + 1) * HY_W],
                                           hid[0:HY_W, :],
                                           start=True, stop=True))
            wait(VE, got_decay)
            dve.did(VE.tensor_tensor(fsd[0:HY_W, 0, :, :], fwo[:, :, 0], fwo[:, :, 1], ALU.add))
            fsd_done = dve.did(VE.tensor_tensor(fsd[0:HY_W, 1, :, :], fwo[:, :, 0], fwo[:, :, 1], ALU.subtract))
            th = dve.did(VE.tensor_copy(tabh[:, :, :], tabr))
            wait(GP, th)
            tab_done = pool.did(GP.tensor_tensor(tabl[:, :, :], tabr, f32(tabh[:, :, :]), ALU.subtract))

            def modulate(first, ring):
                for slot in range(2):
                    transfer = first + slot
                    wait(SP, Token(mod_used, transfer + 1))
                    s_mod[ring + slot].did(SP.dma_start(MW[:, ring + slot, :, :], a["mod_w"][bass.ds(transfer.of(p.index), 1)]
                                                 .rearrange("a p k n -> (a p) k n")), 16)
                t = [None, None]
                for k in range(KD):
                    for slot in range(2):
                        src, dst = MW[:, ring + slot, k, :], macc[:, slot, :]
                        if k == 0:
                            wait(VE, Token(s_mod[ring + slot], s_mod[ring + slot].val),
                                 Token(mod_summed, first + (slot + 1)))
                            ins = VE.tensor_scalar(dst, src, sc[:, 0:1], None, ALU.mult)
                        else:
                            wait(VE, t[slot])
                            ins = VE.scalar_tensor_tensor(out=dst, in0=src, scalar=sc[:, k:k + 1], in1=dst,
                                                          op0=ALU.mult, op1=ALU.add)
                        if k < KD - 1:
                            t[slot] = dve.did(ins)
                        else:
                            mod_used.did(ins)

            def mod_sum(transfer, slot):
                wait(PE, Token(mod_used, transfer + 5))
                for i in range(MC):
                    col = ps[:, 7, bass.ds((transfer * MC + i).of(p.index), 1)]
                    ins = PE.matmul(col, macc[:, slot, i * P:(i + 1) * P], ones[:, 0:1], start=True, stop=True)
                mod_summed.did(ins)

            wait(PE, got_sc, h_done, fsd_done)
            wait(VE, got_decay)
            rises = {pe: 4 * (1 + 4), dve: 4 * (4 + 2 + 4 + 2 * 7), pool: 8, mod_summed: 8, act: 4 * (4 + 2), s_spec: 64, mod_used: 8,
                     **{m: 32 for m in s_mod}}
            wait(SP, fsd_done)
            for k in range(KD):
                got_x = s_x.did(SP.dma_start(X[:, k, :], a["xT"][k * P:(k + 1) * P, :]), 16)
            with p.loop(2, rises, extra=[s_spec, mod_used, mod_summed, *s_mod]) as order:
                stored = Token(s_spec, s_spec.val)
                butterfly = Token(dve, dve.val)
                got_before = Token(pe, pe.val)
                for n in range(2):
                    for kind in range(2):
                        unit = 2 * n + kind
                        for q in range(4):
                            if q == 3:
                                wait(PE, butterfly)
                            fw = fsd[:, kind, bass.ds(order, 1), n * 512:(n + 1) * 512].rearrange("p a b -> p (a b)")
                            ins = PE.matmul(ps[:, q, :], hid[:, q * P:(q + 1) * P], fw, start=True, stop=True)
                        taps = pe.did(ins)
                        wait(VE, taps)
                        wait(GP, got_before)
                        tok = []
                        for q in range(4):
                            tok.append(dve.did(VE.tensor_tensor(flt[:, q, :], ps[:, q, :],
                                                                decay[:, q, n * 512:(n + 1) * 512], ALU.mult)))
                        his = []
                        for q in range(4):
                            wait(SC, tok[q])
                            his.append(act.did(SC.activation(flh[:, q, :], flt[:, q, :], ACT.Copy)))
                        los = []
                        for q in range(4):
                            engine, count = (GP, pool) if q % 2 == 0 else (VE, dve)
                            wait(engine, his[q])
                            los.append(count.did(engine.tensor_tensor(fll[:, q, :], flt[:, q, :],
                                                                      f32(flh[:, q, :]), ALU.subtract)))
                        modulate(Val(2 * unit, 8), 2 * (unit % 2))
                        wait(PE, los[2], los[3], tab_done)
                        copied = []
                        for f, banks in enumerate(((4, 5), (6, 3))):
                            for parity in range(2):
                                for k in range(2):
                                    b = ((kind * 2 + parity) * 2 + k) * 2 + f
                                    ins = mm3(ps[:, banks[parity], :], tabh[:, b, :], tabl[:, b, :],
                                              flh[:, 2 * parity + k, :], fll[:, 2 * parity + k, :], k == 0, k == 1)
                                got = got_before = pe.did(ins)
                            wait(SC, got)
                            copied.append(act.did(SC.activation(odd[:, f, :], ps[:, banks[1], :], ACT.Copy)))
                        for slot in range(2):
                            mod_sum(Val(2 * unit + slot, 8), slot)
                        for f, banks in enumerate(((4, 5), (6, 3))):
                            wait(VE, copied[f])
                            if kind == 0 and f == 0:
                                wait(VE, stored)
                            dve.did(VE.tensor_tensor(kspec[:, f, 2 * kind, :], ps[:, banks[0], :], odd[:, f, :],
                                                     ALU.add))
                            butterfly = dve.did(VE.tensor_tensor(kspec[:, f, 2 * kind + 1, :], ps[:, banks[0], :],
                                                                 odd[:, f, :], ALU.subtract))
                    wait(SC, butterfly)
                    for f in range(2):
                        dst = a["spectra"][bass.ds(order, 1), n, f].rearrange("a p c t -> (a p) c t")
                        stored = s_spec.did(SC.dma_start(dst, kspec[:, f, :, :]), 16)
            spectra_stored = s_spec.val

            wait(VE, Token(mod_summed, mod_summed.val))
            mod_done = dve.did(VE.tensor_tensor(MOD[:, :], ps[:, 7, 0:48], par_all("mod_b"), ALU.add))
            wait(VE, mod_done)
            SH1, SC1, G1, SH2, SC2, G2 = (MOD[:, 8 * i:8 * i + 8] for i in range(6))
            dve.did(VE.tensor_scalar(AFF[:, 0, 0, :], SC1, 1.0, None, ALU.add))
            t = dve.did(VE.tensor_scalar(AFF[:, 1, 1, :], SC2, 1.0, None, ALU.add))
            wait(VE, t)
            dve.did(VE.tensor_tensor(AFF[:, 1, 0, :], par_all("ln_g0"), AFF[:, 1, 1, :], ALU.mult))
            t = dve.did(VE.tensor_tensor(AFF[:, 1, 1, :], par_all("ln_b0"), AFF[:, 1, 1, :], ALU.mult))
            wait(VE, t)
            dve.did(VE.tensor_tensor(AFF[:, 1, 1, :], AFF[:, 1, 1, :], SH2, ALU.add))
            dve.did(VE.tensor_tensor(AFF[:, 0, 1, :], G1, par_all("pool_scale"), ALU.mult))
            for row, (g, b), alpha in ((2, ("ln_g0", "ln_b0"), ALPHA_1), (3, ("ln_g1", "ln_b1"), ALPHA_2),
                                       (4, ("a_g0", "a_b0"), ALPHA_2), (5, ("f_g0", "f_b0"), ALPHA_2),
                                       (6, ("a_g1", "a_b1"), ALPHA_2)):
                dve.did(VE.tensor_scalar(AFF[:, row, 0, :], par_all(g), alpha, None, ALU.mult))
                aff_done = dve.did(VE.tensor_scalar(AFF[:, row, 1, :], par_all(b), alpha, None, ALU.mult))
            stage1_dve = aff_done

        def layer_norm(tag, arrived, mean_by_sum, eps, to_a, keep, last=False):
            st = ExitStack()
            with st:
                sq = p.sb(st, f"{tag}_squares", [P, 2, T])
                val = p.sb(st, f"{tag}_values", [P, 2, T])
                settle(SC, VE)
                if mean_by_sum is not None:
                    wait(PE, arrived[-1], made_ones)
                    ins = PE.matmul(ps[:, 0, :], mean_w[:, :], mean_by_sum, start=True, stop=True)
                else:
                    for k in range(KD):
                        wait(PE, arrived[k])
                        ins = PE.matmul(ps[:, 0, :], mean_w[:, :], X[:, k, :], start=(k == 0), stop=(k == KD - 1))
                mean = pe.did(ins)
                wait(VE, mean)
                summed = [None] * KD
                for k in range(KD):
                    centred = dve.did(VE.tensor_tensor(X[:, k, :], X[:, k, :], ps[:, 0, :], ALU.subtract))
                    wait(SC, centred, summed[k - 2] if k >= 2 else None)
                    squared = act.did(SC.activation(sq[:, k % 2, :], X[:, k, :], ACT.Square))
                    wait(PE, squared)
                    for q in range(4):
                        ins = PE.matmul(ps[:, 1, q:q + 1], sq[:, k % 2, q * P:(q + 1) * P], ones[:, 0:1],
                                        start=(k == 0 and q == 0), stop=(k == KD - 1), skip_group_check=True)
                    summed[k] = pe.did(ins)
                wait(VE, summed[-1])
                t = dve.did(VE.tensor_scalar(stat[:, 0, :], ps[:, 1, 0:4], 1.0 / D, eps, ALU.mult, ALU.add))
                wait(GP, t)
                t = pool.did(GP.tensor_tensor(stat[:, 1, :], stat[:, 0, :], minus_half[:, :], ALU.pow))
                wait(PE, t)
                for q in range(4):
                    ins = PE.matmul(ps[:, 2, q * P:(q + 1) * P], stat[:, 1, q:q + 1].broadcast_to([P, P]),
                                    ident[:, :], start=True, stop=True, skip_group_check=True)
                rstd = pe.did(ins)
                wait(VE, rstd)
                ready, lows = [], []
                gain, bias = to_a if to_a is not None else (None, None)
                keep_g, keep_b = keep
                for k in range(KD):
                    normed = dve.did(VE.tensor_tensor(X[:, k, :], X[:, k, :], ps[:, 2, :], ALU.mult))
                    if last:
                        wait(SC, normed)
                        ready.append(act.did(SC.activation(X[:, k, :], X[:, k, :], ACT.Identity,
                                                           scale=keep_g[:, k:k + 1], bias=keep_b[:, k:k + 1])))
                        continue
                    wait(SC, normed)
                    hi = act.did(SC.activation(AH[:, k, :], X[:, k, :], ACT.Identity,
                                               scale=gain[:, k:k + 1], bias=bias[:, k:k + 1]))
                    wait(VE, normed, lows[k - 2] if k >= 2 else None)
                    value = dve.did(VE.tensor_scalar(val[:, k % 2, :], X[:, k, :], gain[:, k:k + 1],
                                                     bias[:, k:k + 1], ALU.mult, ALU.add))
                    if k % 2:
                        wait(VE, hi, value)
                        lows.append(dve.did(VE.tensor_tensor(AL[:, k, :], val[:, 1, :], f32(AH[:, k, :]),
                                                             ALU.subtract)))
                    else:
                        wait(GP, hi, value)
                        lows.append(pool.did(GP.tensor_tensor(AL[:, k, :], val[:, 0, :], f32(AH[:, k, :]),
                                                              ALU.subtract)))
                    ready.append(lows[-1])
                    wait(SC, value)
                    kept = act.did(SC.activation(X[:, k, :], X[:, k, :], ACT.Identity,
                                                 scale=keep_g[:, k:k + 1], bias=keep_b[:, k:k + 1]))
                if not last:
                    wait(VE, kept, lows[-2])
                    wait(SC, lows[-1], lows[-2])
                    wait(GP, lows[-1])
                return ready

        def settle(*engines):
            for engine in engines:
                wait(engine, *(Token(c, c.val) for c in (pe, act, dve, pool)))

        def conv3(dst, bank, taps, used_tok, free_tok):
            wait(SC, used_tok, free_tok)
            t = act.did(SC.activation(dst, ps[:, bank, :], ACT.Copy, scale=taps[1]))
            wait(VE, t)
            t = dve.did(VE.scalar_tensor_tensor(out=dst[:, 1:T], in0=ps[:, bank, 0:T - 1], scalar=taps[0],
                                                in1=dst[:, 1:T], op0=ALU.mult, op1=ALU.add))
            wait(VE, t)
            return dve.did(VE.scalar_tensor_tensor(out=dst[:, 0:T - 1], in0=ps[:, bank, 1:T], scalar=taps[2],
                                                   in1=dst[:, 0:T - 1], op0=ALU.mult, op1=ALU.add))

        def split_act(dst_hi, dst_lo, src, ready, hi_by=None):
            wait(VE, ready)
            hi = dve.did(VE.tensor_copy(dst_hi, src))
            wait(VE, hi)
            return dve.did(VE.tensor_tensor(dst_lo, src, f32(dst_hi), ALU.subtract))

        def column(name, k):
            at, n = PARAMS[name]
            if isinstance(k, Val) and k.step:
                return PV[:, bass.ds((k + at).of(p.index), 1)]
            k = k.const if isinstance(k, Val) else k
            return PV[:, at + k:at + k + 1]

        def ffn(tag, up, down, conv, a_ready, gate_col):
            st = ExitStack()
            with st:
                HH = p.sb(st, f"{tag}_hidden_hi", [P, KF, T], F32R)
                HL = p.sb(st, f"{tag}_hidden_lo", [P, KF, T], F32R)
                CA = p.sb(st, f"{tag}_value", [P, 2, T])
                CG = p.sb(st, f"{tag}_gate", [P, 2, T])
                HF = p.sb(st, f"{tag}_hidden", [P, 2, T])
                base_c = FIRST_CHUNK[up]
                settle(VE, SC)

                def multiply(c, bank, free, tiles):
                    wh, wl = take(c)
                    wait(PE, *free)
                    for k in range(KD):
                        if tiles is not None:
                            wait(PE, tiles[k])
                        ins = mm3(ps[:, bank, :], wh[:, k, :], wl[:, k, :], AH[:, k, :], AL[:, k, :],
                                  k == 0, k == KD - 1)
                    return used.did(ins)

                def finish_first(j, u, done, free):
                    if conv is None:
                        wait(SC, done, free)
                        return act.did(SC.activation(CG[:, u, :], ps[:, 2 * u, :], ACT.Silu))
                    return conv3(CA[:, u, :], 2 * u, [column(conv, j * 3 + s) for s in range(3)], done, free)

                def finish_second(j, u, first, done):
                    if conv is None:
                        wait(VE, first, done)
                        h = dve.did(VE.tensor_tensor(HF[:, u, :], CG[:, u, :], ps[:, 2 * u + 1, :], ALU.mult))
                        freed = h
                    else:
                        freed = conv3(CG[:, u, :], 2 * u + 1, [column(conv, j * 3 + (3 * KF + s)) for s in range(3)],
                                      done, None)
                        wait(SC, freed)
                        g = act.did(SC.activation(CG[:, u, :], CG[:, u, :], ACT.Silu))
                        wait(VE, g)
                        h = dve.did(VE.tensor_tensor(HF[:, u, :], CG[:, u, :], CA[:, u, :], ALU.mult))
                    split_act(tile(HH, j), tile(HL, j), HF[:, u, :], h)
                    return freed, h

                def step(c, j, u, free_first, free_second, tiles, pend):
                    d0 = multiply(c, 2 * u, free_first, tiles)
                    fin = finish_second(*pend) if pend is not None else None
                    d1 = multiply(c + 1, 2 * u + 1, free_second, None)
                    f = finish_first(j, u, d0, free_first[-1] if free_first else None)
                    return (j, u, f, d1), fin

                pend0, _ = step(Val(base_c), Val(0), 0, [], [], a_ready, None)
                pend1, fin0 = step(Val(base_c + 2), Val(1), 1, [], [], None, pend0)
                n_dve = 2 * (3 if conv is None else 7)
                n_act = 2 * (1 if conv is None else 3)

                def moved(tok, step_):
                    return Token(tok.count, Val(tok.val.const, step_[tok.count]))

                rise = {dve: n_dve, act: n_act, used: 4}
                with p.loop(KF // 2 - 1, per(4, dve=n_dve, act=n_act)):
                    j0, j1 = Val(2, 2), Val(3, 2)
                    c = Val(base_c + 4, 4)
                    free0 = [moved(pend0[2], rise), moved(fin0[1], rise)]
                    free0s = [moved(fin0[0], rise)]
                    before = (Val(1, 2), 1, moved(pend1[2], rise), moved(pend1[3], rise))
                    a0, fin1 = step(c, j0, 0, free0, free0s, None, before)
                    free1 = [moved(pend1[2], rise), fin1[1]]
                    a1, fin0 = step(c + 2, j1, 1, free1, [fin1[0]], None, a0)
                n = KF // 2 - 2

                def ended(tok):
                    return Token(tok.count, Val(tok.val.const + n * tok.val.step))

                finish_second(Val(KF - 1), 1, ended(a1[2]), ended(a1[3]))
                hidden_done = Token(dve, dve.val)

                base_d = FIRST_CHUNK[down]

                def down_chunk(c, k, first, last_):
                    wh, wl = take(c)
                    for m in range(KD):
                        ins = mm3(ps[:, m, :], wh[:, m, :], wl[:, m, :], tile(HH, k), tile(HL, k), first, last_)
                        if last_:
                            banks.append(pe.did(ins))
                    return ins

                banks = []
                wait(PE, hidden_done)
                used.did(down_chunk(Val(base_d), 0, True, False))
                used.did(down_chunk(Val(base_d + 1), 1, False, False))
                with p.loop(KF // 2 - 2, per(2)):
                    for s in range(2):
                        used.did(down_chunk(Val(base_d + 2 + s, 2), Val(2 + s, 2), False, False))
                used.did(down_chunk(Val(base_d + KF - 2), KF - 2, False, False))
                last_ins = down_chunk(Val(base_d + KF - 1), KF - 1, False, True)
                wait(PE, banks[-1])
                used.did(PE.nop())
                arrived = []
                for m in range(KD):
                    wait(VE, banks[m])
                    factor = gate_col[:, m:m + 1] if gate_col is not None else 1.0
                    arrived.append(dve.did(VE.scalar_tensor_tensor(out=X[:, m, :], in0=ps[:, m, :], scalar=factor,
                                                                   in1=X[:, m, :], op0=ALU.mult, op1=ALU.add)))
                return arrived

        def out_linear(tag, layer, rh, rl, tiles, st):
            acc = p.sb(st, f"{tag}_sum", [P, T])
            base = FIRST_CHUNK[layer]

            def one(c, m, s, first):
                wh, wl = take(c)
                out_bank = tile(ps, m)
                for k in range(KD):
                    if first:
                        wait(PE, tiles[k])
                    ins = mm3(out_bank, wh[:, k, :], wl[:, k, :], rh[:, k, :], rl[:, k, :], k == 0, k == KD - 1)
                done = used.did(ins)
                wait(VE, done)
                t = dve.did(VE.tensor_tensor(tile(X, m), tile(X, m), out_bank, ALU.add))
                wait(VE, t)
                if first:
                    return dve.did(VE.tensor_copy(acc[:, :], tile(X, m)))
                return dve.did(VE.tensor_tensor(acc[:, :], acc[:, :], tile(X, m), ALU.add))

            one(Val(base), Val(0), 0, True)
            one(Val(base + 1), Val(1), 1, False)
            with p.loop(KD // 2 - 1, per(2, dve=4)):
                for s in range(2):
                    t = one(Val(base + 2 + s, 2), Val(2 + s, 2), s, False)
            return [Token(dve, dve.val)], acc[:, :]

        wait(SP, tab_done)
        fetch(Val(0))
        fetch(Val(1))
        split(Val(0))

        s2 = ExitStack()
        with s2:
            hx = p.sb(s2, "pool_in", [P, KD, T + 2 * PAD])
            sums_n = p.sb(s2, "pool_sums_narrow", [P, 4, T + 2 * PAD])
            scratch_n = p.sb(s2, "pool_scratch_narrow", [P, 1, T + 2 * PAD])
            scratch_w = p.sb(s2, "pool_scratch_wide", [P, 2, T + 2 * PAD])
            edge = p.sb(s2, "pool_edges", [P, 4, PAD])
            df = p.sb(s2, "pool_diff", [P, KD, T])
            for engine in (VE, SC, GP):
                wait(engine, Token(mod_summed, mod_summed.val))
            settle(VE, SC, GP)
            dve.did(VE.memset(hx[:, :, 0:PAD], 0.0))
            clear = dve.did(VE.memset(hx[:, :, PAD + T:], 0.0))
            wait(VE, got_x, got_decay, stage1_dve, clear)
            wait(GP, got_x, got_decay, stage1_dve, clear)
            wait(SC, stage1_dve, got_x)
            lows, scaled = {}, {}
            L = T + 2 * PAD

            def window_sum(engine, count, bufs, k, w, t):
                steps = w.bit_length() - 1
                src, lo, hi, width, at = hx[:, k, :], 1, 0, 2, steps % 2
                low_edge, high_edge = 1, L
                while True:
                    dst = bufs[at % 2]
                    wait(engine, t)
                    t = count.did(engine.tensor_tensor(dst[:, low_edge:high_edge],
                                                       src[:, low_edge - lo:high_edge - lo],
                                                       src[:, low_edge + hi:high_edge + hi], ALU.add))
                    if width == w:
                        return dst, t
                    src, lo, hi = dst, width // 2, width // 2
                    low_edge, high_edge = low_edge + lo, high_edge - hi
                    width, at = 2 * width, at + 1

            inputs = {}
            for k in (0, 1, 4, 2, 3, 5, 6, 7):
                t = dve.did(VE.tensor_scalar(hx[:, k, PAD:PAD + T], X[:, k, :], AFF[:, 0, 0, k:k + 1],
                                             MOD[:, k:k + 1], ALU.mult, ALU.add))
                inputs[k] = t
                wait(SC, t)
                scaled[k] = act.did(SC.activation(X[:, k, :], X[:, k, :], ACT.Copy, scale=ALPHA_1))
            def finish_pool(k, total, t, sub_engine, sub_count):
                w = POOL_WINDOWS[k // 2]
                wait(VE, t)
                inside = dve.did(VE.scalar_tensor_tensor(out=df[:, k, :], in0=total[:, PAD:PAD + T], scalar=1.0 / w,
                                                         in1=hx[:, k, PAD:PAD + T], op0=ALU.mult,
                                                         op1=ALU.subtract))
                sides = ((slice(0, PAD), slice(PAD, 2 * PAD)), (slice(T - PAD, T), slice(T, T + PAD)))
                for side, (cols, at) in enumerate(sides):
                    u = dve.did(VE.tensor_tensor(edge[:, 2 * (k // 4) + side, :], total[:, at],
                                                 icnt[:, k // 2, side * PAD:(side + 1) * PAD], ALU.mult))
                for side, (cols, at) in enumerate(sides):
                    wait(VE, u, inside)
                    t = dve.did(VE.tensor_tensor(df[:, k, cols], edge[:, 2 * (k // 4) + side, :], hx[:, k, at],
                                                 ALU.subtract))
                wait(SC, t)
                hi = act.did(SC.activation(AH[:, k, :], df[:, k, :], ACT.Copy))
                wait(sub_engine, hi)
                lows[k] = sub_count.did(sub_engine.tensor_tensor(AL[:, k, :], df[:, k, :], f32(AH[:, k, :]),
                                                                 ALU.subtract))

            narrow = {}
            for k in range(4):
                wait(GP, narrow[k - 1][1] if k else None)
                narrow[k] = window_sum(GP, pool, (scratch_n[:, 0, :], sums_n[:, k, :]), k, POOL_WINDOWS[k // 2],
                                       inputs[k])
            for k in range(4):
                wait(VE, Token(dve, dve.val))
                total, t = window_sum(VE, dve, (scratch_w[:, 0, :], scratch_w[:, 1, :]), 4 + k,
                                      POOL_WINDOWS[2 + k // 2], inputs[4 + k])
                finish_pool(k, *narrow[k], GP, pool)
                finish_pool(4 + k, total, t, VE, dve)
            arrived = []
            for cc in range(2):
                wh, wl = take(Val(cc))
                for g2 in range(2):
                    g = 2 * cc + g2
                    wait(PE, lows[2 * g], lows[2 * g + 1])
                    for m in range(2):
                        for k in range(2):
                            b = (g2 * 2 + m) * 2 + k
                            ins = mm3(ps[:, 2 * g + m, :], wh[:, b, :], wl[:, b, :], AH[:, 2 * g + k, :],
                                      AL[:, 2 * g + k, :], k == 0, k == 1)
                done = used.did(ins)
                wait(VE, done)
                for m in range(4 * cc, 4 * cc + 4):
                    wait(VE, scaled[m])
                    arrived.append(dve.did(VE.scalar_tensor_tensor(out=X[:, m, :], in0=ps[:, m, :],
                                                                   scalar=AFF[:, 0, 1, m:m + 1], in1=X[:, m, :],
                                                                   op0=ALU.mult, op1=ALU.add)))
        ready = layer_norm("n0", arrived, None, EPS_1, (AFF[:, 1, 0, :], AFF[:, 1, 1, :]),
                           (AFF[:, 2, 0, :], AFF[:, 2, 1, :]))
        for engine in (VE, SC):
            wait(engine, Token(s_spec, s_spec.val))
        arrived = ffn("f0", "up_1", "down_1", None, ready, G2)
        ready = layer_norm("n1", arrived, None, EPS_1, (par_all("ln_g1"), par_all("ln_b1")),
                           (AFF[:, 3, 0, :], AFF[:, 3, 1, :]))

        s4 = ExitStack()
        with s4:
            OH = p.sb(s4, "heads_hi", [P, HEADS, T], F32R)
            OL = p.sb(s4, "heads_lo", [P, HEADS, T], F32R)
            cosv = p.sb(s4, "rope_cos", [P, T])
            sinv = p.sb(s4, "rope_sin", [P, T])
            swap = p.sb(s4, "rope_swap", [P, P])
            rc = p.sb(s4, "rope_consts", [P, 2])
            krh = p.sb(s4, "k_rope_hi", [P, T], F32R)
            krl = p.sb(s4, "k_rope_lo", [P, T], F32R)
            W0 = p.sb(s4, "rope_a", [P, T])
            W1 = p.sb(s4, "rope_b", [P, T])
            s_rope = p.count("rope")
            settle(SP, VE, SC)
            s_rope.did(SP.dma_start(swap[:, :], a["rope_swap"]), 16)
            s_rope.did(SP.dma_start(rc[:, :], a["rope_consts"]), 16)
            s4a = ExitStack()
            with s4a:
                LAT = p.sb(s4a, "latents", [P, 6, T])
                posi = p.sb(s4a, "positions", [P, T], I32)
                turns = p.sb(s4a, "rope_turns", [P, T])
                sq2 = p.sb(s4a, "rms_squares", [P, 2, T])
                got_rope = s_rope.did(SP.dma_start(posi[:, :], a["positions"].broadcast_to([P, T])), 16)
                wait(VE, got_rope)
                t = dve.did(VE.tensor_copy(W0[:, :], posi[:, :]))
                wait(VE, t)
                t = dve.did(VE.tensor_scalar(W0[:, :], W0[:, :], rc[:, 0:1], None, ALU.mult))
                wait(VE, t)
                t = reduce_sin(None, W0[:, :], turns[:, :], P)
                wait(SC, t)
                sine = act.did(SC.activation(sinv[:, :], W0[:, :], ACT.Sin))
                wait(VE, t)
                t = dve.did(VE.scalar_tensor_tensor(out=turns[:, :], in0=W0[:, :], scalar=-1.0, in1=W0[:, :],
                                                    op0=ALU.mult, op1=ALU.max))
                wait(VE, t)
                t = dve.did(VE.tensor_scalar(turns[:, :], turns[:, :], -1.0, math.pi / 2, ALU.mult, ALU.add))
                wait(SC, t)
                cosine = act.did(SC.activation(cosv[:, :], turns[:, :], ACT.Sin))
                wait(VE, sine)
                signed = dve.did(VE.tensor_scalar(sinv[:, :], sinv[:, :], rc[:, 1:2], None, ALU.mult))

                base = FIRST_CHUNK["mla_in"]
                lat = []
                for m in range(6):
                    wh, wl = take(Val(base + m))
                    for k in range(KD):
                        if m == 0:
                            wait(PE, ready[k])
                        ins = mm3(ps[:, m, :], wh[:, k, :], wl[:, k, :], AH[:, k, :], AL[:, k, :],
                                  k == 0, k == KD - 1)
                    done = used.did(ins)
                    wait(SC, done)
                    lat.append(act.did(SC.activation(LAT[:, m, :], ps[:, m, :], ACT.Copy)))
                sums, free = [], [None, None]
                for m in range(KQ + KKV):
                    group, first = (6, m == 0) if m < KQ else (7, m == KQ)
                    wait(SC, lat[m], free[m % 2])
                    t = act.did(SC.activation(sq2[:, m % 2, :], LAT[:, m, :], ACT.Square))
                    wait(PE, t)
                    for q in range(4):
                        ins = PE.matmul(ps[:, group, q:q + 1], sq2[:, m % 2, q * P:(q + 1) * P], ones[:, 0:1],
                                        start=(first and q == 0), stop=(m in (KQ - 1, KQ + KKV - 1)),
                                        skip_group_check=True)
                    free[m % 2] = pe.did(ins)
                a_lows = []
                for g, (bank, rank, first, n) in enumerate(((6, RQ, 0, KQ), (7, RKV, KQ, KKV))):
                    wait(VE, free[0], free[1])
                    t = dve.did(VE.tensor_scalar(stat[:, 2 * g, :], ps[:, bank, 0:4], 1.0 / rank, EPS_RMS,
                                                 ALU.mult, ALU.add))
                    wait(GP, t)
                    t = pool.did(GP.tensor_tensor(stat[:, 2 * g + 1, :], stat[:, 2 * g, :], minus_half[:, :],
                                                  ALU.pow))
                    wait(PE, t, lat[g])
                    for q in range(4):
                        ins = PE.matmul(ps[:, g, q * P:(q + 1) * P],
                                        stat[:, 2 * g + 1, q:q + 1].broadcast_to([P, P]),
                                        ident[:, :], start=True, stop=True, skip_group_check=True)
                    t = pe.did(ins)
                    wait(VE, t, lat[5])
                    for m in range(first, first + n):
                        gcol = par("g_q", m) if g == 0 else par("g_kv", m - KQ)
                        t = dve.did(VE.scalar_tensor_tensor(out=LAT[:, m, :], in0=LAT[:, m, :], scalar=gcol,
                                                            in1=ps[:, g, :], op0=ALU.mult, op1=ALU.mult))
                        a_lows.append(split_act(AH[:, m, :], AL[:, m, :], LAT[:, m, :], t))

                def rotate(bank_swap, src, tmp, dst_hi, dst_lo, ready_tok):
                    wait(PE, ready_tok, got_rope)
                    t1 = pe.did(PE.matmul(ps[:, bank_swap, :], swap[:, :], src, start=True, stop=True))
                    wait(VE, t1, signed)
                    t2 = dve.did(VE.tensor_tensor(tmp, sinv[:, :], ps[:, bank_swap, :], ALU.mult))
                    wait(VE, t1, cosine)
                    t3 = dve.did(VE.tensor_tensor(src, src, cosv[:, :], ALU.mult))
                    wait(VE, t2, t3)
                    t4 = dve.did(VE.tensor_tensor(src, src, tmp, ALU.add))
                    return split_act(dst_hi, dst_lo, src, t4)

                wait(PE, a_lows[-1])
                k_rope = rotate(2, LAT[:, 5, :], W1[:, :], krh[:, :], krl[:, :], lat[5])
                lat_done = k_rope

            QH = p.sb(s4, "q_hi", [P, 6, T], F32R)
            QL = p.sb(s4, "q_lo", [P, 6, T], F32R)
            KH = p.sb(s4, "k_hi", [P, 4, T], F32R)
            KL = p.sb(s4, "k_lo", [P, 4, T], F32R)
            VH = p.sb(s4, "v_hi", [P, 4, T], F32R)
            VL = p.sb(s4, "v_lo", [P, 4, T], F32R)
            PB = p.sb(s4, "probabilities", [P, 2, T])
            PTH = p.sb(s4, "probs_t_hi", [P, 4, T], F32R)
            PTL = p.sb(s4, "probs_t_lo", [P, 4, T], F32R)
            sm = p.sb(s4, "softmax_stats", [P, 4, 4])
            settle(VE, SC, PE)
            base = FIRST_CHUNK["mla_heads"]

            def head_group(g, base_c):
                banks_read = {}
                for ch in range(4):
                    wh, wl = take(base_c + ch)
                    tiles_of = (2 * ch, 2 * ch + 1) if ch < 2 else (2 + ch,)
                    for i, m in enumerate(tiles_of):
                        for k in range(KQ):
                            b = i * KQ + k
                            ins = mm3(ps[:, m, :], wh[:, b, :], wl[:, b, :], AH[:, k, :], AL[:, k, :],
                                      k == 0, k == KQ - 1)
                    done = used.did(ins)
                    for m in tiles_of:
                        if ch < 2:
                            wait(SC, done)
                            hi = act.did(SC.activation(QH[:, m, :], ps[:, m, :], ACT.Copy))
                            wait(VE, hi)
                            banks_read[m] = dve.did(VE.tensor_tensor(QL[:, m, :], ps[:, m, :], f32(QH[:, m, :]),
                                                                     ALU.subtract))
                        else:
                            wait(SC, done, banks_read.get("w0"))
                            raw = act.did(SC.activation(W0[:, :], ps[:, m, :], ACT.Copy))
                            banks_read["w0"] = rotate(6, W0[:, :], W1[:, :], QH[:, m, :], QL[:, m, :], raw)
                wh, wl = take(base_c + 4)
                wait(PE, *[banks_read[m] for m in range(4)])
                for h in range(4):
                    for k in range(KKV):
                        ins = mm3(ps[:, h, :], wh[:, h * KKV + k, :], wl[:, h * KKV + k, :], AH[:, KQ + k, :],
                                  AL[:, KQ + k, :], k == 0, k == KKV - 1)
                done = used.did(ins)
                kread = []
                for h in range(4):
                    wait(SC, done)
                    hi = act.did(SC.activation(KH[:, h, :], ps[:, h, :], ACT.Copy))
                    wait(VE, hi)
                    kread.append(dve.did(VE.tensor_tensor(KL[:, h, :], ps[:, h, :], f32(KH[:, h, :]), ALU.subtract)))
                slot = (base_c + 5).const % 2
                take(base_c + 5)
                vread = []
                wait(PE, banks_read["w0"])
                for q in range(4):
                    bank = 4 + q
                    for k in range(KKV):
                        cols = slice(q * P, (q + 1) * P)
                        ins = mm3(ps[:, bank, :], AH[:, KQ + k, cols], AL[:, KQ + k, cols],
                                  WH[:, slot, k * T:(k + 1) * T], WL[:, slot, k * T:(k + 1) * T],
                                  k == 0, k == KKV - 1)
                done = used.did(ins)
                for q in range(4):
                    wait(SC, done)
                    hi = act.did(SC.activation(VH[:, q, :], ps[:, 4 + q, :], ACT.Copy))
                    wait(VE, hi)
                    vread.append(dve.did(VE.tensor_tensor(VL[:, q, :], ps[:, 4 + q, :], f32(VH[:, q, :]),
                                                          ALU.subtract)))
                wait(PE, kread[-1], vread[-1])
                score_read = {}
                pt_read = {}
                pv_done = {}
                o_read = {}
                p_free = {}
                for h in range(4):
                    rows = slice((h % 2) * ROPE, (h % 2) * ROPE + ROPE)
                    scores = []
                    for q in range(4):
                        cols = slice(q * P, (q + 1) * P)
                        wait(PE, score_read.get(q))
                        mm3(ps[:, q, :], QH[:, h, cols], QL[:, h, cols], KH[:, h, :], KL[:, h, :], True, False)
                        ins = mm3(ps[:, q, :], QH[rows, 4 + h // 2, cols], QL[rows, 4 + h // 2, cols],
                                  krh[rows, :], krl[rows, :], False, True)
                        scores.append(pe.did(ins))
                    pts = []
                    for q in range(4):
                        n = 4 * h + q
                        slot = n % 2
                        wait(VE, scores[q])
                        t = dve.did(VE.tensor_reduce(sm[:, q, 0:1], ps[:, q, :], AX_X, ALU.max))
                        wait(VE, t)
                        t = dve.did(VE.tensor_scalar(sm[:, q, 1:2], sm[:, q, 0:1], -SM_SCALE, None, ALU.mult))
                        wait(SC, t, p_free.get(slot))
                        e = act.did(SC.activation(PB[:, slot, :], ps[:, q, :], ACT.Exp, bias=sm[:, q, 1:2],
                                                  scale=SM_SCALE, accum_out=sm[:, q, 2:3]))
                        score_read[q] = e
                        wait(VE, e)
                        t = dve.did(VE.reciprocal(sm[:, q, 3:4], sm[:, q, 2:3]))
                        wait(VE, t)
                        t = dve.did(VE.tensor_scalar(PB[:, slot, :], PB[:, slot, :], sm[:, q, 3:4], None, ALU.mult))
                        bank = 4 + slot
                        wait(PE, t, pt_read.get(bank))
                        for kt in range(4):
                            ins = PE.transpose(ps[:, bank, kt * P:(kt + 1) * P], PB[:, slot, kt * P:(kt + 1) * P],
                                               ident[:, :])
                        t = pe.did(ins)
                        p_free[slot] = t
                        cols = slice(q * P, (q + 1) * P)
                        src = ps[:, bank, :].rearrange("p (k q) -> p k q", k=4)
                        wait(SC, t, pv_done.get("last"))
                        hi = act.did(SC.activation(PTH[:, :, cols], src, ACT.Copy))
                        wait(VE, hi)
                        pt_read[bank] = dve.did(VE.tensor_tensor(PTL[:, :, cols], src, f32(PTH[:, :, cols]),
                                                                 ALU.subtract))
                    bank = 6 + h % 2
                    wait(PE, pt_read[4], pt_read[5], o_read.get(bank))
                    for kt in range(4):
                        ins = mm3(ps[:, bank, :], VH[:, kt, h * P:(h + 1) * P], VL[:, kt, h * P:(h + 1) * P],
                                  PTH[:, kt, :], PTL[:, kt, :], kt == 0, kt == 3)
                    pv_done["last"] = pe.did(ins)
                    wait(SC, pv_done["last"])
                    oh, ol = tile(OH, g + h), tile(OL, g + h)
                    hi = act.did(SC.activation(oh, ps[:, bank, :], ACT.Copy))
                    wait(VE, hi)
                    o_read[bank] = dve.did(VE.tensor_tensor(ol, ps[:, bank, :], f32(oh), ALU.subtract))
                wait(PE, o_read[6], o_read[7])
                wait(SC, pv_done["last"])
                wait(VE, pv_done["last"])

            with p.loop(N_GROUPS, per(6, pe=2 + 4 * (4 + 4 + 1), act=4 + 2 + 4 + 4 + 4 * (4 + 4 + 1),
                                      dve=4 + 2 * 5 + 4 + 4 + 4 * (4 * 5 + 1))):
                head_group(Val(0, 4), Val(base, 6))
            heads_done = Token(dve, dve.val)
            arrived, acc = out_linear("mla", "mla_out", OH, OL, [heads_done] * KD, s4)
            ready = layer_norm("n2", arrived, acc, EPS_2, (par_all("a_g0"), par_all("a_b0")),
                               (AFF[:, 4, 0, :], AFF[:, 4, 1, :]))

        arrived = ffn("f1", "up_2", "down_2", "conv0", ready, None)
        ready = layer_norm("n3", arrived, None, EPS_2, (par_all("f_g0"), par_all("f_b0")),
                           (AFF[:, 5, 0, :], AFF[:, 5, 1, :]))

        s5 = ExitStack()
        with s5:
            U = p.sb(s5, "hy_branches", [P, 24, T])
            YH = p.sb(s5, "hy_product_hi", [P, 2, 4, T], F32R)
            YL = p.sb(s5, "hy_product_lo", [P, 2, 4, T], F32R)
            FH = p.sb(s5, "dft_fwd_hi", [P, 16, P], F32R)
            FL = p.sb(s5, "dft_fwd_lo", [P, 16, P], F32R)
            IH = p.sb(s5, "dft_inv_hi", [P, 8, HALF], F32R)
            IL = p.sb(s5, "dft_inv_lo", [P, 8, HALF], F32R)
            KS = p.sb(s5, "hy_filter", [P, 4, T])
            s_tab, s_xs, s_ks = p.count("tables"), p.count("x_spill"), p.count("filter_load")
            spilled = []
            SP_wait = ready
            kept_all = Token(act, act.val)
            wait(SP, kept_all)
            for k in range(KD):
                spilled = s_xs.did(SP.dma_start(a["x_spill"][k], X[:, k, :]), 16)
            base = FIRST_CHUNK["hy_in"]
            settle(VE, SC, SP)

            def branch(c, m, u, prev, tiles):
                wh, wl = take(c)
                wait(PE, prev)
                for k in range(KD):
                    if tiles is not None:
                        wait(PE, tiles[k])
                    ins = mm3(ps[:, u, :], wh[:, k, :], wl[:, k, :], AH[:, k, :], AL[:, k, :], k == 0, k == KD - 1)
                done = used.did(ins)
                return conv3(tile(U, m), u, [column("hy_short", m * 3 + s) for s in range(3)], done, None)

            b0 = branch(Val(base), Val(0), 0, None, ready)
            b1 = branch(Val(base + 1), Val(1), 1, None, None)
            with p.loop(11, per(2, act=2, dve=4)):
                for u, b in ((0, b0), (1, b1)):
                    branch(Val(base + 2 + u, 2), Val(2 + u, 2), u, Token(dve, Val(b.val.const, 4)), None)
            branches = Token(dve, dve.val)

            raw_t = X[:, 0:4, :].rearrange("p a b -> p (a b)")
            raw_i = X[:, 4:8, :].rearrange("p a b -> p (a b)")
            wait(SP, spilled)
            s_tab.did(SP.dma_start(raw_t, a["dft_fwd"].rearrange("p a b -> p (a b)")), 16)
            got_tabs = s_tab.did(SP.dma_start(raw_i, a["dft_inv"].rearrange("p a b -> p (a b)")), 16)
            wait(VE, got_tabs)
            flat = lambda t: t[:, :, :].rearrange("p a b -> p (a b)")
            for raw_, h_, l_ in ((raw_t, FH, FL), (raw_i, IH, IL)):
                tabs_done = split_act(flat(h_), flat(l_), raw_, None)

            def conv_half(order, n, z_ready):
                wait(PE, z_ready)
                zsplit = []
                for q in range(4):
                    for m in range(4):
                        zt_ = U[:, 4 * n + m, :].rearrange("p (t two) -> p two t", two=2)
                        src = zt_[:, q // 2, (q % 2) * P:(q % 2 + 1) * P]
                        ins = PE.transpose(ps[:, q, m * P:(m + 1) * P], src, ident[:, :])
                    t = pe.did(ins)
                    wait(SC, t)
                    hi = act.did(SC.activation(AH[:, 4 + q, :], ps[:, q, :], ACT.Copy))
                    wait(VE, hi)
                    zsplit.append(dve.did(VE.tensor_tensor(AL[:, 4 + q, :], ps[:, q, :], f32(AH[:, 4 + q, :]),
                                                           ALU.subtract)))
                wait(PE, zsplit[-1])
                mult_done = zsplit[-1]
                for f in range(2):
                    wait(SP, mult_done, tabs_done, Token(s_spec, Val(s_spec.val.const)))
                    ks = s_ks.did(SP.dma_start(KS[:, :, :], a["spectra"][order, n, f]), 16)
                    for kind in range(2):
                        for parity in range(2):
                            for k in range(2):
                                b = ((kind * 2 + parity) * 2 + k) * 2 + f
                                ins = mm3(ps[:, 4 * (1 - f) + 2 * kind + parity, :], FH[:, b, :], FL[:, b, :],
                                          AH[:, 4 + 2 * parity + k, :], AL[:, 4 + 2 * parity + k, :], k == 0, k == 1)
                    fwd = pe.did(ins)
                    bk = 4 * (1 - f)
                    S = lambda i: X[:, i, :]
                    wait(SC, fwd, mult_done)
                    act.did(SC.activation(S(4), ps[:, bk + 1, :], ACT.Copy))
                    t = act.did(SC.activation(S(5), ps[:, bk + 3, :], ACT.Copy))
                    wait(VE, t, mult_done)
                    dve.did(VE.tensor_tensor(S(0), ps[:, bk, :], S(4), ALU.add))
                    dve.did(VE.tensor_tensor(S(1), ps[:, bk + 2, :], S(5), ALU.add))
                    dve.did(VE.tensor_tensor(S(2), ps[:, bk, :], S(4), ALU.subtract))
                    zpm = dve.did(VE.tensor_tensor(S(3), ps[:, bk + 2, :], S(5), ALU.subtract))
                    wait(GP, zpm, ks)
                    pool.did(GP.tensor_tensor(S(6), S(2), KS[:, 1, :], ALU.mult))
                    t = pool.did(GP.tensor_tensor(S(7), S(3), KS[:, 3, :], ALU.mult))
                    wait(GP, t)
                    t = pool.did(GP.tensor_tensor(S(6), S(6), S(7), ALU.subtract))
                    pool.did(GP.tensor_tensor(S(2), S(2), KS[:, 3, :], ALU.mult))
                    t = pool.did(GP.tensor_tensor(S(3), S(3), KS[:, 1, :], ALU.mult))
                    wait(GP, t)
                    vdone = pool.did(GP.tensor_tensor(S(2), S(2), S(3), ALU.add))
                    wait(VE, zpm, ks)
                    dve.did(VE.tensor_tensor(S(4), S(0), KS[:, 0, :], ALU.mult))
                    t = dve.did(VE.tensor_tensor(S(5), S(1), KS[:, 2, :], ALU.mult))
                    wait(VE, t)
                    dve.did(VE.tensor_tensor(S(4), S(4), S(5), ALU.subtract))
                    dve.did(VE.tensor_tensor(S(0), S(0), KS[:, 2, :], ALU.mult))
                    t = dve.did(VE.tensor_tensor(S(1), S(1), KS[:, 0, :], ALU.mult))
                    wait(VE, t)
                    t = dve.did(VE.tensor_tensor(S(0), S(0), S(1), ALU.add))
                    wait(VE, t, vdone)
                    sums = []
                    for i, (dst, x1, x2, op) in enumerate(((1, 4, 6, ALU.add), (3, 0, 2, ALU.add),
                                                           (5, 4, 6, ALU.subtract), (7, 0, 2, ALU.subtract))):
                        sums.append(dve.did(VE.tensor_tensor(S(dst), S(x1), S(x2), op)))
                    for i, dst in enumerate((1, 3, 5, 7)):
                        wait(SC, sums[i])
                        hi = act.did(SC.activation(YH[:, f, i, :], S(dst), ACT.Copy))
                        wait(VE, hi)
                        mult_done = dve.did(VE.tensor_tensor(YL[:, f, i, :], S(dst), f32(YH[:, f, i, :]),
                                                             ALU.subtract))
                wait(PE, mult_done)
                outs = []
                for m in range(4):
                    for parity in range(2):
                        n_k = 0
                        for f in range(2):
                            for kind in range(2):
                                b = (kind * 2 + parity) * 2 + f
                                cols = slice(m * P, (m + 1) * P)
                                ins = mm3(ps[:, m, parity * HALF:(parity + 1) * HALF],
                                          YH[:, f, 2 * parity + kind, cols], YL[:, f, 2 * parity + kind, cols],
                                          IH[:, b, :], IL[:, b, :], n_k == 0, n_k == 3)
                                n_k += 1
                    t = pe.did(ins)
                    wait(VE, t)
                    view = lambda ap: ap.rearrange("p (t two) -> p two t", two=2)
                    z = U[:, 4 * n + m, :]
                    gate = U[:, 8 * (order + 1) + 4 * n + m, :]
                    y = ps[:, m, :].rearrange("p (two t) -> p two t", two=2)
                    t = dve.did(VE.scalar_tensor_tensor(out=view(z), in0=view(z),
                                                        scalar=par("hy_d", 8 * order + 4 * n + m), in1=y,
                                                        op0=ALU.mult, op1=ALU.add))
                    wait(VE, t)
                    t = dve.did(VE.tensor_tensor(z, z, gate, ALU.mult))
                    if order == 1:
                        t = split_act(AH[:, 4 * n + m, :], AL[:, 4 * n + m, :], z, t)
                    outs.append(t)
                wait(PE, outs[-1])
                return outs

            z0 = conv_half(0, 0, branches)
            z1 = conv_half(0, 1, branches)
            r0 = conv_half(1, 0, z0[-1])
            r1 = conv_half(1, 1, z1[-1])
            wait(SP, r1[-1])
            for k in range(KD):
                back = s_xs.did(SP.dma_start(X[:, k, :], a["x_spill"][k]), 16)
            wait(VE, back)
            arrived, acc = out_linear("hy", "hy_out", AH, AL, r0 + r1, s5)
            ready = layer_norm("n4", arrived, acc, EPS_2, (par_all("a_g1"), par_all("a_b1")),
                               (AFF[:, 6, 0, :], AFF[:, 6, 1, :]))

        arrived = ffn("f2", "up_3", "down_3", "conv1", ready, None)
        done = layer_norm("n5", arrived, None, EPS_2, None, (par_all("f_g1"), par_all("f_b1")), last=True)
        s_out = p.count("stored")
        for k in range(KD):
            wait(SP, done[k])
            stored = s_out.did(SP.dma_start(out[k * P:(k + 1) * P, :], X[:, k, :]), 16)
        wait(SP, stored)
        wait(SP, Token(s_xs, s_xs.val))


def time_order():
    return np.concatenate([np.arange(0, T, 2), np.arange(1, T, 2)])


def shape_constants():
    f32 = np.float32
    order = time_order()
    freq = (2 * np.arange(HALF) + 1) * np.pi / (2 * T)
    fwd = np.zeros((P, 16, P), f32)
    inv = np.zeros((P, 8, HALF), f32)
    for kind, fn in enumerate((np.cos, np.sin)):
        for parity in range(2):
            times = np.arange(parity, T, 2)
            table = fn(np.outer(times, freq))
            for k in range(2):
                for f in range(2):
                    fwd[:, ((kind * 2 + parity) * 2 + k) * 2 + f] = table[k * P:(k + 1) * P, f * P:(f + 1) * P]
            for f in range(2):
                inv[:, (kind * 2 + parity) * 2 + f] = table.T[f * P:(f + 1) * P] / T
    t = np.linspace(0.0, 1.0, T, dtype=f32)[:, None]
    bands = (HY_EMB - 1) // 2
    w = (2.0 * math.pi * np.arange(T, dtype=f32)[:, None] / T).astype(f32)
    fr = np.linspace(1e-4, bands - 1, bands, dtype=f32)[None, :]
    z = np.concatenate([t, np.cos(fr * w), -np.sin(fr * w)], axis=-1).astype(f32)
    deltas = np.abs(np.linspace(math.log(0.3) / 1e-2, math.log(1.5) / 1e-2, D, dtype=f32))
    decay = np.exp(-t * deltas).astype(f32)
    steps = np.arange(T)
    counts = []
    for win in POOL_WINDOWS:
        lo = win // 2
        start, end = np.clip(steps - lo, 0, T), np.clip(steps + win - lo, 0, T)
        counts.append(np.concatenate([1.0 / (end - start)[:PAD], 1.0 / (end - start)[T - PAD:]]))
    inv_freq = (1.0 / (10000.0 ** (np.arange(0, ROPE, 2, dtype=f32) / f32(ROPE)))).astype(f32)
    rope = np.stack([np.tile(inv_freq, 4), np.tile(np.repeat([-1.0, 1.0], ROPE // 2), 2)], 1).astype(f32)
    swap = np.zeros((P, P), f32)
    rows = np.arange(P)
    swap[rows, rows ^ (ROPE // 2)] = 1.0
    return {
        "dft_fwd": fwd, "dft_inv": inv, "hy_z": np.ascontiguousarray(z[order].T),
        "decay": np.ascontiguousarray(decay[order].reshape(4, P, D).transpose(1, 0, 2)),
        "inv_count": np.ascontiguousarray(np.broadcast_to(np.array(counts, f32), (P, 4, 2 * PAD))),
        "rope_consts": rope, "rope_swap": swap, "identity": np.eye(P, dtype=f32),
    }


def columns(v):
    return np.asarray(v).reshape(-1, P).T


def by_output_tile(w):
    k, m = w.shape
    return w.reshape(k // P, P, m // P, P).transpose(2, 1, 0, 3).reshape(m // P, P, k)


def weight_stream(i):
    parts = []
    pw = i["pool_w"][0].reshape(2, 2, 2, P, 2, P)
    parts.append(pw.transpose(0, 3, 1, 4, 2, 5).reshape(2, P, CHUNK))
    w = by_output_tile(i["ffn_w_in"][0])
    parts.append(w.reshape(2, KF, P, CHUNK).transpose(1, 0, 2, 3).reshape(2 * KF, P, CHUNK))
    parts.append(i["ffn_w_out"][0].reshape(KF, P, D))
    w = i["mla_w_in_2"][0]
    parts.append(by_output_tile(np.concatenate([w, w[:, RQ + RKV:]], axis=1)))
    uq = i["mla_w_uq_2"][0].reshape(KQ, P, HEADS, NOPE + ROPE)
    ukv = i["mla_w_ukv_2"][0].reshape(KKV, P, HEADS, NOPE + VD)
    for g in range(N_GROUPS):
        hs = slice(4 * g, 4 * g + 4)
        nope = uq[:, :, hs, :NOPE].reshape(KQ, P, 2, 2, P).transpose(2, 1, 3, 0, 4).reshape(2, P, 2 * KQ * P)
        rope = uq[:, :, hs, NOPE:].reshape(KQ, P, 2, P).transpose(2, 1, 0, 3).reshape(2, P, KQ * P)
        for part in (nope, rope):
            padded = np.zeros((2, P, CHUNK), part.dtype)
            padded[:, :, :part.shape[2]] = part
            parts.append(padded)
        parts.append(ukv[:, :, hs, :NOPE].transpose(1, 2, 0, 3).reshape(1, P, CHUNK))
        parts.append(ukv[:, :, hs, NOPE:].transpose(1, 0, 2, 3).reshape(1, P, CHUNK))
    parts.append(by_output_tile(i["mla_w_o_2"][0]))

    def conv_ffn(layer):
        w = by_output_tile(i["ffn_w_up_2"][layer])
        parts.append(w.reshape(2, KF, P, CHUNK).transpose(1, 0, 2, 3).reshape(2 * KF, P, CHUNK))
        parts.append(i["ffn_w_down_2"][layer].reshape(KF, P, D))

    conv_ffn(0)
    parts.append(by_output_tile(i["hy_w_in_2"][0]))
    parts.append(by_output_tile(i["hy_w_o_2"][0]))
    conv_ffn(1)
    out = np.concatenate(parts, axis=0)
    assert out.shape == (N_CHUNKS, P, CHUNK), out.shape
    return out


def taps(w):
    return w.reshape(3, -1, P).transpose(2, 1, 0).reshape(P, -1)


def lay_out(i):
    cols = {
        "c": columns(i["c"][0]), "mod_b": columns(i["mod_b"][0]),
        "ln_g0": columns(i["ln_g"][0, 0]), "ln_b0": columns(i["ln_b"][0, 0]),
        "ln_g1": columns(i["ln_g"][0, 1]), "ln_b1": columns(i["ln_b"][0, 1]),
        "pool_scale": columns(i["pool_scale"][0]), "g_q": columns(i["mla_g_q_2"][0]),
        "g_kv": columns(i["mla_g_kv_2"][0]), "hy_short": taps(i["hy_w_short_2"][0]),
        "hy_d": columns(i["hy_d_bias_2"][0]), "conv0": taps(i["ffn_w_conv_2"][0]),
        "conv1": taps(i["ffn_w_conv_2"][1]),
    }
    for layer in range(2):
        for key, name in (("a", "ln1"), ("f", "ln2")):
            cols[f"{key}_g{layer}"] = columns(i[f"{name}_g_2"][layer])
            cols[f"{key}_b{layer}"] = columns(i[f"{name}_b_2"][layer])
    arrays = {
        "params": np.ascontiguousarray(np.concatenate([cols[n] for n in PARAMS], axis=1)),
        "xT": np.ascontiguousarray(i["x"][0].T),
        "mod_w": np.ascontiguousarray(i["mod_w"][0].reshape(KD, P, 16, 3 * P).transpose(2, 1, 0, 3)),
        "w_stream": weight_stream(i),
        "positions": np.ascontiguousarray(i["positions_2"]),
        "hy_fw1": np.ascontiguousarray(i["hy_fw1_2"][0]),
        "hy_small": np.ascontiguousarray(np.concatenate(
            [i["hy_fw2_2"][0], i["hy_fw3_2"][0]] +
            [i[n][0][:, None] for n in ("hy_fb1_2", "hy_fb2_2", "hy_fb3_2", "hy_freq_2")], axis=1)),
        "hy_fw_out": np.ascontiguousarray(i["hy_fw_out_2"][0].reshape(HY_W, 2, 2, D)),
    }
    arrays.update(shape_constants())
    return arrays


def kernel(**inputs):
    import concourse.bacc as bacc
    from concourse.bass_utils import run_bass_kernel_spmd

    arrays = lay_out({k: np.asarray(v) for k, v in inputs.items()})
    nc = bacc.Bacc("TRN2", target_bir_lowering=False, num_devices=1)
    aps = {n: nc.dram_tensor(f"in_{n}", v.shape, mybir.dt.from_np(v.dtype), kind="ExternalInput").ap()
           for n, v in arrays.items()}
    aps["spectra"] = nc.dram_tensor("spectra", (2, 2, 2, P, 4, T), F32, kind="Internal").ap()
    aps["x_spill"] = nc.dram_tensor("x_spill", (KD, P, T), F32, kind="Internal").ap()
    out = nc.dram_tensor("out_x", (D, T), F32, kind="ExternalOutput").ap()
    build_program(nc, aps, out)
    result = run_bass_kernel_spmd(nc, [{f"in_{n}": v for n, v in arrays.items()}], core_ids=[0])
    return np.ascontiguousarray(result.results[0]["out_x"].T)[None]
```

```python
import math
from contextlib import ExitStack, contextmanager

import numpy as np

import concourse.bass as bass
from concourse import mybir

F32 = mybir.dt.float32
F32R = mybir.dt.float32r
I32 = mybir.dt.int32
ACT = mybir.ActivationFunctionType
ALU = mybir.AluOpType
AX_X = mybir.AxisListType.X

P = 128
T = 512
D = 1024
KD = D // P
FF = 2816
KF = FF // P
CHUNK = 1024
HEADS, NOPE, ROPE, VD = 8, 128, 64, 128
RQ, RKV = 384, 256
KQ, KKV = RQ // P, RKV // P
POOL_WINDOWS = (2, 4, 8, 16)
PAD = 8
HALF = T // 2
ALPHA_1 = 2.0 ** 0.25
ALPHA_2 = 4.0 ** 0.25
EPS_1, EPS_2, EPS_RMS = 1e-6, 1e-5, 1e-6
HY_EMB, HY_W = 33, 64
SM_SCALE = (NOPE + ROPE) ** -0.5

INV_2PI = float(np.float32(1.0 / (2 * math.pi)))
PI2_A = 6.28125
PI2_B = float(np.float32(2 * math.pi - PI2_A))
PI2_C = float(np.float32(2 * math.pi - PI2_A - PI2_B))
ROUND = float(1.5 * 2 ** 23)
PI_LOW = 3.1415925

PARAMS = {}
_at = 0
for _name, _n in (("c", KD), ("mod_b", 48), ("ln_g0", KD), ("ln_b0", KD), ("ln_g1", KD), ("ln_b1", KD),
                  ("pool_scale", KD), ("g_q", KQ), ("g_kv", KKV), ("hy_short", 3 * 24), ("hy_d", 2 * KD),
                  ("conv0", 3 * 2 * KF), ("conv1", 3 * 2 * KF),
                  ("a_g0", KD), ("a_b0", KD), ("f_g0", KD), ("f_b0", KD),
                  ("a_g1", KD), ("a_b1", KD), ("f_g1", KD), ("f_b1", KD)):
    PARAMS[_name] = (_at, _n)
    _at += _n
N_PARAMS = _at

N_GROUPS = 2
STREAM = (("pool", 2), ("up_1", 2 * KF), ("down_1", KF), ("mla_in", 6), ("mla_heads", 6 * N_GROUPS),
          ("mla_out", KD), ("up_2", 2 * KF), ("down_2", KF), ("hy_in", 24), ("hy_out", KD),
          ("up_3", 2 * KF), ("down_3", KF))
FIRST_CHUNK = {}
_at = 0
for _name, _n in STREAM:
    FIRST_CHUNK[_name] = _at
    _at += _n
N_CHUNKS = _at


class Val:

    def __init__(self, const, step=0):
        self.const, self.step = const, step

    def __add__(self, n):
        return Val(self.const + n, self.step)

    def __mul__(self, n):
        return Val(self.const * n, self.step * n)

    def half(self):
        assert self.step % 2 == 0
        return Val(self.const // 2, self.step // 2)

    def of(self, loop_index):
        return self.const if not self.step else loop_index * self.step + self.const


class Token:

    def __init__(self, count, val):
        self.count, self.val = count, val

    def before(self):
        assert self.val.step
        return Token(self.count, self.val + -self.val.step)


class Count:

    def __init__(self, handle):
        self.handle, self.val = handle, Val(0)

    def did(self, instruction, by=1):
        instruction.then_inc(self.handle, by)
        self.val = self.val + by
        return Token(self, self.val)


class Program:
    def __init__(self, nc, ctx):
        self.nc, self.ctx, self.index = nc, ctx, None
        self.pe, self.act, self.dve, self.pool = (self.count(n) for n in ("pe", "act", "dve", "pool"))
        self.raw = [self.count("raw_even"), self.count("raw_odd")]
        self.hi_done, self.lo_done = self.count("hi_done"), self.count("lo_done")
        self.used = self.count("chunk_used")
        self.everything = [self.pe, self.act, self.dve, self.pool, *self.raw, self.hi_done, self.lo_done, self.used]

    def count(self, name):
        return Count(self.ctx.enter_context(self.nc.semaphore("s_" + name)))

    def sb(self, ctx, name, shape, dt=F32):
        return ctx.enter_context(self.nc.sbuf_tensor(name, shape, dt))

    def wait(self, engine, *tokens):
        for t in tokens:
            if t is not None:
                engine.wait_ge(t.count.handle, t.val.of(self.index))

    @contextmanager
    def loop(self, n, per, extra=()):
        start = {c: c.val.const for c in self.everything + list(extra)}
        with self.nc.Fori(0, n) as i:
            self.index = i
            for c in start:
                c.val = Val(start[c], per.get(c, 0))
            yield i
        for c, v in start.items():
            assert c.val.const - v == per.get(c, 0), (c.handle, c.val.const - v, per.get(c, 0))
            c.val = Val(v + n * per.get(c, 0))
        self.index = None


def build_program(nc, a, out):
    ctx = ExitStack()
    with ctx:
        p = Program(nc, ctx)
        PE, SC, VE, GP, SP = nc.tensor, nc.scalar, nc.vector, nc.gpsimd, nc.sync
        pe, act, dve, pool, used = p.pe, p.act, p.dve, p.pool, p.used
        wait = p.wait

        X = p.sb(ctx, "x_residual", [P, KD, T])
        AH = p.sb(ctx, "act_hi", [P, KD, T], F32R)
        AL = p.sb(ctx, "act_lo", [P, KD, T], F32R)
        WR = p.sb(ctx, "w_raw", [P, 2, CHUNK])
        WH = p.sb(ctx, "w_hi", [P, 2, CHUNK], F32R)
        WL = p.sb(ctx, "w_lo", [P, 2, CHUNK], F32R)
        PV = p.sb(ctx, "params", [P, N_PARAMS])
        MOD = p.sb(ctx, "mod_x", [P, 48])
        icnt = p.sb(ctx, "pool_1_over_count", [P, 4, 2 * PAD])
        AFF = p.sb(ctx, "affine", [P, 7, 2, KD])
        ident = p.sb(ctx, "identity", [P, P])
        mean_w = p.sb(ctx, "mean_weights", [P, P])
        ones = p.sb(ctx, "ones", [P, P])
        stat = p.sb(ctx, "stat", [P, 4, 4])
        x_sum = p.sb(ctx, "x_sum", [P, T])
        minus_half = p.sb(ctx, "minus_half", [P, 4])
        ps = ctx.enter_context(nc.psum_tensor("ps", [P, 8, 512], F32))

        def par(name, k=0):
            at, n = PARAMS[name]
            assert k < n
            return PV[:, at + k:at + k + 1]

        def par_all(name):
            at, n = PARAMS[name]
            return PV[:, at:at + n]

        def f32(ap):
            return ap.bitcast(F32)

        def tile(buf, k):
            if not isinstance(k, Val) or not k.step:
                return buf[:, k.const if isinstance(k, Val) else k, :]
            return buf[:, bass.ds(k.of(p.index), 1), :].rearrange("p a b -> p (a b)")

        def mm3(o, lh, ll, rh, rl, start, stop, **kw):
            PE.matmul(o, lh, rh, start=start, stop=False, **kw)
            PE.matmul(o, lh, rl, start=False, stop=False, **kw)
            return PE.matmul(o, ll, rh, start=False, stop=stop, **kw)

        stream = a["w_stream"]

        def fetch(c):
            if c.step == 0 and c.const >= N_CHUNKS:
                return
            slot = c.const % 2
            if c.const >= 2:
                wait(SP, Token(p.lo_done, c + -1))
            src = stream[c.const] if not c.step else stream[bass.ds(c.of(p.index), 1)].rearrange("a p n -> (a p) n")
            p.raw[slot].did(SP.dma_start(WR[:, slot, :], src), 16)

        def split(c):
            if c.step == 0 and c.const >= N_CHUNKS:
                return
            slot = c.const % 2
            landed = Token(p.raw[slot], c.half() * 16 + 16)
            if c.const >= 2:
                wait(SC, Token(used, c + -1))
            wait(SC, landed)
            p.hi_done.did(SC.activation(WH[:, slot, :], WR[:, slot, :], ACT.Copy))
            wait(GP, Token(p.hi_done, c + 1))
            p.lo_done.did(GP.tensor_tensor(WL[:, slot, :], WR[:, slot, :], f32(WH[:, slot, :]), ALU.subtract))

        early = set()

        def split_early(chunk):
            early.add(chunk)
            split(Val(chunk))

        def take(c):
            if c.step or c.const + 1 not in early:
                split(c + 1)
            fetch(c + 2)
            wait(PE, Token(p.lo_done, c + 1))
            slot = c.const % 2
            return (WH[:, slot, :].rearrange("p (b m) -> p b m", m=P),
                    WL[:, slot, :].rearrange("p (b m) -> p b m", m=P))

        def take_two(c, tiles):
            blocks, done = [take(c), take(c + 1)], []
            behind = 3
            for k in range(KD + behind):
                for bank, at in ((0, k), (1, k - behind)):
                    if 0 <= at < KD:
                        wh, wl = blocks[bank]
                        if bank == 0:
                            wait(PE, tiles[at])
                        ins = mm3(ps[:, bank, :], wh[:, at, :], wl[:, at, :], AH[:, at, :], AL[:, at, :],
                                  at == 0, at == KD - 1)
                        if at == KD - 1:
                            done.append(used.did(ins))
            return done

        def per(chunks, **own):
            rises = {used: chunks, p.hi_done: chunks, p.lo_done: chunks, p.raw[0]: 8 * chunks, p.raw[1]: 8 * chunks}
            rises.update({{"pe": pe, "act": act, "dve": dve, "pool": pool}[k]: v for k, v in own.items()})
            return rises

        s_par, s_x, s_hy, s_con = p.count("params"), p.count("x"), p.count("hyena_small"), p.count("constants")
        got_par = s_par.did(SP.dma_start(PV[:, :], a["params"]), 16)
        VE.memset(ones[:, :], 1.0)
        VE.memset(minus_half[:, :], -0.5)
        made_ones = dve.did(VE.memset(mean_w[:, :], 1.0 / D))

        s1 = ExitStack()
        with s1:
            MC = 3
            MW = p.sb(s1, "mod_ring", [P, 4, KD, MC * P])
            macc = p.sb(s1, "mod_sums", [P, 2, MC * P])
            sc = p.sb(s1, "silu_c", [P, KD])
            zt = p.sb(s1, "positions_features", [HY_EMB, T])
            fw1 = p.sb(s1, "fw1", [HY_EMB, HY_W])
            fws = p.sb(s1, "fw23_bias_freq", [HY_W, 2 * HY_W + 4])
            fwo = X[0:HY_W, :, :].rearrange("p (o d h) t -> p o d (h t)", o=2, d=2)
            fsd = p.sb(s1, "fw_out_sum_diff", [P, 2, 2, D])
            hid = p.sb(s1, "filter_hidden", [P, T])
            red = p.sb(s1, "sin_turns", [HY_W, T])
            decay = p.sb(s1, "decay", [P, 4, D])
            tabr = WR[:, :, :].rearrange("p s (b m) -> p (s b) m", m=P)
            tabh, tabl = (t[:, 4:8, :].rearrange("p k (b m) -> p (k b) m", m=P) for t in (AH, AL))
            flt = p.sb(s1, "filter_taps", [P, 4, T])
            flh, fll = AH[:, 0:4, :], AL[:, 0:4, :]
            odd = p.sb(s1, "odd_spectrum", [P, 2, T])
            kspec = p.sb(s1, "filter_spectra", [P, 2, 4, T])

            s_fwo, s_dft = p.count("filter_out_weights"), p.count("dft_first")
            for dst, name in ((zt, "hy_z"), (fw1, "hy_fw1"), (fws, "hy_small")):
                got_small = s_hy.did(SP.dma_start(dst[:, :], a[name]), 16)
            got_fwo = s_fwo.did(SP.dma_start(fwo, a["hy_fw_out"]), 16)
            got_tab = s_dft.did(SP.dma_start(tabr, a["dft_fwd"]), 16)
            got_decay = s_con.did(SP.dma_start(decay[:, :, :], a["decay"]), 16)
            s_spec = p.count("filter_io")
            got_decay = s_con.did(SP.dma_start(icnt[:, :, :], a["inv_count"]), 16)
            s_spec.did(SP.dma_start(ident[:, :], a["identity"]), 16)

            s_mod = [p.count(f"mod{i}") for i in range(4)]
            mod_used, mod_summed = p.count("mod_used"), p.count("mod_summed")
            for h in range(4):
                mod_used.did(VE.memset(hid[:, h * P:(h + 1) * P], 0.0))
                if h < 2:
                    mod_summed.did(PE.nop())
            cleared = pool.did(GP.memset(fsd[:, :, :, :], 0.0))
            wait(VE, Token(mod_used, Val(4)))
            wait(SC, Token(mod_used, Val(4)))

            wait(SC, got_par)
            got_sc = act.did(SC.activation(sc[:, :], par_all("c"), ACT.Silu))

            def reduce_sin(out_ap, arg, turns):
                t = dve.did(VE.tensor_scalar(turns, arg, INV_2PI, ROUND, ALU.mult, ALU.add))
                wait(VE, t)
                t = dve.did(VE.tensor_scalar(turns, turns, ROUND, None, ALU.subtract))
                for part in (PI2_A, PI2_B, PI2_C):
                    wait(VE, t)
                    t = dve.did(VE.scalar_tensor_tensor(out=arg, in0=turns, scalar=-part, in1=arg,
                                                        op0=ALU.mult, op1=ALU.add))
                wait(VE, t)
                t = dve.did(VE.tensor_scalar(arg, arg, PI_LOW, -PI_LOW, ALU.min, ALU.max))
                if out_ap is None:
                    return t
                wait(SC, t)
                return act.did(SC.activation(out_ap, arg, ACT.Sin))

            wait(PE, got_small)
            mlp = pe.did(PE.matmul(ps[0:HY_W, 0, :], fw1[:, :], zt[:, :], start=True, stop=True))
            for layer in range(3):
                wait(VE, mlp, got_small)
                at = 2 * HY_W
                arg = flt[0:HY_W, 0, :]
                t = dve.did(VE.tensor_scalar(arg, ps[0:HY_W, 0, :], fws[:, at + layer:at + layer + 1],
                                             fws[:, at + 3:at + 4], ALU.add, ALU.mult))
                wait(VE, t)
                h_done = reduce_sin(hid[0:HY_W, :], arg, red[:, :])
                if layer == 0:
                    wait(SC, got_tab)
                    tab_hi = act.did(SC.activation(tabh[:, :, :], tabr, ACT.Copy))
                if layer < 2:
                    wait(PE, h_done)
                    mlp = pe.did(PE.matmul(ps[0:HY_W, 0, :], fws[:, layer * HY_W:(layer + 1) * HY_W],
                                           hid[0:HY_W, :],
                                           start=True, stop=True))
            wait(GP, got_fwo, cleared)
            pool.did(GP.tensor_tensor(fsd[0:HY_W, 0, :, :], fwo[:, :, 0], fwo[:, :, 1], ALU.add))
            fsd_done = pool.did(GP.tensor_tensor(fsd[0:HY_W, 1, :, :], fwo[:, :, 0], fwo[:, :, 1], ALU.subtract))
            wait(GP, tab_hi)
            tab_done = pool.did(GP.tensor_tensor(tabl[:, :, :], tabr, f32(tabh[:, :, :]), ALU.subtract))

            def load_modulation(first, ring):
                for slot in range(2):
                    transfer = first + slot
                    wait(SP, Token(mod_used, transfer + 1))
                    src = a["mod_w"][bass.ds(transfer.of(p.index), 1)].rearrange("a p k n -> (a p) k n")
                    s_mod[ring + slot].did(SP.dma_start(MW[:, ring + slot, :, :], src), 16)

            def modulate(first, ring):
                t = [None, None]
                for k in range(KD):
                    for slot in range(2):
                        src, dst = MW[:, ring + slot, k, :], macc[:, slot, :]
                        if k == 0:
                            wait(VE, Token(s_mod[ring + slot], s_mod[ring + slot].val),
                                 Token(mod_summed, first + (slot + 1)))
                            ins = VE.tensor_scalar(dst, src, sc[:, 0:1], None, ALU.mult)
                        else:
                            wait(VE, t[slot])
                            ins = VE.scalar_tensor_tensor(out=dst, in0=src, scalar=sc[:, k:k + 1], in1=dst,
                                                          op0=ALU.mult, op1=ALU.add)
                        t[slot] = (mod_used if k == KD - 1 else dve).did(ins)

            def mod_sum(transfer, slot):
                wait(PE, Token(mod_used, transfer + 5))
                for i in range(MC):
                    col = ps[:, 7, bass.ds((transfer * MC + i).of(p.index), 1)]
                    ins = PE.matmul(col, macc[:, slot, i * P:(i + 1) * P], ones[:, 0:1], start=True, stop=True)
                mod_summed.did(ins)

            wait(PE, got_sc, h_done, fsd_done)
            wait(VE, got_decay)
            rises = {pe: 4 * (1 + 4), dve: 4 * (4 + 2 + 4 + 2 * 7), pool: 8, act: 4 * (4 + 2), s_spec: 64,
                     mod_summed: 8, mod_used: 8,
                     **{m: 32 for m in s_mod}}
            with p.loop(2, rises, extra=[s_spec, mod_used, mod_summed, *s_mod]) as order:
                stored = Token(s_spec, s_spec.val)
                butterfly = Token(dve, dve.val)
                transformed = Token(pe, pe.val)

                def make_taps(unit, read):
                    n, kind = divmod(unit, 2)
                    wait(PE, read)
                    for q in range(4):
                        fw = fsd[:, kind, bass.ds(order, 1), n * 512:(n + 1) * 512].rearrange("p a b -> p (a b)")
                        ins = PE.matmul(ps[:, q, :], hid[:, q * P:(q + 1) * P], fw, start=True, stop=True)
                    return pe.did(ins)

                def apply_decay(unit, taps, split_before):
                    n = unit // 2
                    wait(VE, taps, *split_before)
                    return [dve.did(VE.tensor_tensor(flt[:, q, :], ps[:, q, :], decay[:, q, n * 512:(n + 1) * 512],
                                                     ALU.mult)) for q in range(4)]

                def store_spectra(queue, n, made):
                    wait(queue, made)
                    for f in range(2):
                        dst = a["spectra"][bass.ds(order, 1), n, f].rearrange("a p c t -> (a p) c t")
                        tok = s_spec.did(queue.dma_start(dst, kspec[:, f, :, :]), 16)
                    return tok

                decayed = apply_decay(0, make_taps(0, butterfly), [])
                for unit in range(4):
                    n, kind = divmod(unit, 2)
                    if unit == 2:
                        load_modulation(Val(4, 8), 0)
                        load_modulation(Val(6, 8), 2)
                        stored = store_spectra(SP, 0, first_half)
                    elif unit < 2:
                        load_modulation(Val(2 * unit, 8), 2 * (unit % 2))
                    his, los = [], []
                    for q in range(4):
                        wait(SC, decayed[q], transformed)
                        his.append(act.did(SC.activation(flh[:, q, :], flt[:, q, :], ACT.Copy)))
                    for q in range(4):
                        engine, count = (GP, pool) if q % 2 == 0 else (VE, dve)
                        wait(engine, his[q])
                        los.append(count.did(engine.tensor_tensor(fll[:, q, :], flt[:, q, :],
                                                                  f32(flh[:, q, :]), ALU.subtract)))
                    modulate(Val(2 * unit, 8), 2 * (unit % 2))
                    taps = make_taps(unit + 1, decayed[3]) if unit < 3 else None
                    wait(PE, tab_done, butterfly)
                    copied, transformed_at = {}, {}
                    for f, parity in ((0, 1), (0, 0), (1, 0), (1, 1)):
                        bank = 5 if parity else 4 + 2 * f
                        if parity:
                            wait(PE, copied.get(0))
                        for k in range(2):
                            b = ((kind * 2 + parity) * 2 + k) * 2 + f
                            wait(PE, los[2 * parity + k])
                            ins = mm3(ps[:, bank, :], tabh[:, b, :], tabl[:, b, :],
                                      flh[:, 2 * parity + k, :], fll[:, 2 * parity + k, :], k == 0, k == 1)
                        transformed = transformed_at[f, parity] = pe.did(ins)
                        if parity:
                            wait(SC, transformed, butterfly)
                            copied[f] = act.did(SC.activation(odd[:, f, :], ps[:, 5, :], ACT.Copy))
                    for slot in range(2):
                        mod_sum(Val(2 * unit + slot, 8), slot)
                    if unit < 3:
                        decayed = apply_decay(unit + 1, taps, los)
                    for f in range(2):
                        wait(VE, copied[f], transformed_at[f, 0])
                        if kind == 0 and f == 0:
                            wait(VE, stored)
                        dve.did(VE.tensor_tensor(kspec[:, f, 2 * kind, :], ps[:, 4 + 2 * f, :], odd[:, f, :],
                                                 ALU.add))
                        butterfly = dve.did(VE.tensor_tensor(kspec[:, f, 2 * kind + 1, :], ps[:, 4 + 2 * f, :],
                                                             odd[:, f, :], ALU.subtract))
                    if unit == 1:
                        first_half = butterfly
                store_spectra(SC, 1, butterfly)
            for k in range(KD):
                got_x = s_x.did(SP.dma_start(X[:, k, :], a["xT"][k * P:(k + 1) * P, :]), 16)

            wait(VE, Token(mod_summed, mod_summed.val))
            mod_done = dve.did(VE.tensor_tensor(MOD[:, :], ps[:, 7, 0:48], par_all("mod_b"), ALU.add))
            wait(VE, mod_done)
            _, SC1, G1, SH2, SC2, G2 = (MOD[:, 8 * i:8 * i + 8] for i in range(6))
            dve.did(VE.tensor_scalar(AFF[:, 0, 0, :], SC1, 1.0, None, ALU.add))
            t = dve.did(VE.tensor_scalar(AFF[:, 1, 1, :], SC2, 1.0, None, ALU.add))
            wait(VE, t)
            dve.did(VE.tensor_tensor(AFF[:, 1, 0, :], par_all("ln_g0"), AFF[:, 1, 1, :], ALU.mult))
            t = dve.did(VE.tensor_tensor(AFF[:, 1, 1, :], par_all("ln_b0"), AFF[:, 1, 1, :], ALU.mult))
            wait(VE, t)
            dve.did(VE.tensor_tensor(AFF[:, 1, 1, :], AFF[:, 1, 1, :], SH2, ALU.add))
            dve.did(VE.tensor_tensor(AFF[:, 0, 1, :], G1, par_all("pool_scale"), ALU.mult))
            for row, (g, b), alpha in ((2, ("ln_g0", "ln_b0"), ALPHA_1), (3, ("ln_g1", "ln_b1"), ALPHA_2),
                                       (4, ("a_g0", "a_b0"), ALPHA_2), (5, ("f_g0", "f_b0"), ALPHA_2),
                                       (6, ("a_g1", "a_b1"), ALPHA_2)):
                if row == 2:
                    dve.did(VE.tensor_scalar(AFF[:, row, 0, :], par_all(g), alpha, None, ALU.mult))
                aff_done = dve.did(VE.tensor_scalar(AFF[:, row, 1, :], par_all(b), alpha, None, ALU.mult))
            stage1_dve = aff_done

        def layer_norm(tag, arrived, mean_by_sum, eps, to_a, keep, next_chunk):
            st = ExitStack()
            with st:
                sq = p.sb(st, f"{tag}_squares", [P, 4, T])
                var = p.sb(st, f"{tag}_variance", [P, T])
                val = p.sb(st, f"{tag}_values", [P, KD, T])
                if not mean_by_sum:
                    by_pool, summed_up = 5, None
                    for k in range(1, by_pool):
                        wait(GP, arrived[0], arrived[k], summed_up)
                        summed_up = pool.did(GP.tensor_tensor(x_sum[:, :], X[:, 0, :] if k == 1 else x_sum[:, :],
                                                              X[:, k, :], ALU.add))
                settle(SC, VE, GP)
                if next_chunk is not None:
                    split_early(next_chunk + 1)
                if mean_by_sum:
                    wait(PE, arrived[-1], made_ones)
                    ins = PE.matmul(ps[:, 0, :], mean_w[:, :], x_sum[:, :], start=True, stop=True)
                else:
                    for k in range(by_pool, KD):
                        wait(PE, arrived[k], arrived[0])
                        PE.matmul(ps[:, 0, :], mean_w[:, :], X[:, k, :], start=(k == by_pool), stop=False)
                    wait(PE, summed_up)
                    ins = PE.matmul(ps[:, 0, :], mean_w[:, :], x_sum[:, :], start=False, stop=True)
                mean = pe.did(ins)
                wait(VE, mean)
                summed = [None] * KD
                for k in range(KD):
                    centred = dve.did(VE.tensor_tensor(X[:, k, :], X[:, k, :], ps[:, 0, :], ALU.subtract))
                    wait(SC, centred, summed[k - 4] if k >= 4 else None)
                    squared = act.did(SC.activation(sq[:, k % 4, :], X[:, k, :], ACT.Square))
                    wait(PE, squared)
                    summed[k] = pe.did(PE.matmul(ps[:, 1, :], mean_w[:, :], sq[:, k % 4, :], start=(k == 0),
                                                 stop=(k == KD - 1)))
                wait(VE, summed[-1])
                t = dve.did(VE.tensor_scalar(var[:, :], ps[:, 1, :], eps, None, ALU.add))
                wait(PE, t)
                for q in range(4):
                    ins = PE.matmul(ps[:, 2, q:q + 1], var[:, q * P:(q + 1) * P], ident[:, 0:1],
                                    start=(q == 0), stop=(q == 3), skip_group_check=True)
                wait(VE, pe.did(ins))
                t = dve.did(VE.tensor_copy(stat[:, 0, :], ps[:, 2, 0:4]))
                wait(GP, t)
                t = pool.did(GP.tensor_tensor(stat[:, 1, :], stat[:, 0, :], minus_half[:, :], ALU.pow))
                wait(PE, t)
                for q in range(4):
                    ins = PE.matmul(ps[:, 3, q * P:(q + 1) * P], stat[:, 1, q:q + 1].broadcast_to([P, P]),
                                    ident[:, :], start=True, stop=True, skip_group_check=True)
                rstd = pe.did(ins)
                wait(VE, rstd)
                gain, bias = to_a if to_a is not None else keep
                ready, scaled = [], []

                def scale(k, columns, dst):
                    return dve.did(VE.scalar_tensor_tensor(out=dst, in0=X[:, k, :], scalar=columns[:, k:k + 1],
                                                           in1=ps[:, 3, :], op0=ALU.mult, op1=ALU.mult))

                if to_a is None:
                    for k in range(KD):
                        wait(SC, scale(k, gain, val[:, k, :]))
                        ready.append(act.did(SC.activation(X[:, k, :], val[:, k, :], ACT.Identity,
                                                           bias=bias[:, k:k + 1])))
                    return ready
                his = []
                own_gain = not isinstance(keep[0], float)
                for k in range(KD + 1):
                    if k < KD:
                        scaled.append(scale(k, gain, val[:, k, :]))
                        wait(SC, scaled[k])
                        his.append(act.did(SC.activation(AH[:, k, :], val[:, k, :], ACT.Identity,
                                                         bias=bias[:, k:k + 1])))
                    if k and not own_gain:
                        act.did(SC.activation(X[:, k - 1, :], val[:, k - 1, :], ACT.Identity, scale=keep[0],
                                              bias=keep[1][:, k - 1:k]))
                    if k:
                        wait(VE, his[k - 1], scaled[k - 1])
                        ready.append(dve.did(VE.scalar_tensor_tensor(
                            out=AL[:, k - 1, :], in0=val[:, k - 1, :], scalar=bias[:, k - 1:k],
                            in1=f32(AH[:, k - 1, :]), op0=ALU.add, op1=ALU.subtract)))
                if own_gain:
                    for k in range(KD):
                        wait(SC, scale(k, keep[0], X[:, k, :]))
                        act.did(SC.activation(X[:, k, :], X[:, k, :], ACT.Identity, bias=keep[1][:, k:k + 1]))
                return ready

        def settle(*engines):
            for engine in engines:
                wait(engine, *(Token(c, c.val) for c in (pe, act, dve, pool)))

        def conv3(dst, bank, taps, used_tok, free_tok):
            wait(SC, used_tok, free_tok)
            t = act.did(SC.activation(dst, ps[:, bank, :], ACT.Copy, scale=taps[1]))
            wait(VE, t)
            t = dve.did(VE.scalar_tensor_tensor(out=dst[:, 1:T], in0=ps[:, bank, 0:T - 1], scalar=taps[0],
                                                in1=dst[:, 1:T], op0=ALU.mult, op1=ALU.add))
            wait(VE, t)
            return dve.did(VE.scalar_tensor_tensor(out=dst[:, 0:T - 1], in0=ps[:, bank, 1:T], scalar=taps[2],
                                                   in1=dst[:, 0:T - 1], op0=ALU.mult, op1=ALU.add))

        def split_act(dst_hi, dst_lo, src, ready):
            wait(VE, ready)
            hi = dve.did(VE.tensor_copy(dst_hi, src))
            wait(VE, hi)
            return dve.did(VE.tensor_tensor(dst_lo, src, f32(dst_hi), ALU.subtract))

        def column(name, k):
            at, n = PARAMS[name]
            if isinstance(k, Val) and k.step:
                return PV[:, bass.ds((k + at).of(p.index), 1)]
            k = k.const if isinstance(k, Val) else k
            return PV[:, at + k:at + k + 1]

        def ffn(tag, up, down, conv, a_ready, gate_col):
            st = ExitStack()
            with st:
                HH = p.sb(st, f"{tag}_hidden_hi", [P, KF, T], F32R)
                HL = p.sb(st, f"{tag}_hidden_lo", [P, KF, T], F32R)
                CA = p.sb(st, f"{tag}_value", [P, 2, T])
                CG = p.sb(st, f"{tag}_gate", [P, 2, T])
                HF = p.sb(st, f"{tag}_hidden", [P, 2, T])
                base_c = FIRST_CHUNK[up]
                settle(VE, SC)

                def multiply(c, bank, free):
                    wh, wl = take(c)
                    wait(PE, *free)
                    for k in range(KD):
                        ins = mm3(ps[:, bank, :], wh[:, k, :], wl[:, k, :], AH[:, k, :], AL[:, k, :],
                                  k == 0, k == KD - 1)
                    return used.did(ins)

                def finish_first(j, u, done, free):
                    if conv is None:
                        wait(SC, done, free)
                        return act.did(SC.activation(CG[:, u, :], ps[:, 2 * u, :], ACT.Silu))
                    return conv3(CA[:, u, :], 2 * u, [column(conv, j * 3 + s) for s in range(3)], done, free)

                def finish_second(j, u, first, done):
                    if conv is None:
                        wait(VE, first, done)
                        h = dve.did(VE.tensor_tensor(HF[:, u, :], CG[:, u, :], ps[:, 2 * u + 1, :], ALU.mult))
                        freed = h
                    else:
                        freed = conv3(CG[:, u, :], 2 * u + 1, [column(conv, j * 3 + (3 * KF + s)) for s in range(3)],
                                      done, None)
                        wait(SC, freed)
                        g = act.did(SC.activation(CG[:, u, :], CG[:, u, :], ACT.Silu))
                        wait(VE, g)
                        h = dve.did(VE.tensor_tensor(HF[:, u, :], CG[:, u, :], CA[:, u, :], ALU.mult))
                    split_act(tile(HH, j), tile(HL, j), HF[:, u, :], h)
                    return freed, h

                def step(c, j, u, free_first, free_second, pend):
                    d0 = multiply(c, 2 * u, free_first)
                    fin = finish_second(*pend)
                    d1 = multiply(c + 1, 2 * u + 1, free_second)
                    f = finish_first(j, u, d0, free_first[-1] if free_first else None)
                    return (j, u, f, d1), fin

                d0, d1 = take_two(Val(base_c), a_ready)
                pend0 = (Val(0), 0, finish_first(Val(0), 0, d0, None), d1)
                pend1, fin0 = step(Val(base_c + 2), Val(1), 1, [], [], pend0)
                n_dve = 2 * (3 if conv is None else 7)
                n_act = 2 * (1 if conv is None else 3)

                def moved(tok, step_):
                    return Token(tok.count, Val(tok.val.const, step_[tok.count]))

                rise = {dve: n_dve, act: n_act, used: 4}
                with p.loop(KF // 2 - 1, per(4, dve=n_dve, act=n_act)):
                    j0, j1 = Val(2, 2), Val(3, 2)
                    c = Val(base_c + 4, 4)
                    free0 = [moved(pend0[2], rise), moved(fin0[1], rise)]
                    free0s = [moved(fin0[0], rise)]
                    before = (Val(1, 2), 1, moved(pend1[2], rise), moved(pend1[3], rise))
                    a0, fin1 = step(c, j0, 0, free0, free0s, before)
                    free1 = [moved(pend1[2], rise), fin1[1]]
                    a1, fin0 = step(c + 2, j1, 1, free1, [fin1[0]], a0)
                n = KF // 2 - 2

                def ended(tok):
                    return Token(tok.count, Val(tok.val.const + n * tok.val.step))

                finish_second(Val(KF - 1), 1, ended(a1[2]), ended(a1[3]))
                hidden_done = Token(dve, dve.val)

                base_d = FIRST_CHUNK[down]

                def down_chunk(c, k, first, last_):
                    wh, wl = take(c)
                    for m in range(KD):
                        ins = mm3(ps[:, m, :], wh[:, m, :], wl[:, m, :], tile(HH, k), tile(HL, k), first, last_)
                        if last_:
                            banks.append(pe.did(ins))
                    return ins

                banks = []
                wait(PE, hidden_done)
                used.did(down_chunk(Val(base_d), 0, True, False))
                used.did(down_chunk(Val(base_d + 1), 1, False, False))
                with p.loop(KF // 2 - 2, per(2)):
                    for s in range(2):
                        used.did(down_chunk(Val(base_d + 2 + s, 2), Val(2 + s, 2), False, False))
                used.did(down_chunk(Val(base_d + KF - 2), KF - 2, False, False))
                down_chunk(Val(base_d + KF - 1), KF - 1, False, True)
                wait(PE, banks[-1])
                used.did(PE.nop())
                arrived = []
                for m in range(KD):
                    wait(VE, banks[m])
                    factor = gate_col[:, m:m + 1] if gate_col is not None else 1.0
                    arrived.append(dve.did(VE.scalar_tensor_tensor(out=X[:, m, :], in0=ps[:, m, :], scalar=factor,
                                                                   in1=X[:, m, :], op0=ALU.mult, op1=ALU.add)))
                return arrived

        def out_linear(layer, rh, rl, tiles):
            base = FIRST_CHUNK[layer]

            def one(c, m, s, first):
                wh, wl = take(c)
                out_bank = tile(ps, m)
                for k in range(KD):
                    if first:
                        wait(PE, tiles[k])
                    ins = mm3(out_bank, wh[:, k, :], wl[:, k, :], rh[:, k, :], rl[:, k, :], k == 0, k == KD - 1)
                done = used.did(ins)
                wait(VE, done)
                t = dve.did(VE.tensor_tensor(tile(X, m), tile(X, m), out_bank, ALU.add))
                wait(VE, t)
                if first:
                    return dve.did(VE.tensor_copy(x_sum[:, :], tile(X, m)))
                return dve.did(VE.tensor_tensor(x_sum[:, :], x_sum[:, :], tile(X, m), ALU.add))

            one(Val(base), Val(0), 0, True)
            one(Val(base + 1), Val(1), 1, False)
            with p.loop(KD // 2 - 1, per(2, dve=4)):
                for s in range(2):
                    t = one(Val(base + 2 + s, 2), Val(2 + s, 2), s, False)
            return [Token(dve, dve.val)]

        wait(SP, tab_done)
        fetch(Val(0))
        fetch(Val(1))
        split(Val(0))

        s2 = ExitStack()
        with s2:
            hx = p.sb(s2, "pool_in", [P, KD, T + 2 * PAD])
            sums_n = p.sb(s2, "pool_sums_narrow", [P, 4, T + 2 * PAD])
            scratch_n = p.sb(s2, "pool_scratch_narrow", [P, 1, T + 2 * PAD])
            scratch_w = p.sb(s2, "pool_scratch_wide", [P, 2, T + 2 * PAD])
            edge = p.sb(s2, "pool_edges", [P, 4, PAD])
            df = p.sb(s2, "pool_diff", [P, KD, T])
            for engine in (VE, SC, GP):
                wait(engine, Token(mod_summed, mod_summed.val))
            settle(VE, SC, GP)
            dve.did(VE.memset(hx[:, :, 0:PAD], 0.0))
            clear = dve.did(VE.memset(hx[:, :, PAD + T:], 0.0))
            wait(VE, got_x, got_decay, stage1_dve, clear)
            wait(GP, got_x, got_decay, stage1_dve, clear)
            wait(SC, stage1_dve, got_x)
            lows, scaled = {}, {}
            L = T + 2 * PAD

            def window_sum(engine, count, bufs, k, w, t):
                steps = w.bit_length() - 1
                src, lo, hi, width, at = hx[:, k, :], 1, 0, 2, steps % 2
                low_edge, high_edge = 1, L
                while True:
                    dst = bufs[at % 2]
                    wait(engine, t)
                    t = count.did(engine.tensor_tensor(dst[:, low_edge:high_edge],
                                                       src[:, low_edge - lo:high_edge - lo],
                                                       src[:, low_edge + hi:high_edge + hi], ALU.add))
                    if width == w:
                        return dst, t
                    src, lo, hi = dst, width // 2, width // 2
                    low_edge, high_edge = low_edge + lo, high_edge - hi
                    width, at = 2 * width, at + 1

            inputs = {}
            for k in (0, 1, 4, 2, 3, 5, 6, 7):
                t = dve.did(VE.tensor_scalar(hx[:, k, PAD:PAD + T], X[:, k, :], AFF[:, 0, 0, k:k + 1],
                                             MOD[:, k:k + 1], ALU.mult, ALU.add))
                inputs[k] = t
                wait(SC, t)
                scaled[k] = act.did(SC.activation(X[:, k, :], X[:, k, :], ACT.Copy, scale=ALPHA_1))
            def finish_pool(k, total, t, sub_engine, sub_count):
                w = POOL_WINDOWS[k // 2]
                wait(VE, t)
                inside = dve.did(VE.scalar_tensor_tensor(out=df[:, k, :], in0=total[:, PAD:PAD + T], scalar=1.0 / w,
                                                         in1=hx[:, k, PAD:PAD + T], op0=ALU.mult,
                                                         op1=ALU.subtract))
                sides = ((slice(0, PAD), slice(PAD, 2 * PAD)), (slice(T - PAD, T), slice(T, T + PAD)))
                for side, (cols, at) in enumerate(sides):
                    u = dve.did(VE.tensor_tensor(edge[:, 2 * (k // 4) + side, :], total[:, at],
                                                 icnt[:, k // 2, side * PAD:(side + 1) * PAD], ALU.mult))
                for side, (cols, at) in enumerate(sides):
                    wait(VE, u, inside)
                    t = dve.did(VE.tensor_tensor(df[:, k, cols], edge[:, 2 * (k // 4) + side, :], hx[:, k, at],
                                                 ALU.subtract))
                wait(SC, t)
                hi = act.did(SC.activation(AH[:, k, :], df[:, k, :], ACT.Copy))
                wait(sub_engine, hi)
                lows[k] = sub_count.did(sub_engine.tensor_tensor(AL[:, k, :], df[:, k, :], f32(AH[:, k, :]),
                                                                 ALU.subtract))

            narrow = {}
            for k in range(4):
                wait(GP, narrow[k - 1][1] if k else None)
                narrow[k] = window_sum(GP, pool, (scratch_n[:, 0, :], sums_n[:, k, :]), k, POOL_WINDOWS[k // 2],
                                       inputs[k])
            for k in range(4):
                wait(VE, Token(dve, dve.val))
                total, t = window_sum(VE, dve, (scratch_w[:, 0, :], scratch_w[:, 1, :]), 4 + k,
                                      POOL_WINDOWS[2 + k // 2], inputs[4 + k])
                finish_pool(k, *narrow[k], GP, pool)
                finish_pool(4 + k, total, t, VE, dve)
            arrived = []
            for cc in range(2):
                wh, wl = take(Val(cc))
                for g2 in range(2):
                    g = 2 * cc + g2
                    wait(PE, lows[2 * g], lows[2 * g + 1])
                    for m in range(2):
                        for k in range(2):
                            b = (g2 * 2 + m) * 2 + k
                            ins = mm3(ps[:, 2 * g + m, :], wh[:, b, :], wl[:, b, :], AH[:, 2 * g + k, :],
                                      AL[:, 2 * g + k, :], k == 0, k == 1)
                done = used.did(ins)
                wait(VE, done)
                for m in range(4 * cc, 4 * cc + 4):
                    wait(VE, scaled[m])
                    arrived.append(dve.did(VE.scalar_tensor_tensor(out=X[:, m, :], in0=ps[:, m, :],
                                                                   scalar=AFF[:, 0, 1, m:m + 1], in1=X[:, m, :],
                                                                   op0=ALU.mult, op1=ALU.add)))
        ready = layer_norm("n0", arrived, False, EPS_1, (AFF[:, 1, 0, :], AFF[:, 1, 1, :]),
                           (AFF[:, 2, 0, :], AFF[:, 2, 1, :]), FIRST_CHUNK["up_1"])
        for engine in (VE, SC):
            wait(engine, Token(s_spec, s_spec.val))
        arrived = ffn("f0", "up_1", "down_1", None, ready, G2)
        ready = layer_norm("n1", arrived, False, EPS_1, (par_all("ln_g1"), par_all("ln_b1")),
                           (ALPHA_2, AFF[:, 3, 1, :]), FIRST_CHUNK["mla_in"])

        s4 = ExitStack()
        with s4:
            cosv = p.sb(s4, "rope_cos", [P, T])
            sinv = p.sb(s4, "rope_sin", [P, T])
            swap = p.sb(s4, "rope_swap", [P, P])
            rc = p.sb(s4, "rope_consts", [P, 2])
            krh = p.sb(s4, "k_rope_hi", [P, T], F32R)
            krl = p.sb(s4, "k_rope_lo", [P, T], F32R)
            W0 = p.sb(s4, "rope_in", [P, 2, T])
            W1 = p.sb(s4, "rope_swapped", [P, T])
            QH = p.sb(s4, "q_hi", [P, 6, T], F32R)
            QL = p.sb(s4, "q_lo", [P, 6, T], F32R)
            KH = p.sb(s4, "k_hi", [P, 4, T], F32R)
            KL = p.sb(s4, "k_lo", [P, 4, T], F32R)
            VH = p.sb(s4, "v_hi", [P, 4, T], F32R)
            VL = p.sb(s4, "v_lo", [P, 4, T], F32R)
            PB = p.sb(s4, "probabilities", [P, 4, T])
            PTH = p.sb(s4, "probs_t_hi", [P, 4, T], F32R)
            PTL = p.sb(s4, "probs_t_lo", [P, 4, T], F32R)
            sm = p.sb(s4, "softmax_stats", [P, 4, 4])
            with ExitStack() as s4a:
                LAT = p.sb(s4a, "latents", [P, 6, T])
                posi = p.sb(s4a, "positions", [P, T], I32)[:, :]
                turns = p.sb(s4a, "rope_turns", [P, T])[:, :]
                sq2 = p.sb(s4a, "rms_squares", [P, 2, T])
            OH = p.sb(s4, "heads_hi", [P, HEADS, T], F32R)
            OL = p.sb(s4, "heads_lo", [P, HEADS, T], F32R)
            s_rope = p.count("rope")
            first_two = take_two(Val(FIRST_CHUNK["mla_in"]), ready)
            settle(SP, VE, SC)
            s_rope.did(SP.dma_start(swap[:, :], a["rope_swap"]), 16)
            s_rope.did(SP.dma_start(rc[:, :], a["rope_consts"]), 16)
            got_rope = s_rope.did(SP.dma_start(posi, a["positions"].broadcast_to([P, T])), 16)
            angle = W0[:, 0, :]
            wait(VE, got_rope)
            t = dve.did(VE.tensor_copy(angle, posi))
            wait(VE, t)
            t = dve.did(VE.tensor_scalar(angle, angle, rc[:, 0:1], None, ALU.mult))
            wait(VE, t)
            reduced = reduce_sin(None, angle, turns)
            wait(VE, reduced)
            t = dve.did(VE.scalar_tensor_tensor(out=turns, in0=angle, scalar=-1.0, in1=angle,
                                                op0=ALU.mult, op1=ALU.max))
            wait(VE, t)
            from_quarter = dve.did(VE.tensor_scalar(turns, turns, -1.0, math.pi / 2, ALU.mult, ALU.add))

            def split_kept(dst_hi, dst_lo, src, ready_tok):
                wait(SC, ready_tok)
                hi = act.did(SC.activation(dst_hi, src, ACT.Copy))
                wait(VE, hi)
                return dve.did(VE.tensor_tensor(dst_lo, src, f32(dst_hi), ALU.subtract))

            base = FIRST_CHUNK["mla_in"]
            lat, squared, summed = [], [], []

            def sum_squares(m):
                group, first = (6, m == 0) if m < KQ else (7, m == KQ)
                wait(PE, squared[m])
                for q in range(4):
                    ins = PE.matmul(ps[:, group, q:q + 1], sq2[:, m % 2, q * P:(q + 1) * P], ones[:, 0:1],
                                    start=(first and q == 0), stop=(m in (KQ - 1, KQ + KKV - 1)),
                                    skip_group_check=True)
                summed.append(pe.did(ins))

            def inverse_rms(g, rank):
                wait(VE, summed[-1])
                t = dve.did(VE.tensor_scalar(stat[:, 2 * g, :], ps[:, 6 + g, 0:4], 1.0 / rank, EPS_RMS,
                                             ALU.mult, ALU.add))
                wait(GP, t)
                return pool.did(GP.tensor_tensor(stat[:, 2 * g + 1, :], stat[:, 2 * g, :], minus_half[:, :], ALU.pow))

            def normalise(g, tiles, gains, inverse):
                wait(PE, inverse, lat[4 * g])
                for q in range(4):
                    ins = PE.matmul(ps[:, 4 * g, q * P:(q + 1) * P], stat[:, 2 * g + 1, q:q + 1].broadcast_to([P, P]),
                                    ident[:, :], start=True, stop=True, skip_group_check=True)
                wait(VE, pe.did(ins))
                toks = []
                for i, m in enumerate(tiles):
                    wait(VE, lat[m])
                    toks.append(dve.did(VE.scalar_tensor_tensor(out=LAT[:, m, :], in0=LAT[:, m, :],
                                                                scalar=par(gains, i), in1=ps[:, 4 * g, :],
                                                                op0=ALU.mult, op1=ALU.mult)))
                return toks

            for m in range(6):
                if m < 2:
                    done = first_two[m]
                else:
                    wh, wl = take(Val(base + m))
                    for k in range(KD):
                        ins = mm3(ps[:, m, :], wh[:, k, :], wl[:, k, :], AH[:, k, :], AL[:, k, :],
                                  k == 0, k == KD - 1)
                    done = used.did(ins)
                wait(SC, done)
                lat.append(act.did(SC.activation(LAT[:, m, :], ps[:, m, :], ACT.Copy)))
                if m == 2:
                    sum_squares(0)
                    sum_squares(1)
                if m >= 3:
                    sum_squares(m - 1)
                if m < KQ + KKV:
                    wait(SC, lat[m], summed[m - 2] if m >= 2 else None)
                    squared.append(act.did(SC.activation(sq2[:, m % 2, :], LAT[:, m, :], ACT.Square)))
                if m == 3:
                    wait(SC, reduced)
                    sine = act.did(SC.activation(sinv[:, :], angle, ACT.Sin))
                    wait(SC, from_quarter)
                    cosine = act.did(SC.activation(cosv[:, :], turns, ACT.Sin))
                    inverse_q = inverse_rms(0, RQ)
                    wait(VE, sine)
                    signed = dve.did(VE.tensor_scalar(sinv[:, :], sinv[:, :], rc[:, 1:2], None, ALU.mult))
                if m == 4:
                    scaled_q = normalise(0, range(KQ), "g_q", inverse_q)
            wait(SC, done)
            inputs = [split_kept(AH[:, m, :], AL[:, m, :], LAT[:, m, :], scaled_q[m]) for m in range(KQ)]
            inverse_kv = inverse_rms(1, RKV)

            def swap_halves(bank, src, raw):
                wait(PE, raw, got_rope)
                return pe.did(PE.matmul(ps[:, bank, :], swap[:, :], src, start=True, stop=True))

            def rotate(bank, src, swapped, dst_hi, dst_lo):
                wait(VE, swapped, signed)
                t2 = dve.did(VE.tensor_tensor(W1[:, :], sinv[:, :], ps[:, bank, :], ALU.mult))
                wait(VE, cosine)
                t3 = dve.did(VE.tensor_tensor(src, src, cosv[:, :], ALU.mult))
                wait(VE, t2, t3)
                t4 = dve.did(VE.tensor_tensor(src, src, W1[:, :], ALU.add))
                return t2, split_act(dst_hi, dst_lo, src, t4)

            swapped = swap_halves(5, LAT[:, 5, :], lat[5])
            scaled_kv = normalise(1, range(KQ, KQ + KKV), "g_kv", inverse_kv)
            inputs += [split_kept(AH[:, m, :], AL[:, m, :], LAT[:, m, :], scaled_kv[m - KQ])
                       for m in range(KQ, KQ + KKV)]
            _, k_rope = rotate(5, LAT[:, 5, :], swapped, krh[:, :], krl[:, :])
            wait(PE, *inputs[:KQ])
            base = FIRST_CHUNK["mla_heads"]

            def head_group(g, base_c):
                before_act, before_dve = act.val, dve.val

                def keep(dst_hi, dst_lo, bank, done):
                    wait(SC, done)
                    hi = act.did(SC.activation(dst_hi, ps[:, bank, :], ACT.Copy))
                    wait(VE, hi)
                    return dve.did(VE.tensor_tensor(dst_lo, ps[:, bank, :], f32(dst_hi), ALU.subtract))

                q_kept, raw = [], []
                wait(PE, Token(act, before_act + -6))
                for ch in range(4):
                    wh, wl = take(base_c + ch)
                    if ch == 2:
                        wait(PE, k_rope)
                    tiles_of = (2 * ch, 2 * ch + 1) if ch < 2 else (2 + ch,)
                    for i, m in enumerate(tiles_of):
                        for k in range(KQ):
                            b = i * KQ + k
                            ins = mm3(ps[:, m, :], wh[:, b, :], wl[:, b, :], AH[:, k, :], AL[:, k, :],
                                      k == 0, k == KQ - 1)
                    done = used.did(ins)
                    for m in tiles_of:
                        if ch < 2:
                            q_kept.append(keep(QH[:, m, :], QL[:, m, :], m, done))
                        else:
                            wait(SC, done, Token(dve, before_dve))
                            raw.append(act.did(SC.activation(W0[:, m - 4, :], ps[:, m, :], ACT.Copy)))
                wait(PE, Token(dve, before_dve))
                swapped = swap_halves(6, W0[:, 0, :], raw[0])
                rope0 = rotate(6, W0[:, 0, :], swapped, QH[:, 4, :], QL[:, 4, :])
                wh, wl = take(base_c + 4)
                wait(PE, q_kept[-1])
                for h in range(4):
                    for k in range(KKV):
                        ins = mm3(ps[:, h, :], wh[:, h * KKV + k, :], wl[:, h * KKV + k, :], AH[:, KQ + k, :],
                                  AL[:, KQ + k, :], k == 0, k == KKV - 1)
                done = used.did(ins)
                k_kept = [keep(KH[:, h, :], KL[:, h, :], h, done) for h in range(4)]
                swapped = swap_halves(7, W0[:, 1, :], raw[1])
                rope1 = rotate(7, W0[:, 1, :], swapped, QH[:, 5, :], QL[:, 5, :])
                slot = (base_c + 5).const % 2
                take(base_c + 5)
                for q in range(4):
                    bank = 4 + q
                    wait(PE, (raw[0], raw[1], rope0[0], rope1[0])[q])
                    for k in range(KKV):
                        cols = slice(q * P, (q + 1) * P)
                        ins = mm3(ps[:, bank, :], AH[:, KQ + k, cols], AL[:, KQ + k, cols],
                                  WH[:, slot, k * T:(k + 1) * T], WL[:, slot, k * T:(k + 1) * T],
                                  k == 0, k == KKV - 1)
                done = used.did(ins)
                v_kept = [keep(VH[:, q, :], VL[:, q, :], 4 + q, done) for q in range(4)]

                tops, exps, probs, transposed, result_read = {}, {}, {}, {}, {}

                def score(h, q):
                    rows = slice((h % 2) * ROPE, (h % 2) * ROPE + ROPE)
                    cols = slice(q * P, (q + 1) * P)
                    wait(PE, exps.get((h - 1, q)))
                    mm3(ps[:, q, :], QH[:, h, cols], QL[:, h, cols], KH[:, h, :], KL[:, h, :], True, False)
                    scored = pe.did(mm3(ps[:, q, :], QH[rows, 4 + h // 2, cols], QL[rows, 4 + h // 2, cols],
                                        krh[rows, :], krl[rows, :], False, True))
                    wait(VE, scored)
                    t = dve.did(VE.tensor_reduce(sm[:, q, 0:1], ps[:, q, :], AX_X, ALU.max))
                    wait(VE, t)
                    tops[h, q] = dve.did(VE.tensor_scalar(sm[:, q, 1:2], sm[:, q, 0:1], -SM_SCALE, None, ALU.mult))

                def exponent(h, q):
                    wait(SC, tops[h, q], transposed.get((h - 1, q)))
                    exps[h, q] = act.did(SC.activation(PB[:, q, :], ps[:, q, :], ACT.Exp, bias=sm[:, q, 1:2],
                                                       scale=SM_SCALE, accum_out=sm[:, q, 2:3]))

                def divide(h, q):
                    wait(VE, exps[h, q])
                    t = dve.did(VE.reciprocal(sm[:, q, 3:4], sm[:, q, 2:3]))
                    wait(VE, t)
                    probs[h, q] = dve.did(VE.tensor_scalar(PB[:, q, :], PB[:, q, :], sm[:, q, 3:4], None, ALU.mult))

                wait(PE, k_kept[-1], rope1[1])
                for q in range(4):
                    score(0, q)
                    exponent(0, q)
                    if q:
                        divide(0, q - 1)
                divide(0, 3)
                kept, results = {}, None
                wait(PE, v_kept[-1])
                for h in range(4):
                    for q in range(4):
                        bank = 4 + q % 2
                        wait(PE, probs[h, q], kept.get(bank))
                        for kt in range(4):
                            ins = PE.transpose(ps[:, bank, kt * P:(kt + 1) * P], PB[:, q, kt * P:(kt + 1) * P],
                                               ident[:, :])
                        transposed[h, q] = pe.did(ins)
                        cols = slice(q * P, (q + 1) * P)
                        src = ps[:, bank, :].rearrange("p (k q) -> p k q", k=4)
                        wait(SC, transposed[h, q], results)
                        hi = act.did(SC.activation(PTH[:, :, cols], src, ACT.Copy))
                        wait(VE, hi)
                        kept[bank] = dve.did(VE.tensor_tensor(PTL[:, :, cols], src, f32(PTH[:, :, cols]),
                                                              ALU.subtract))
                        if h < 3:
                            score(h + 1, q)
                            if q:
                                exponent(h + 1, q - 1)
                                divide(h + 1, q - 1)
                    if h < 3:
                        exponent(h + 1, 3)
                        divide(h + 1, 3)
                    bank = 6 + h % 2
                    wait(PE, kept[4], kept[5], result_read.get(bank))
                    for kt in range(4):
                        ins = mm3(ps[:, bank, :], VH[:, kt, h * P:(h + 1) * P], VL[:, kt, h * P:(h + 1) * P],
                                  PTH[:, kt, :], PTL[:, kt, :], kt == 0, kt == 3)
                    results = pe.did(ins)
                    result_read[bank] = keep(tile(OH, g + h), tile(OL, g + h), bank, results)

            with p.loop(N_GROUPS, per(6, pe=2 + 4 * (4 + 4 + 1), act=4 + 2 + 4 + 4 + 4 * (4 + 4 + 1),
                                      dve=4 + 2 * 5 + 4 + 4 + 4 * (4 * 5 + 1))):
                head_group(Val(0, 4), Val(base, 6))
            heads_done = Token(dve, dve.val)
            arrived = out_linear("mla_out", OH, OL, [heads_done] * KD)
        ready = layer_norm("n2", arrived, True, EPS_2, (par_all("a_g0"), par_all("a_b0")),
                           (ALPHA_2, AFF[:, 4, 1, :]), FIRST_CHUNK["up_2"])

        arrived = ffn("f1", "up_2", "down_2", "conv0", ready, None)
        ready = layer_norm("n3", arrived, False, EPS_2, (par_all("f_g0"), par_all("f_b0")),
                           (ALPHA_2, AFF[:, 5, 1, :]), FIRST_CHUNK["hy_in"])

        s5 = ExitStack()
        with s5:
            U = p.sb(s5, "hy_branches", [P, 24, T])
            FH = p.sb(s5, "dft_fwd_hi", [P, 16, P], F32R)
            FL = p.sb(s5, "dft_fwd_lo", [P, 16, P], F32R)
            IH = p.sb(s5, "dft_inv_hi", [P, 8, HALF], F32R)
            IL = p.sb(s5, "dft_inv_lo", [P, 8, HALF], F32R)
            KS = p.sb(s5, "hy_filter", [P, 4, T])
            s_tab, s_xs, s_ks = p.count("tables"), p.count("x_spill"), p.count("filter_load")
            with ExitStack() as s5a:
                raw_tabs = p.sb(s5a, "dft_raw", [P, 2, 4 * T])
            YH = p.sb(s5, "hy_product_hi", [P, 2, 4, T], F32R)
            YL = p.sb(s5, "hy_product_lo", [P, 2, 4, T], F32R)
            kept_all = Token(act, act.val)
            base = FIRST_CHUNK["hy_in"]
            first_two = take_two(Val(base), ready)
            settle(VE, SC, SP)
            def short_conv(m, bank, done):
                return conv3(tile(U, m), bank, [column("hy_short", m * 3 + s) for s in range(3)], done, None)

            def branch(c, m, bank, read):
                wh, wl = take(c)
                wait(PE, read)
                for k in range(KD):
                    ins = mm3(ps[:, bank, :], wh[:, k, :], wl[:, k, :], AH[:, k, :], AL[:, k, :],
                              k == 0, k == KD - 1)
                return short_conv(m, bank, used.did(ins))

            for m in range(4):
                if m < 2:
                    short_conv(Val(m), m, first_two[m])
                else:
                    branch(Val(base + m), Val(m), m, None)
            for i, name in enumerate(("dft_fwd", "dft_inv")):
                got_tabs = s_tab.did(SP.dma_start(raw_tabs[:, i, :], a[name].rearrange("p a b -> p (a b)")), 16)
            wait(SP, kept_all)
            for k in range(KD):
                spilled = s_xs.did(SP.dma_start(a["x_spill"][k], X[:, k, :]), 16)
            wait(VE, got_tabs)
            flat = lambda t: t[:, :, :].rearrange("p a b -> p (a b)")
            for i, (h_, l_) in enumerate(((FH, FL), (IH, IL))):
                tabs_done = split_act(flat(h_), flat(l_), raw_tabs[:, i, :], None)
            with p.loop(5, per(4, act=4, dve=8)):
                reads = [Token(dve, dve.val + (2 * (u + 1) - 8)) for u in range(4)]
                for u in range(4):
                    branch(Val(base + 4 + u, 4), Val(4 + u, 4), u, reads[u])
            branches = Token(dve, dve.val)

            left = {0: branches, 1: branches}
            z_ready = {0: branches, 1: branches}
            filter_read, multiplied, inverted, outs = [Token(s_spec, s_spec.val)], [], [], []
            S = lambda i: X[:, i, :]
            for engine in (SC, VE, GP):
                wait(engine, spilled)

            def product_slot(s):
                slot = s % 3
                return (YH[:, slot], YL[:, slot]) if slot < 2 else (AH[:, 0:4, :], AL[:, 0:4, :])

            def transpose_z(half, bank_set, transformed):
                n = half % 2
                wait(PE, z_ready[n], left[bank_set], tabs_done)
                for q in range(4):
                    bank = 4 * bank_set + q
                    for m in range(4):
                        zt_ = U[:, 4 * n + m, :].rearrange("p (t two) -> p two t", two=2)
                        src = zt_[:, q // 2, (q % 2) * P:(q % 2 + 1) * P]
                        ins = PE.transpose(ps[:, bank, m * P:(m + 1) * P], src, ident[:, :])
                    t = pe.did(ins)
                    wait(SC, t, transformed)
                    hi = act.did(SC.activation(AH[:, 4 + q, :], ps[:, bank, :], ACT.Copy))
                    wait(VE, hi)
                    left[bank_set] = dve.did(VE.tensor_tensor(AL[:, 4 + q, :], ps[:, bank, :], f32(AH[:, 4 + q, :]),
                                                              ALU.subtract))
                return left[bank_set]

            def forward(f, bank_set, z_split):
                wait(PE, z_split, left[bank_set])
                for kind in range(2):
                    for parity in range(2):
                        for k in range(2):
                            b = ((kind * 2 + parity) * 2 + k) * 2 + f
                            ins = mm3(ps[:, 4 * bank_set + 2 * kind + parity, :], FH[:, b, :], FL[:, b, :],
                                      AH[:, 4 + 2 * parity + k, :], AL[:, 4 + 2 * parity + k, :], k == 0, k == 1)
                return pe.did(ins)

            def butterfly(half, f, bank_set, transformed):
                wait(SP, *filter_read)
                ks = s_ks.did(SP.dma_start(KS[:, :, :], a["spectra"][half // 2, half % 2, f]), 16)
                scratch_free = multiplied[-1] if multiplied else None
                bk = 4 * bank_set
                wait(SC, transformed, scratch_free)
                act.did(SC.activation(S(4), ps[:, bk + 1, :], ACT.Copy))
                t = act.did(SC.activation(S(5), ps[:, bk + 3, :], ACT.Copy))
                wait(VE, t, scratch_free)
                dve.did(VE.tensor_tensor(S(2), ps[:, bk, :], S(4), ALU.subtract))
                minus = dve.did(VE.tensor_tensor(S(3), ps[:, bk + 2, :], S(5), ALU.subtract))
                dve.did(VE.tensor_tensor(S(0), ps[:, bk, :], S(4), ALU.add))
                left[bank_set] = dve.did(VE.tensor_tensor(S(1), ps[:, bk + 2, :], S(5), ALU.add))
                wait(GP, minus, ks)
                pool.did(GP.tensor_tensor(S(6), S(2), KS[:, 1, :], ALU.mult))
                t = pool.did(GP.tensor_tensor(S(7), S(3), KS[:, 3, :], ALU.mult))
                wait(GP, t)
                v_cos = pool.did(GP.tensor_tensor(S(6), S(6), S(7), ALU.subtract))
                pool.did(GP.tensor_tensor(S(2), S(2), KS[:, 3, :], ALU.mult))
                t = pool.did(GP.tensor_tensor(S(3), S(3), KS[:, 1, :], ALU.mult))
                wait(GP, t)
                v_sin = pool.did(GP.tensor_tensor(S(2), S(2), S(3), ALU.add))
                return ks, v_cos, v_sin

            def products(half, f, bank_set, ks, v_cos, v_sin):
                wait(VE, left[bank_set], ks)
                dve.did(VE.tensor_tensor(S(4), S(0), KS[:, 0, :], ALU.mult))
                t = dve.did(VE.tensor_tensor(S(5), S(1), KS[:, 2, :], ALU.mult))
                wait(VE, t)
                dve.did(VE.tensor_tensor(S(4), S(4), S(5), ALU.subtract))
                dve.did(VE.tensor_tensor(S(0), S(0), KS[:, 2, :], ALU.mult))
                t = dve.did(VE.tensor_tensor(S(1), S(1), KS[:, 0, :], ALU.mult))
                wait(VE, t)
                t = dve.did(VE.tensor_tensor(S(0), S(0), S(1), ALU.add))
                filter_read[:] = [t, v_sin]
                s = 2 * half + f
                high, low = product_slot(s)
                sums = {}
                for i, dst, x1, x2, op, v in ((0, 1, 4, 6, ALU.add, v_cos), (2, 5, 4, 6, ALU.subtract, v_cos),
                                              (1, 3, 0, 2, ALU.add, v_sin), (3, 7, 0, 2, ALU.subtract, v_sin)):
                    wait(VE, t, v)
                    sums[i] = dst, dve.did(VE.tensor_tensor(S(dst), S(x1), S(x2), op))
                    wait(SC, sums[i][1], inverted[(s - 3) // 2] if s >= 3 else None)
                    sums[i] += (act.did(SC.activation(high[:, i, :], S(dst), ACT.Copy)),)
                for i in (0, 2, 1, 3):
                    dst, _, hi = sums[i]
                    wait(VE, hi)
                    t = dve.did(VE.tensor_tensor(low[:, i, :], S(dst), f32(high[:, i, :]), ALU.subtract))
                multiplied.append(t)

            def invert(half, bank_set):
                order, n = divmod(half, 2)
                slots = [product_slot(2 * half + f) for f in range(2)]
                wait(PE, left[bank_set])
                backs = []
                for f in range(2):
                    wait(PE, multiplied[2 * half + f])
                    high, low = slots[f]
                    for m in range(4):
                        bank = 4 * bank_set + m
                        cols = slice(m * P, (m + 1) * P)
                        for parity in range(2):
                            for kind in range(2):
                                b = (kind * 2 + parity) * 2 + f
                                ins = mm3(ps[:, bank, parity * HALF:(parity + 1) * HALF],
                                          high[:, 2 * parity + kind, cols], low[:, 2 * parity + kind, cols],
                                          IH[:, b, :], IL[:, b, :], (f, parity, kind) == (0, 0, 0),
                                          (f, kind) == (1, 1), skip_group_check=True)
                        if f == 1:
                            backs.append(pe.did(ins))
                inverted.append(backs[-1])
                gated = []

                def split_result(m):
                    outs.append(split_kept(AH[:, 4 * n + m, :], AL[:, 4 * n + m, :], U[:, 4 * n + m, :], gated[m]))

                for m in range(4):
                    wait(VE, backs[m])
                    view = lambda ap: ap.rearrange("p (t two) -> p two t", two=2)
                    z = U[:, 4 * n + m, :]
                    gate = U[:, 8 * (order + 1) + 4 * n + m, :]
                    y = ps[:, 4 * bank_set + m, :].rearrange("p (two t) -> p two t", two=2)
                    left[bank_set] = dve.did(VE.scalar_tensor_tensor(out=view(z), in0=view(z),
                                                                     scalar=par("hy_d", 8 * order + 4 * n + m),
                                                                     in1=y, op0=ALU.mult, op1=ALU.add))
                    wait(VE, left[bank_set])
                    gated.append(dve.did(VE.tensor_tensor(z, z, gate, ALU.mult)))
                    if half == 3 and m:
                        split_result(m - 1)
                z_ready[n] = gated[-1]
                if half == 2:
                    wait(SC, backs[-1])
                    for m in range(4):
                        split_result(m)
                if half == 3:
                    split_result(3)

            def to_frequency(half, transformed):
                z_split = transpose_z(half, 1, transformed)
                return forward(0, 1, z_split), forward(1, 0, z_split)

            spectra = to_frequency(0, None)
            for half in range(4):
                multiply_first = butterfly(half, 0, 1, spectra[0])
                products(half, 0, 1, *multiply_first)
                if half:
                    invert(half - 1, 1)
                multiply_second = butterfly(half, 1, 0, spectra[1])
                if half < 3:
                    spectra = to_frequency(half + 1, spectra[1])
                products(half, 1, 0, *multiply_second)
            invert(3, 1)
            wait(SP, multiplied[-1])
            for k in range(KD):
                back = s_xs.did(SP.dma_start(X[:, k, :], a["x_spill"][k]), 16)
            wait(VE, back)
            arrived = out_linear("hy_out", AH, AL, outs)
        ready = layer_norm("n4", arrived, True, EPS_2, (par_all("a_g1"), par_all("a_b1")),
                           (ALPHA_2, AFF[:, 6, 1, :]), FIRST_CHUNK["up_3"])

        arrived = ffn("f2", "up_3", "down_3", "conv1", ready, None)
        done = layer_norm("n5", arrived, False, EPS_2, None, (par_all("f_g1"), par_all("f_b1")), None)
        s_out = p.count("stored")
        for k in range(KD):
            wait(SP, done[k])
            stored = s_out.did(SP.dma_start(out[k * P:(k + 1) * P, :], X[:, k, :]), 16)
        wait(SP, stored)
        wait(SP, Token(s_xs, s_xs.val))


def time_order():
    return np.concatenate([np.arange(0, T, 2), np.arange(1, T, 2)])


def shape_constants():
    f32 = np.float32
    order = time_order()
    freq = (2 * np.arange(HALF) + 1) * np.pi / (2 * T)
    fwd = np.zeros((P, 16, P), f32)
    inv = np.zeros((P, 8, HALF), f32)
    for kind, fn in enumerate((np.cos, np.sin)):
        for parity in range(2):
            times = np.arange(parity, T, 2)
            table = fn(np.outer(times, freq))
            for k in range(2):
                for f in range(2):
                    fwd[:, ((kind * 2 + parity) * 2 + k) * 2 + f] = table[k * P:(k + 1) * P, f * P:(f + 1) * P]
            for f in range(2):
                inv[:, (kind * 2 + parity) * 2 + f] = table.T[f * P:(f + 1) * P] / T
    t = np.linspace(0.0, 1.0, T, dtype=f32)[:, None]
    bands = (HY_EMB - 1) // 2
    w = (2.0 * math.pi * np.arange(T, dtype=f32)[:, None] / T).astype(f32)
    fr = np.linspace(1e-4, bands - 1, bands, dtype=f32)[None, :]
    z = np.concatenate([t, np.cos(fr * w), -np.sin(fr * w)], axis=-1).astype(f32)
    deltas = np.abs(np.linspace(math.log(0.3) / 1e-2, math.log(1.5) / 1e-2, D, dtype=f32))
    decay = np.exp(-t * deltas).astype(f32)
    steps = np.arange(T)
    counts = []
    for win in POOL_WINDOWS:
        lo = win // 2
        start, end = np.clip(steps - lo, 0, T), np.clip(steps + win - lo, 0, T)
        counts.append(np.concatenate([1.0 / (end - start)[:PAD], 1.0 / (end - start)[T - PAD:]]))
    inv_freq = (1.0 / (10000.0 ** (np.arange(0, ROPE, 2, dtype=f32) / f32(ROPE)))).astype(f32)
    rope = np.stack([np.tile(inv_freq, 4), np.tile(np.repeat([-1.0, 1.0], ROPE // 2), 2)], 1).astype(f32)
    swap = np.zeros((P, P), f32)
    rows = np.arange(P)
    swap[rows, rows ^ (ROPE // 2)] = 1.0
    return {
        "dft_fwd": fwd, "dft_inv": inv, "hy_z": np.ascontiguousarray(z[order].T),
        "decay": np.ascontiguousarray(decay[order].reshape(4, P, D).transpose(1, 0, 2)),
        "inv_count": np.ascontiguousarray(np.broadcast_to(np.array(counts, f32), (P, 4, 2 * PAD))),
        "rope_consts": rope, "rope_swap": swap, "identity": np.eye(P, dtype=f32),
    }


def columns(v):
    return np.asarray(v).reshape(-1, P).T


def by_output_tile(w):
    k, m = w.shape
    return w.reshape(k // P, P, m // P, P).transpose(2, 1, 0, 3).reshape(m // P, P, k)


def weight_stream(i):
    parts = []
    pw = i["pool_w"][0].reshape(2, 2, 2, P, 2, P)
    parts.append(pw.transpose(0, 3, 1, 4, 2, 5).reshape(2, P, CHUNK))
    w = by_output_tile(i["ffn_w_in"][0])
    parts.append(w.reshape(2, KF, P, CHUNK).transpose(1, 0, 2, 3).reshape(2 * KF, P, CHUNK))
    parts.append(i["ffn_w_out"][0].reshape(KF, P, D))
    w = i["mla_w_in_2"][0]
    parts.append(by_output_tile(np.concatenate([w, w[:, RQ + RKV:]], axis=1)))
    uq = i["mla_w_uq_2"][0].reshape(KQ, P, HEADS, NOPE + ROPE)
    ukv = i["mla_w_ukv_2"][0].reshape(KKV, P, HEADS, NOPE + VD)
    for g in range(N_GROUPS):
        hs = slice(4 * g, 4 * g + 4)
        nope = uq[:, :, hs, :NOPE].reshape(KQ, P, 2, 2, P).transpose(2, 1, 3, 0, 4).reshape(2, P, 2 * KQ * P)
        rope = uq[:, :, hs, NOPE:].reshape(KQ, P, 2, P).transpose(2, 1, 0, 3).reshape(2, P, KQ * P)
        for part in (nope, rope):
            padded = np.zeros((2, P, CHUNK), part.dtype)
            padded[:, :, :part.shape[2]] = part
            parts.append(padded)
        parts.append(ukv[:, :, hs, :NOPE].transpose(1, 2, 0, 3).reshape(1, P, CHUNK))
        parts.append(ukv[:, :, hs, NOPE:].transpose(1, 0, 2, 3).reshape(1, P, CHUNK))
    parts.append(by_output_tile(i["mla_w_o_2"][0]))

    def conv_ffn(layer):
        w = by_output_tile(i["ffn_w_up_2"][layer])
        parts.append(w.reshape(2, KF, P, CHUNK).transpose(1, 0, 2, 3).reshape(2 * KF, P, CHUNK))
        parts.append(i["ffn_w_down_2"][layer].reshape(KF, P, D))

    conv_ffn(0)
    parts.append(by_output_tile(i["hy_w_in_2"][0]))
    parts.append(by_output_tile(i["hy_w_o_2"][0]))
    conv_ffn(1)
    out = np.concatenate(parts, axis=0)
    assert out.shape == (N_CHUNKS, P, CHUNK), out.shape
    return out


def taps(w):
    return w.reshape(3, -1, P).transpose(2, 1, 0).reshape(P, -1)


def lay_out(i):
    cols = {
        "c": columns(i["c"][0]), "mod_b": columns(i["mod_b"][0]),
        "ln_g0": columns(i["ln_g"][0, 0]), "ln_b0": columns(i["ln_b"][0, 0]),
        "ln_g1": columns(i["ln_g"][0, 1]), "ln_b1": columns(i["ln_b"][0, 1]),
        "pool_scale": columns(i["pool_scale"][0]), "g_q": columns(i["mla_g_q_2"][0]),
        "g_kv": columns(i["mla_g_kv_2"][0]), "hy_short": taps(i["hy_w_short_2"][0]),
        "hy_d": columns(i["hy_d_bias_2"][0]), "conv0": taps(i["ffn_w_conv_2"][0]),
        "conv1": taps(i["ffn_w_conv_2"][1]),
    }
    for layer in range(2):
        for key, name in (("a", "ln1"), ("f", "ln2")):
            cols[f"{key}_g{layer}"] = columns(i[f"{name}_g_2"][layer])
            cols[f"{key}_b{layer}"] = columns(i[f"{name}_b_2"][layer])
    arrays = {
        "params": np.ascontiguousarray(np.concatenate([cols[n] for n in PARAMS], axis=1)),
        "xT": np.ascontiguousarray(i["x"][0].T),
        "mod_w": np.ascontiguousarray(i["mod_w"][0].reshape(KD, P, 16, 3 * P).transpose(2, 1, 0, 3)),
        "w_stream": weight_stream(i),
        "positions": np.ascontiguousarray(i["positions_2"]),
        "hy_fw1": np.ascontiguousarray(i["hy_fw1_2"][0]),
        "hy_small": np.ascontiguousarray(np.concatenate(
            [i["hy_fw2_2"][0], i["hy_fw3_2"][0]] +
            [i[n][0][:, None] for n in ("hy_fb1_2", "hy_fb2_2", "hy_fb3_2", "hy_freq_2")], axis=1)),
        "hy_fw_out": np.ascontiguousarray(i["hy_fw_out_2"][0].reshape(HY_W, 2, 2, D)),
    }
    arrays.update(shape_constants())
    return arrays


def kernel(**inputs):
    import concourse.bacc as bacc
    from concourse.bass_utils import run_bass_kernel_spmd

    arrays = lay_out({k: np.asarray(v) for k, v in inputs.items()})
    nc = bacc.Bacc("TRN2", target_bir_lowering=False, num_devices=1)
    aps = {n: nc.dram_tensor(f"in_{n}", v.shape, mybir.dt.from_np(v.dtype), kind="ExternalInput").ap()
           for n, v in arrays.items()}
    aps["spectra"] = nc.dram_tensor("spectra", (2, 2, 2, P, 4, T), F32, kind="Internal").ap()
    aps["x_spill"] = nc.dram_tensor("x_spill", (KD, P, T), F32, kind="Internal").ap()
    out = nc.dram_tensor("out_x", (D, T), F32, kind="ExternalOutput").ap()
    build_program(nc, aps, out)
    result = run_bass_kernel_spmd(nc, [{f"in_{n}": v for n, v in arrays.items()}], core_ids=[0])
    return np.ascontiguousarray(result.results[0]["out_x"].T)[None]
```
